# Optimizing a Trainium2 kernel written in Bass

```python
import jax, jax.numpy as jnp
from jax import lax
import numpy as np

D_MODEL = 1024
BATCH = 1
SEQ = 512
DEPTH = 2

CHUNK = 64
N_META = 16
N_PAD = CHUNK - N_META
EPS = 1e-6

ML_HEADS = 8
ML_DV = D_MODEL // ML_HEADS
ML_DK = ML_DV // 2
ML_QK = ML_HEADS * ML_DK
ML_V = ML_HEADS * ML_DV
ML_CONV = 4
GATE_CAP = 15.0

RT_HEADS = D_MODEL // 256
RT_DK = D_MODEL // RT_HEADS
RT_DV = 2 * RT_DK
RT_QK = RT_HEADS * RT_DK
RT_V = RT_HEADS * RT_DV
ROPE_BASE = 10000.0

D_FF = ((8 * D_MODEL + 3 * 256 - 1) // (3 * 256)) * 256

N_MLSTM = (DEPTH + 1) // 2
N_RET = DEPTH // 2

kernel_name = 'hybrid_mlstm_retention_chunk_causal'

def rmsnorm(x, g):
    x32 = x.astype(jnp.float32)
    y = x32 * lax.rsqrt(jnp.mean(x32 * x32, axis=-1, keepdims=True) + EPS)
    return (y * g.astype(jnp.float32)).astype(x.dtype)

def causal_depthwise_conv(u, w):
    K, C = w.shape
    return lax.conv_general_dilated(u, w[:, None, :].astype(u.dtype), window_strides=(1,),
                                    padding=[(K - 1, 0)], dimension_numbers=('NWC', 'WIO', 'NWC'),
                                    feature_group_count=C)

def rope(x, pos):
    half = x.shape[-1] // 2
    inv = ROPE_BASE ** (-jnp.arange(half, dtype=jnp.float32) / half)
    ang = pos.astype(jnp.float32)[:, None] * inv[None, :]
    cos = jnp.cos(ang)[None, :, None, :]
    sin = jnp.sin(ang)[None, :, None, :]
    x1, x2 = x[..., :half], x[..., half:]
    return jnp.concatenate([x1 * cos - x2 * sin, x2 * cos + x1 * sin], axis=-1)

def to_chunks(t):
    B, L, H, d = t.shape
    return t.reshape(B, L // CHUNK, CHUNK, H, d).transpose(1, 0, 3, 2, 4)

def gate_chunks(t):
    B, L, H = t.shape
    return t.reshape(B, L // CHUNK, CHUNK, H).transpose(1, 0, 3, 2)

def from_chunks(t):
    NC, B, H, C, d = t.shape
    return t.transpose(1, 0, 3, 2, 4).reshape(B, NC * C, H, d)

def mlstm_chunk_step(carry, xs):
    C_prev, n_prev, m_prev = carry
    q, k, v, log_i, log_f = xs
    F = jnp.cumsum(log_f, axis=-1)
    D = log_i[..., None, :] - jnp.abs(F[..., :, None] - F[..., None, :])
    inter_log = F + m_prev[..., None]
    m = jnp.maximum(inter_log, jnp.max(D, axis=-1))
    w = jnp.exp(D - m[..., None])
    a = jnp.exp(inter_log - m)
    s = jnp.einsum('bhid,bhjd->bhij', q, k) * w
    num = a[..., None] * jnp.einsum('bhid,bhde->bhie', q, C_prev) + jnp.einsum('bhij,bhje->bhie', s, v)
    den = a * jnp.einsum('bhid,bhd->bhi', q, n_prev) + jnp.sum(s, axis=-1)
    h = num / jnp.maximum(jnp.abs(den), jnp.exp(-m))[..., None]
    F_end = F[..., -1]
    g_log = log_i + F_end[..., None] - F
    m_new = jnp.maximum(F_end + m_prev, jnp.max(g_log, axis=-1))
    g = jnp.exp(g_log - m_new[..., None])
    decay = jnp.exp(F_end + m_prev - m_new)
    C_new = decay[..., None, None] * C_prev + jnp.einsum('bhj,bhjd,bhje->bhde', g, k, v)
    n_new = decay[..., None] * n_prev + jnp.einsum('bhj,bhjd->bhd', g, k)
    return (C_new, n_new, m_new), h

def mlstm_mixer(h, valid, w_in, b_gate, w_conv, g_norm, w_out):
    B, L, _ = h.shape
    f32 = jnp.float32
    u = h @ w_in
    vmask = valid[None, :, None]
    qk = jnp.where(vmask, u[..., :2 * ML_QK], 0.0)
    v = u[..., 2 * ML_QK:2 * ML_QK + ML_V]
    o = u[..., 2 * ML_QK + ML_V:2 * ML_QK + 2 * ML_V]
    gates = u[..., 2 * ML_QK + 2 * ML_V:].astype(f32) + b_gate.astype(f32)
    qk = jax.nn.silu(causal_depthwise_conv(qk, w_conv)).astype(f32)
    q = qk[..., :ML_QK].reshape(B, L, ML_HEADS, ML_DK) * (ML_DK ** -0.5)
    k = qk[..., ML_QK:].reshape(B, L, ML_HEADS, ML_DK)
    v = v.astype(f32).reshape(B, L, ML_HEADS, ML_DV)
    gates = GATE_CAP * jnp.tanh(gates / GATE_CAP)
    log_i = jnp.where(vmask, gates[..., :ML_HEADS], -jnp.inf)
    log_f = jnp.where(vmask, jax.nn.log_sigmoid(gates[..., ML_HEADS:]), 0.0)
    init = (jnp.zeros((B, ML_HEADS, ML_DK, ML_DV), f32),
            jnp.zeros((B, ML_HEADS, ML_DK), f32),
            jnp.zeros((B, ML_HEADS), f32))
    xs = (to_chunks(q), to_chunks(k), to_chunks(v), gate_chunks(log_i), gate_chunks(log_f))
    _, hs = lax.scan(mlstm_chunk_step, init, xs)
    hs = from_chunks(hs)
    hs = hs * lax.rsqrt(jnp.mean(hs * hs, axis=-1, keepdims=True) + EPS)
    hs = hs.reshape(B, L, ML_V) * g_norm.astype(f32) * jax.nn.sigmoid(o.astype(f32))
    return hs.astype(h.dtype) @ w_out

def retention_mixer(h, valid, pos, w_in, g_norm, w_out):
    B, L, _ = h.shape
    f32 = jnp.float32
    u = h @ w_in
    q = u[..., :RT_QK].astype(f32).reshape(B, L, RT_HEADS, RT_DK)
    k = u[..., RT_QK:2 * RT_QK].astype(f32).reshape(B, L, RT_HEADS, RT_DK) * (RT_DK ** -0.5)
    v = u[..., 2 * RT_QK:2 * RT_QK + RT_V].astype(f32).reshape(B, L, RT_HEADS, RT_DV)
    g = u[..., 2 * RT_QK + RT_V:].astype(f32)
    q = rope(q, pos)
    k = jnp.where(valid[None, :, None, None], rope(k, pos), 0.0)
    log_gamma = jnp.log1p(-jnp.exp2(-5.0 - jnp.arange(RT_HEADS, dtype=f32)))
    idx = jnp.arange(CHUNK, dtype=f32)
    intra_decay = jnp.exp(log_gamma[:, None, None] * jnp.abs(idx[:, None] - idx[None, :]))
    q_decay = jnp.exp(log_gamma[:, None] * (idx + 1.0))[None, :, :, None]
    k_decay = jnp.exp(log_gamma[:, None] * (CHUNK - 1.0 - idx))[None, :, :, None]
    chunk_decay = jnp.exp(log_gamma * CHUNK)[None, :, None, None]

    def step(S, xs):
        qc, kc, vc = xs
        s = jnp.einsum('bhid,bhjd->bhij', qc, kc) * intra_decay
        out = jnp.einsum('bhij,bhje->bhie', s, vc) + q_decay * jnp.einsum('bhid,bhde->bhie', qc, S)
        S = chunk_decay * S + jnp.einsum('bhjd,bhje->bhde', kc * k_decay, vc)
        return S, out

    S0 = jnp.zeros((B, RT_HEADS, RT_DK, RT_DV), f32)
    _, hs = lax.scan(step, S0, (to_chunks(q), to_chunks(k), to_chunks(v)))
    hs = from_chunks(hs)
    mu = jnp.mean(hs, axis=-1, keepdims=True)
    var = jnp.mean((hs - mu) ** 2, axis=-1, keepdims=True)
    hs = ((hs - mu) * lax.rsqrt(var + EPS)).reshape(B, L, RT_V)
    hs = hs * g_norm.astype(f32) * jax.nn.silu(g)
    return hs.astype(h.dtype) @ w_out

def swiglu(h, w_gu, w_down):
    gu = h @ w_gu
    return (jax.nn.silu(gu[..., :D_FF]) * gu[..., D_FF:]) @ w_down

def setup_inputs(seed: int = 0) -> dict:
    key = jax.random.key(seed)
    ks = jax.random.split(key, 16)
    f32 = jnp.float32

    def dense(k, shape, fan_in):
        return jax.random.normal(k, shape, f32) * (fan_in ** -0.5)

    def gain(k, shape):
        return 1.0 + 0.02 * jax.random.normal(k, shape, f32)

    x = jax.random.normal(ks[0], (BATCH, SEQ, D_MODEL), f32)
    meta_tokens = jax.random.normal(ks[1], (N_META, D_MODEL), f32)
    norm_mix = gain(ks[2], (DEPTH, D_MODEL))
    norm_ffn = gain(ks[3], (DEPTH, D_MODEL))
    norm_final = gain(ks[4], (D_MODEL,))
    ml_w_in = dense(ks[5], (N_MLSTM, D_MODEL, 2 * ML_QK + 2 * ML_V + 2 * ML_HEADS), D_MODEL)
    b_i = 0.1 * jax.random.normal(ks[6], (N_MLSTM, ML_HEADS), f32)
    b_f = jnp.linspace(3.0, 6.0, ML_HEADS, dtype=f32)[None, :] + 0.1 * jax.random.normal(ks[7], (N_MLSTM, ML_HEADS), f32)
    ml_b_gate = jnp.concatenate([b_i, b_f], axis=-1)
    ml_w_conv = dense(ks[8], (N_MLSTM, ML_CONV, 2 * ML_QK), ML_CONV)
    ml_norm = gain(ks[9], (N_MLSTM, ML_V))
    ml_w_out = dense(ks[10], (N_MLSTM, ML_V, D_MODEL), ML_V)
    rt_w_in = dense(ks[11], (N_RET, D_MODEL, 2 * RT_QK + 2 * RT_V), D_MODEL)
    rt_norm = gain(ks[12], (N_RET, RT_V))
    rt_w_out = dense(ks[13], (N_RET, RT_V, D_MODEL), RT_V)
    ffn_w_gu = dense(ks[14], (DEPTH, D_MODEL, 2 * D_FF), D_MODEL)
    ffn_w_down = dense(ks[15], (DEPTH, D_FF, D_MODEL), D_FF)
    return {'x': x, 'meta_tokens': meta_tokens, 'norm_mix': norm_mix, 'norm_ffn': norm_ffn,
            'norm_final': norm_final, 'ml_w_in': ml_w_in, 'ml_b_gate': ml_b_gate,
            'ml_w_conv': ml_w_conv, 'ml_norm': ml_norm, 'ml_w_out': ml_w_out,
            'rt_w_in': rt_w_in, 'rt_norm': rt_norm, 'rt_w_out': rt_w_out,
            'ffn_w_gu': ffn_w_gu, 'ffn_w_down': ffn_w_down}

def reference(x, meta_tokens, norm_mix, norm_ffn, norm_final, ml_w_in, ml_b_gate, ml_w_conv,
              ml_norm, ml_w_out, rt_w_in, rt_norm, rt_w_out, ffn_w_gu, ffn_w_down):
    B = x.shape[0]
    meta = jnp.broadcast_to(meta_tokens.astype(x.dtype)[None], (B, N_META, D_MODEL))
    pad = jnp.zeros((B, N_PAD, D_MODEL), x.dtype)
    h = jnp.concatenate([pad, meta, x], axis=1)
    L = h.shape[1]
    valid = jnp.arange(L) >= N_PAD
    pos = jnp.arange(L, dtype=jnp.int32) - N_PAD
    for layer in range(DEPTH):
        j = layer // 2
        hn = rmsnorm(h, norm_mix[layer])
        if layer % 2 == 0:
            h = h + mlstm_mixer(hn, valid, ml_w_in[j], ml_b_gate[j], ml_w_conv[j], ml_norm[j], ml_w_out[j])
        else:
            h = h + retention_mixer(hn, valid, pos, rt_w_in[j], rt_norm[j], rt_w_out[j])
        h = h + swiglu(rmsnorm(h, norm_ffn[layer]), ffn_w_gu[layer], ffn_w_down[layer])
    return rmsnorm(h, norm_final)[:, CHUNK:, :]


_drawn_inputs = setup_inputs


def setup_inputs(seed=0):
    import zlib

    import numpy as np

    out = dict(_drawn_inputs(seed))
    spreads = {}
    factors = {'norm_ffn': 2.817, 'norm_final': 2.87, 'ml_norm': 3.822, 'rt_norm': 6.486}
    for name, (base, spread) in spreads.items():
        noise = np.random.default_rng([zlib.crc32(name.encode()), seed]).standard_normal(out[name].shape)
        drawn = base * np.exp(spread * noise) if base else spread * noise
        out[name] = __import__('jax').numpy.asarray(drawn.astype(out[name].dtype))
    for name, factor in factors.items():
        out[name] = (out[name] * factor).astype(out[name].dtype)
    return out
```

```python
import concourse.bass as bass
from concourse import mybir
from contextlib import ExitStack

D_MODEL, SEQ, META, CHUNK = 1024, 512, 16, 64
NT = META + SEQ
HALF = NT // 2
KT = D_MODEL // 128
XT = SEQ // 128
D_FF = ((8 * D_MODEL + 3 * 256 - 1) // (3 * 256)) * 256
FT = D_FF // 128
ML_HEADS, RT_HEADS = 8, 4
PAIRS = ML_HEADS // 2
YT = 16
GATE_CAP, EPS = 15.0, 1e-6
DOWN_SPLIT = ((0, 8), (8, 7), (15, 7))
JT0, JT1, JT2, JT3, JM, JMM, WSW = 0, 512, 896, 1152, 1280, 1792, 1920
WS_AT = (JT0, JT1, JT2, JT3)

STAGES = (
    ("norm0", 0, 0, 0, KT, 0), ("mlstm", 6 * PAIRS, 3 * PAIRS, 3 * PAIRS, ML_HEADS, 0),
    ("out0", KT, KT // 2, KT // 2, 0, KT), ("norm1", 0, 0, 0, KT, 0),
    ("up0", 2 * FT, FT, 0, FT, 0), ("down0", 3 * KT, KT // 2, KT // 2, 0, KT),
    ("norm2", 0, 0, 0, KT, 0), ("reten", 12 * RT_HEADS, 6 * RT_HEADS, 6 * RT_HEADS, 16, 0),
    ("out1", 2 * KT, KT // 2, KT // 2, 0, KT), ("norm3", 0, 0, 0, KT, 0),
    ("up1", 2 * FT, FT, 0, FT, 0), ("down1", 3 * KT, KT // 2, KT // 2, 0, KT),
    ("norm4", 0, 0, 0, 0, 0),
)
PANELS = sum(s[1] for s in STAGES)


class Start:

    def __init__(self, stage):
        before = STAGES[:[s[0] for s in STAGES].index(stage)]
        self.panel, drain0, drain1, self.piece, res = (sum(s[c] for s in before) for c in range(1, 6))
        self.drain = (drain0, drain1)
        self.res = KT + res


def build_hybrid(nc, h_in, stream, w_gates, small, pair_par, rope_tab, decay_tab, ident_in, out):
    f32, f32r = mybir.dt.float32, mybir.dt.float32r
    ALU, ACT, AX = mybir.AluOpType, mybir.ActivationFunctionType, mybir.AxisListType

    with ExitStack() as keep:
        def sb(name, shape, dt=f32, ctx=keep):
            return ctx.enter_context(nc.sbuf_tensor(name, shape, dt))

        def sem(name):
            return keep.enter_context(nc.semaphore(name))

        h = sb("h", [128, KT, NT])
        x_hi, x_lo = sb("x_hi", [128, KT, NT], f32r), sb("x_lo", [128, KT, NT], f32r)
        y_hi, y_lo = sb("y_hi", [128, YT, NT], f32r), sb("y_lo", [128, YT, NT], f32r)
        raw = [sb(f"raw{s}", [128, KT, 128]) for s in range(2)]
        w_hi = [sb(f"w_hi{s}", [128, KT, 128], f32r) for s in range(2)]
        w_lo = [sb(f"w_lo{s}", [128, KT, 128], f32r) for s in range(2)]
        src = sb("src", [128, 2, NT])
        square = sb("square", [128, NT])
        sumsq = sb("sumsq", [128, NT])
        rstd = sb("rstd", [128, NT])
        ident = sb("ident", [128, 128])
        ones = sb("ones", [128, 128])
        par = sb("par", [128, small.shape[1]])
        gain = [par[:, KT * r:KT * (r + 1)] for r in range(5)]
        ret_gain = par[:, 5 * KT:5 * KT + 16]
        b_gate = par[:, 5 * KT + 16:5 * KT + 17]
        eps = sb("eps", [128, 1])
        stat = sb("stat", [128, 64])

        with ExitStack() as c:
            v_T = sb("v_T", [128, 2, NT], f32, c)
            v_tok = sb("v_tok", [128, 5, 2, 130], f32, c)
            q_raw = sb("q_raw", [128, 3 + NT], f32, c)
            k_raw = sb("k_raw", [128, 3 + NT], f32, c)
            qs, ks = sb("qs", [128, NT], f32, c), sb("ks", [128, NT], f32, c)
            o_sig = sb("o_sig", [128, 2, NT], f32, c)
            ws = sb("ws", [128, 2, WSW], f32, c)
            hs = sb("hs", [128, 2, 6, 128], f32, c)
            l_row = sb("l_row", [128, 2, NT], f32, c)
            a_row = sb("a_row", [128, 2, SEQ], f32, c)
            dec = sb("dec", [128, 2, XT, 128], f32, c)
            dec_m = sb("dec_m", [META, 2, META], f32, c)
            cols = sb("cols", [128, 20, ML_HEADS], f32, c)
            cols_p = sb("cols_p", [128, 20, 2], f32, c)
            pair_all = sb("pair_all", [128, PAIRS, 10], f32, c)
            pair_p = sb("pair_p", [128, 8], f32, c)
            pair_g = sb("pair_g", [128, 2], f32, c)
            nst = sb("nst", [128, 2, 5, 6], f32, c)
            b_cap = sb("b_cap", [40, 1], f32, c)
        wg_raw = a_row[:, 0, 0:16 * KT].rearrange("p (k n) -> p k n", k=KT)
        wg_hi = y_hi[:, 0, 0:40 * KT].rearrange("p (k n) -> p k n", k=KT)
        wg_lo = y_hi[:, 1, 0:40 * KT].rearrange("p (k n) -> p k n", k=KT)
        gate_rows = ws[:, :, :].rearrange("p a b -> p (a b)")
        tanh_rows = l_row[0:40, 0, :]
        sp_row = l_row[0:ML_HEADS, 1, :]
        li_row = gate_rows[0:ML_HEADS, 0:NT]
        lf_row = gate_rows[0:ML_HEADS, NT:2 * NT]
        e_row = gate_rows[0:ML_HEADS, 2 * NT:3 * NT]
        c_row = [gate_rows[0:ML_HEADS, (3 + t) * NT:(4 + t) * NT] for t in range(4)]
        hsq = src[:, :, :].rearrange("p a b -> p (a b)")[:, 0:768].rearrange("p (a b) -> p a b", a=6)

        with ExitStack() as c:
            z_hi = sb("z_hi", [128, FT - YT, NT], f32r, c)
            z_lo = sb("z_lo", [128, FT - YT, NT], f32r, c)
            silu_g = sb("silu_g", [128, 2, NT], f32, c)

        with ExitStack() as c:
            rv_T = sb("rv_T", [128, 2, NT], f32, c)
            rv_tok = sb("rv_tok", [128, 5, 512], f32, c)
            rq = sb("rq", [128, 2, NT], f32, c)
            rk = sb("rk", [128, 2, NT], f32, c)
            rtmp = sb("rtmp", [128, NT], f32, c)
            cos_sin = sb("cos_sin", [128, 2, NT], f32, c)
            rdec = sb("rdec", [128, SEQ], f32, c)
            rdec_m = sb("rdec_m", [META, SEQ], f32, c)
            rws = sb("rws", [128, JMM], f32, c)
            rgate = sb("rgate", [128, 4, SEQ], f32, c)
            rhs_n = sb("rhs_n", [128, XT, 512], f32, c)
            bn6 = sb("bn6", [128, XT, 6], f32, c)
            mv = sb("mv", [128, XT, 2], f32, c)
            rsd = sb("rsd", [128, XT], f32, c)

        slot = [keep.enter_context(nc.psum_tensor(f"slot{s}", [128, 2, 512], f32)) for s in range(2)]
        bank = keep.enter_context(nc.psum_tensor("bank", [128, 4, 512], f32))
        l_dram = nc.dram_tensor("l_dram", (ML_HEADS, NT), f32, kind="Internal").ap()

        h_loaded, par_loaded, gate_w_loaded = sem("h_loaded"), sem("par_loaded"), sem("gate_w_loaded")
        consts_set = sem("consts_set")
        raw_loaded = [sem("raw_loaded0"), sem("raw_loaded1")]
        w_hi_done, w_lo_done, panel_done = sem("w_hi_done"), sem("w_lo_done"), sem("panel_done")
        drained = [sem("slot0_drained"), sem("slot1_drained")]
        piece_ready, piece_hi, piece_lo = sem("piece_ready"), sem("piece_hi"), sem("piece_lo")
        squared, summed, cleared = sem("squared"), sem("summed"), sem("sumsq_cleared")
        stat_done, std_done, rstd_done = sem("stat_done"), sem("std_done"), sem("rstd_done")
        out_ready, out_stored = sem("out_ready"), sem("out_stored")
        wg_hi_done, wg_lo_done, gates_done = sem("wg_hi_done"), sem("wg_lo_done"), sem("gates_done")
        gate_act, gate_dve = sem("gate_act"), sem("gate_dve")
        l_stored, l_loaded, cols_done, cols_out = sem("l_stored"), sem("l_loaded"), sem("cols_done"), sem("cols_out")
        conv_step = sem("conv_step")
        qs_done, ks_done = sem("qs_done"), sem("ks_done")
        v_turned, v_tok_done = sem("v_turned"), sem("v_tok_done")
        pair_set, diff_done, a_row_done, dec_exp, dec_done = (
            sem("pair_set"), sem("diff_done"), sem("a_row_done"), sem("dec_exp"), sem("dec_done"))
        gain_set, sub_done = sem("gain_set"), sem("sub_done")
        scores_done, ws_done, mix_done = sem("scores_done"), sem("ws_done"), sem("mix_done")
        den_done, rden_done, num_done, hsq_done, ss_done, rms_done, rrms_done, hs_done = (
            sem(n) for n in ("den_done", "rden_done", "num_done", "hsq_done", "ss_done", "rms_done",
                             "rrms_done", "hs_done"))
        y_turned, up_gate = sem("y_turned"), sem("up_gate")
        rope_loaded, rope_step, rv_turned, rv_tok_done = (
            sem("rope_loaded"), sem("rope_step"), sem("rv_turned"), sem("rv_tok_done"))
        rdec_loaded, rgate_done = sem("rdec_loaded"), sem("rgate_done")
        rscores_done, rws_done, rmix_done = sem("rscores_done"), sem("rws_done"), sem("rmix_done")
        bn_done, mv_done, rsd_done, rrsd_done, rhs_done, ry_turned = (
            sem(n) for n in ("bn_done", "mv_done", "rsd_done", "rrsd_done", "rhs_done", "ry_turned"))

        ALL_COLS = ((0, 0, HALF), (1, HALF, HALF))
        X_COLS = ((0, META, SEQ),)

        def slot_view(s, all_tokens):
            return slot[s][:, :, 0:HALF] if all_tokens else slot[s][:, 0, :]

        def row_view(ap, all_tokens):
            return ap.rearrange("p (a b) -> p a b", a=2) if all_tokens else ap[:, META:NT]

        def dyn(t, m):
            return t[:, bass.ds(m, 1), :].rearrange("p a b -> p (a b)")

        def col(ap, m):
            return ap[:, m:m + 1]

        block = keep.enter_context(nc.Block())

        @block.sync
        def _(sp):
            for c in range(2):
                sp.dma_start(h[:, 4 * c:4 * c + 4, :], h_in[:, 4 * c:4 * c + 4, :]).then_inc(h_loaded, 16)
            sp.dma_start(par[:, :], small).then_inc(par_loaded, 16)
            sp.dma_start(ident[:, :], ident_in).then_inc(par_loaded, 16)
            sp.dma_start(wg_raw[:, :, :], w_gates).then_inc(gate_w_loaded, 16)
            sp.dma_start(pair_all[:, :, :], pair_par).then_inc(par_loaded, 16)

            def load(i, s):
                sp.dma_start(raw[s][:, :, :].rearrange("p k n -> p (k n)"),
                             stream[bass.ds(2 * i + s, 1), :, :].rearrange("a p n -> (a p) n")
                             ).then_inc(raw_loaded[s], 16)

            load(0, 0)
            load(0, 1)
            with sp.Fori(1, PANELS // 2) as i:
                for s in range(2):
                    sp.wait_ge(w_lo_done, 2 * i + s - 1)
                    load(i, s)
            for k in range(KT):
                sp.wait_ge(out_ready, k + 1)
                sp.dma_start(out[:, k, :], h[:, k, META:NT]).then_inc(out_stored, 16)
            sp.wait_ge(out_stored, 16 * KT)

        @block.gpsimd
        def _(pool):
            nc.gpsimd.memset(ones[:, :], 1.0).then_inc(consts_set, 1)
            nc.gpsimd.memset(eps[:, :], EPS).then_inc(consts_set, 1)
            nc.gpsimd.memset(wg_hi[:, :, :].bitcast(f32), 0.0).then_inc(consts_set, 1)
            nc.gpsimd.memset(wg_lo[:, :, :].bitcast(f32), 0.0).then_inc(consts_set, 1)
            nc.gpsimd.memset(sumsq[:, :], 0.0).then_inc(consts_set, 1)

            def split_lo(n, s):
                pool.wait_ge(w_hi_done, n + 1)
                nc.gpsimd.tensor_tensor(w_lo[s][:, :, :], raw[s][:, :, :], w_hi[s][:, :, :].bitcast(f32),
                                        ALU.subtract).then_inc(w_lo_done, 1)

            def piece_low(c, dst, hi, b, cs):
                pool.wait_ge(piece_hi, c + 1)
                nc.gpsimd.tensor_tensor(dst[:, cs], src[:, b, cs], hi[:, cs].bitcast(f32),
                                        ALU.subtract).then_inc(piece_lo, 1)

            def norm(stage, cs):
                st = Start(stage)
                for k in range(KT):
                    piece_low(st.piece + k, x_lo[:, k, :], x_hi[:, k, :], k % 2, cs)

            EVERY, X = slice(0, NT), slice(META, NT)
            split_lo(0, 0)
            split_lo(1, 1)
            pool.wait_ge(wg_hi_done, 2)
            nc.gpsimd.tensor_tensor(wg_lo[:, :, 0:8], wg_raw[:, :, 0:8], wg_hi[:, :, 0:8].bitcast(f32),
                                    ALU.subtract).then_inc(wg_lo_done, 1)
            nc.gpsimd.tensor_tensor(wg_lo[:, :, 32:40], wg_raw[:, :, 8:16], wg_hi[:, :, 32:40].bitcast(f32),
                                    ALU.subtract).then_inc(wg_lo_done, 1)
            norm("norm0", EVERY)
            nc.gpsimd.memset(q_raw[:, 0:3], 0.0).then_inc(consts_set, 1)
            nc.gpsimd.memset(k_raw[:, 0:3], 0.0).then_inc(consts_set, 1)
            nc.gpsimd.memset(v_tok[:, :, :, 128:130], 1.0).then_inc(consts_set, 1)
            nc.gpsimd.memset(cols[:, :, :], 0.0).then_inc(consts_set, 1)

            st = Start("mlstm")

            def mlstm_y(p):
                for e in range(2):
                    piece_low(st.piece + 2 * p + e, dyn(y_lo, 2 * p + e), dyn(y_hi, 2 * p + e), e, EVERY)

            def mlstm(p, first):
                n = st.panel + 6 * p
                for j in range(4):
                    split_lo(n + j + 2, j % 2)
                    if j == 2 and not first:
                        mlstm_y(p - 1)
                split_lo(n + 6, 0)
                split_lo(n + 7, 1)

            mlstm(0, True)
            with pool.Fori(1, PAIRS) as p:
                mlstm(p, False)
            mlstm_y(PAIRS - 1)

            def splits(stage, count):
                st = Start(stage)
                with pool.Fori(0, count // 2) as i:
                    for s in range(2):
                        split_lo(st.panel + 2 * i + s + 2, s)

            def up(stage, cs):
                st = Start(stage)

                def two_tiles(i, base, hi, lo):
                    for c in range(2):
                        split_lo(st.panel + 4 * (i + base) + 2 * c + 2, 0)
                        split_lo(st.panel + 4 * (i + base) + 2 * c + 3, 1)
                        piece_low(st.piece + 2 * (i + base) + c, dyn(lo, 2 * i + c), dyn(hi, 2 * i + c), c, cs)

                with pool.Fori(0, YT // 2) as i:
                    two_tiles(i, 0, y_hi, y_lo)
                with pool.Fori(0, (FT - YT) // 2) as i:
                    two_tiles(i, YT // 2, z_hi, z_lo)

            splits("out0", KT)
            norm("norm1", EVERY)
            up("up0", EVERY)
            splits("down0", 3 * KT)
            norm("norm2", EVERY)

            str_ = Start("reten")

            def reten_y(p):
                for e in range(4):
                    piece_low(str_.piece + 4 * p + e, dyn(y_lo, 4 * p + e), dyn(y_hi, 4 * p + e), e % 2, X)

            def reten(p, first):
                n = str_.panel + 12 * p
                for j in range(12):
                    split_lo(n + j + 2, j % 2)
                    if j == 2 and not first:
                        reten_y(p - 1)

            reten(0, True)
            with pool.Fori(1, RT_HEADS) as p:
                reten(p, False)
            reten_y(RT_HEADS - 1)
            splits("out1", 2 * KT)
            norm("norm3", X)
            up("up1", X)
            st_last = Start("down1")
            with pool.Fori(0, 3 * KT // 2 - 1) as i:
                for s in range(2):
                    split_lo(st_last.panel + 2 * i + s + 2, s)

        @block.scalar
        def _(act):
            def split_hi(half, s, first=False):
                act.wait_ge(raw_loaded[s], 16 * (half + 1))
                if not first:
                    act.wait_ge(panel_done, 2 * half + s - 1)
                nc.scalar.activation(w_hi[s][:, :, :], raw[s][:, :, :], ACT.Copy).then_inc(w_hi_done, 1)

            def piece_high(c, dst, b, cs):
                act.wait_ge(piece_ready, c + 1)
                nc.scalar.activation(dst[:, cs], src[:, b, cs], ACT.Copy).then_inc(piece_hi, 1)

            def norm(stage, r, cs, n_stat):
                st = Start(stage)
                act.wait_ge(stat_done, r + 1)
                full = cs.start == 0
                ins = bank[:, 0:2, 0:HALF] if full else bank[:, 0, :]
                if r > 0:
                    act.wait_ge(rstd_done, r)
                nc.scalar.activation(row_view(rstd[:, :], full), ins, ACT.Sqrt, bias=eps[:, 0:1],
                                     scale=1.0 / D_MODEL).then_inc(std_done, 1)
                if r < 4:
                    for k in range(KT):
                        piece_high(st.piece + k, x_hi[:, k, :], k % 2, cs)

            EVERY, X = slice(0, NT), slice(META, NT)
            act.wait_ge(consts_set, 5)
            split_hi(0, 0, True)
            split_hi(0, 1, True)
            act.wait_ge(gate_w_loaded, 16)
            nc.scalar.activation(wg_hi[:, :, 0:8], wg_raw[:, :, 0:8], ACT.Copy).then_inc(wg_hi_done, 1)
            nc.scalar.activation(wg_hi[:, :, 32:40], wg_raw[:, :, 8:16], ACT.Copy).then_inc(wg_hi_done, 1)
            norm("norm0", 0, EVERY, 1)
            act.wait_ge(par_loaded, 48)
            nc.scalar.activation(b_cap[:, :], b_gate[0:40, :], ACT.Copy, scale=1.0 / GATE_CAP).then_inc(gate_act, 1)
            act.wait_ge(gate_act, 1)
            act.wait_ge(gates_done, 1)
            for b in range(2):
                nc.scalar.activation(tanh_rows[:, b * HALF:(b + 1) * HALF], bank[0:40, b, 0:HALF], ACT.Tanh,
                                     bias=b_cap[:, 0:1], scale=1.0 / GATE_CAP).then_inc(gate_act, 1)
            act.wait_ge(gate_act, 3)
            nc.scalar.activation(sp_row, tanh_rows[32:40, :], ACT.Exp, scale=-GATE_CAP).then_inc(gate_act, 1)
            act.wait_ge(gate_act, 4)
            nc.scalar.activation(sp_row, sp_row, ACT.Ln, bias=1.0).then_inc(gate_act, 1)
            act.wait_ge(gate_dve, 6)
            act.dma_start(l_dram, lf_row).then_inc(l_stored, 16)
            act.wait_ge(gate_dve, 24)
            for t in range(XT):
                w = META + 128 * t
                nc.scalar.activation(c_row[t][:, 0:w], c_row[t][:, 0:w], ACT.Exp).then_inc(gate_act, 1)
            act.wait_ge(l_stored, 16)

            st = Start("mlstm")

            def mlstm_rms(p):
                for e in range(2):
                    act.wait_ge(ss_done, 2 * p + e + 1)
                    nc.scalar.activation(nst[:, e, 3, :], nst[:, e, 2, :], ACT.Sqrt, bias=eps[:, 0:1],
                                         scale=1.0 / 128).then_inc(rms_done, 1)

            def mlstm_y(p):
                for e in range(2):
                    piece_high(st.piece + 2 * p + e, dyn(y_hi, 2 * p + e), e, EVERY)

            def mlstm(p, first):
                half = st.panel // 2 + 3 * p
                if not first:
                    act.wait_ge(diff_done, p)
                    act.wait_ge(a_row_done, p)
                act.dma_start(l_row[:, :, :], l_dram[bass.ds(2 * p, 2), :].partition_broadcast(128)
                              ).then_inc(l_loaded, 16)
                for j in range(2):
                    split_hi(half + 1, j)
                    nc.scalar.activation(row_view(v_T[:, j, :], True), slot_view(j, True),
                                         ACT.Copy).then_inc(drained[j], 1)
                if not first:
                    mlstm_rms(p - 1)
                split_hi(half + 2, 0)
                if first:
                    act.wait_ge(consts_set, 9)
                else:
                    act.wait_ge(conv_step, 8 * p - 4)
                nc.scalar.activation(row_view(q_raw[:, 3:3 + NT], True), slot_view(0, True),
                                     ACT.Copy).then_inc(drained[0], 1)
                if not first:
                    mlstm_y(p - 1)
                split_hi(half + 2, 1)
                if not first:
                    act.wait_ge(conv_step, 8 * p)
                nc.scalar.activation(row_view(k_raw[:, 3:3 + NT], True), slot_view(1, True),
                                     ACT.Copy).then_inc(drained[1], 1)
                act.wait_ge(conv_step, 8 * p + 4)
                nc.scalar.activation(qs[:, :], qs[:, :], ACT.Silu).then_inc(qs_done, 1)
                act.wait_ge(v_turned, p + 1)
                for e in range(2):
                    nc.scalar.activation(v_tok[:, 0:4, e, 0:128],
                                         bank[:, e, :].rearrange("p (t n) -> p t n", t=4), ACT.Copy)
                nc.scalar.activation(v_tok[0:META, 4, :, 0:128],
                                     bank[0:META, 2, 0:256].rearrange("p (e n) -> p e n", e=2),
                                     ACT.Copy).then_inc(v_tok_done, 1)
                split_hi(half + 3, 0)
                nc.scalar.activation(row_view(o_sig[:, 0, :], True), slot_view(0, True),
                                     ACT.Sigmoid).then_inc(drained[0], 1)
                act.wait_ge(conv_step, 8 * p + 8)
                nc.scalar.activation(ks[:, :], ks[:, :], ACT.Silu).then_inc(ks_done, 1)
                act.wait_ge(l_loaded, 16 * (p + 1))
                if not first:
                    act.wait_ge(ws_done, 2 * p)
                nc.scalar.activation(a_row[:, :, :], l_row[:, :, META:NT], ACT.Exp).then_inc(a_row_done, 1)
                act.wait_ge(diff_done, p + 1)
                for e in range(2):
                    for t in range(XT):
                        nc.scalar.activation(dec[:, e, t, :], dec[:, e, t, :], ACT.Exp, scale=-1.0,
                                             bias=cols_p[:, 16 + t, e:e + 1])
                    last = nc.scalar.activation(dec_m[:, e, :], dec_m[:, e, :], ACT.Exp, scale=-1.0,
                                                bias=cols_p[0:META, 5, e:e + 1])
                last.then_inc(dec_exp, 1)
                split_hi(half + 3, 1)
                nc.scalar.activation(row_view(o_sig[:, 1, :], True), slot_view(1, True),
                                     ACT.Sigmoid).then_inc(drained[1], 1)

            mlstm(0, True)
            with act.Fori(1, PAIRS) as p:
                mlstm(p, False)
            mlstm_rms(PAIRS - 1)
            mlstm_y(PAIRS - 1)

            def splits(stage, count):
                half = Start(stage).panel // 2
                with act.Fori(0, count // 2) as i:
                    for s in range(2):
                        split_hi(half + i + 1, s)

            def up(stage, cs):
                st = Start(stage)
                full = cs.start == 0

                def two_tiles(i, base, hi):
                    for c in range(2):
                        split_hi(st.panel // 2 + 2 * (i + base) + c + 1, 0)
                        act.wait_ge(piece_ready, st.piece + 2 * (i + base) + c - 1)
                        nc.scalar.activation(row_view(silu_g[:, c, :], full), slot_view(0, full),
                                             ACT.Silu).then_inc(drained[0], 1)
                        split_hi(st.panel // 2 + 2 * (i + base) + c + 1, 1)
                        piece_high(st.piece + 2 * (i + base) + c, dyn(hi, 2 * i + c), c, cs)

                with act.Fori(0, YT // 2) as i:
                    two_tiles(i, 0, y_hi)
                with act.Fori(0, (FT - YT) // 2) as i:
                    two_tiles(i, YT // 2, z_hi)

            splits("out0", KT)
            norm("norm1", 1, EVERY, 1)
            up("up0", EVERY)
            splits("down0", 3 * KT)
            act.wait_ge(stat_done, 3)
            act.dma_start(cos_sin[:, :, :], rope_tab).then_inc(rope_loaded, 16)
            norm("norm2", 2, EVERY, 1)

            sr = Start("reten")

            def reten_y(p):
                for e in range(4):
                    piece_high(sr.piece + 4 * p + e, dyn(y_hi, 4 * p + e), e % 2, X)

            def reten_rsd(p):
                act.wait_ge(mv_done, 4 * p + 4)
                nc.scalar.activation(rsd[:, :], mv[:, :, 1], ACT.Sqrt, bias=eps[:, 0:1]).then_inc(rsd_done, 1)

            def reten_v_tok(p, j):
                act.wait_ge(rv_turned, 4 * p + j + 1)
                nc.scalar.activation(rv_tok[:, 0:4, 128 * j:128 * j + 128],
                                     bank[:, 2 * (j % 2), :].rearrange("p (t n) -> p t n", t=4), ACT.Copy)
                nc.scalar.activation(rv_tok[0:META, 4, 128 * j:128 * j + 128],
                                     bank[0:META, 2 * (j % 2) + 1, 0:128], ACT.Copy).then_inc(rv_tok_done, 1)

            def reten(p, first):
                half = sr.panel // 2 + 6 * p
                if not first:
                    act.wait_ge(rws_done, p)
                act.dma_start(rdec[:, :], decay_tab[bass.ds(p, 1), 0:128, :].rearrange("a p n -> (a p) n")
                              ).then_inc(rdec_loaded, 16)
                act.dma_start(rdec_m[:, :],
                              decay_tab[bass.ds(p, 1), 128:128 + META, :].rearrange("a p n -> (a p) n")
                              ).then_inc(rdec_loaded, 16)
                split_hi(half + 1, 0)
                split_hi(half + 1, 1)
                if not first:
                    reten_rsd(p - 1)
                split_hi(half + 2, 0)
                if not first:
                    reten_y(p - 1)
                split_hi(half + 2, 1)
                for j in range(4):
                    if j >= 2:
                        reten_v_tok(p, j - 2)
                    split_hi(half + 3 + j // 2, j % 2)
                    nc.scalar.activation(row_view(rv_T[:, j % 2, :], True), slot_view(j % 2, True),
                                         ACT.Copy).then_inc(drained[j % 2], 1)
                for j in range(4):
                    if j < 2:
                        reten_v_tok(p, j + 2)
                    split_hi(half + 5 + j // 2, j % 2)
                    nc.scalar.activation(rgate[:, j, :], slot_view(j % 2, False), ACT.Silu
                                         ).then_inc(drained[j % 2], 1)

            reten(0, True)
            with act.Fori(1, RT_HEADS) as p:
                reten(p, False)
            reten_rsd(RT_HEADS - 1)
            reten_y(RT_HEADS - 1)
            splits("out1", 2 * KT)
            norm("norm3", 3, X, 1)
            up("up1", X)
            half = Start("down1").panel // 2
            with act.Fori(0, 3 * KT // 2 - 1) as i:
                for s in range(2):
                    split_hi(half + i + 1, s)
            norm("norm4", 4, X, 1)

        @block.vector
        def _(dve):
            def add_square(res, m, cs):
                nc.vector.tensor_tensor(square[:, cs], dyn(h, m)[:, cs], dyn(h, m)[:, cs],
                                        ALU.mult).then_inc(squared, 1)
                dve.wait_ge(squared, res + 1)
                nc.vector.tensor_tensor(sumsq[:, cs], sumsq[:, cs], square[:, cs], ALU.add).then_inc(summed, 1)

            def residual(stage, res, drains, n_last, m, s, cs):
                full = cs.start == 0
                dve.wait_ge(panel_done, n_last + 1)
                hv = row_view(dyn(h, m), full)
                nc.vector.tensor_tensor(hv, hv, slot_view(s, full), ALU.add).then_inc(drained[s], 1)
                dve.wait_ge(drained[s], drains)
                dve.wait_ge(summed, res)
                add_square(res, m, cs)

            def norm(stage, r, cs):
                st = Start(stage)
                full = cs.start == 0
                dve.wait_ge(std_done, r + 1)
                nc.vector.reciprocal(rstd[:, cs], rstd[:, cs]).then_inc(rstd_done, 1)
                if r < 4:
                    nc.vector.memset(sumsq[:, :], 0.0).then_inc(cleared, 1)
                dve.wait_ge(rstd_done, r + 1)
                for k in range(KT):
                    if r == 4:
                        nc.vector.scalar_tensor_tensor(
                            out=h[:, k, cs], in0=h[:, k, cs], scalar=col(gain[r], k), in1=rstd[:, cs],
                            op0=ALU.mult, op1=ALU.mult).then_inc(out_ready, 1)
                        continue
                    if st.piece + k >= 2:
                        dve.wait_ge(piece_lo, st.piece + k - 1)
                    nc.vector.scalar_tensor_tensor(
                        out=src[:, k % 2, cs], in0=h[:, k, cs], scalar=col(gain[r], k), in1=rstd[:, cs],
                        op0=ALU.mult, op1=ALU.mult).then_inc(piece_ready, 1)

            EVERY, X = slice(0, NT), slice(META, NT)
            dve.wait_ge(h_loaded, 32)
            dve.wait_ge(consts_set, 5)
            for k in range(KT):
                if k > 0:
                    dve.wait_ge(summed, k)
                add_square(k, k, EVERY)
            dve.wait_ge(par_loaded, 48)
            norm("norm0", 0, EVERY)

            g = [0]

            def link(ins):
                g[0] += 1
                ins.then_inc(gate_dve, 1)
                dve.wait_ge(gate_dve, g[0])

            dve.wait_ge(gate_act, 5)
            link(nc.vector.tensor_scalar(li_row, tanh_rows[0:ML_HEADS, :], GATE_CAP, None, ALU.mult))
            tiles = [(0, META)] + [(META + 128 * t, 128) for t in range(XT)]
            for a, w in tiles:
                link(nc.vector.tensor_tensor_scan(lf_row[:, a:a + w], ones[0:ML_HEADS, 0:w], sp_row[:, a:a + w],
                                                  0.0, ALU.mult, ALU.subtract))
            link(nc.vector.tensor_tensor(e_row, li_row, lf_row, ALU.subtract))
            for t in range(4):
                a, w = tiles[t]
                link(nc.vector.tensor_scalar(e_row[:, a:a + w], e_row[:, a:a + w], lf_row[:, a + w - 1:a + w],
                                             None, ALU.add))
            link(nc.vector.tensor_copy(c_row[0][:, 0:META], e_row[:, 0:META]))
            for t in range(3):
                a, w = tiles[t + 1]
                link(nc.vector.tensor_scalar(c_row[t + 1][:, 0:a], c_row[t][:, 0:a], lf_row[:, a + w - 1:a + w],
                                             None, ALU.add))
                link(nc.vector.tensor_copy(c_row[t + 1][:, a:a + w], e_row[:, a:a + w]))
            for _ in range(24 - g[0]):
                link(nc.vector.memset(stat[:, 0:1], 0.0))
            scale = (D_MODEL // ML_HEADS // 2) ** -0.5
            dve.wait_ge(cols_done, 1)
            dve.wait_ge(consts_set, 9)
            pc = bank[:, 3, 0:160].rearrange("p (c h) -> p c h", h=ML_HEADS)
            nc.vector.tensor_scalar(cols[0:META, 0:4, :], pc[0:META, 0:4, :], scale, None, ALU.mult)
            nc.vector.tensor_copy(cols[0:META, 4:6, :], pc[0:META, 4:6, :])
            nc.vector.tensor_scalar(cols[:, 6:12, :], pc[:, 6:12, :], scale, None, ALU.mult)
            nc.vector.tensor_copy(cols[:, 12:20, :], pc[:, 12:20, :]).then_inc(cols_out, 1)
            dve.wait_ge(cols_out, 1)
            nc.vector.memset(ws[0:META, :, JMM + META:WSW], 0.0).then_inc(cols_out, 1)

            st = Start("mlstm")

            def mlstm_norm(p):
                for e in range(2):
                    c = 2 * p + e
                    dve.wait_ge(mix_done, c + 1)
                    o = bank[:, 2 * e:2 * e + 2, 0:480].rearrange("p a (b n) -> p a b n", b=3)
                    den = nst[:, e, 0, :].rearrange("p (a b) -> p a b", a=2)
                    nc.vector.tensor_scalar(den, o[:, :, :, 128], -1.0, 1.0, ALU.mult, ALU.max
                                            ).then_inc(den_done, 1)
                    dve.wait_ge(den_done, 2 * c + 1)
                    nc.vector.tensor_tensor(den, o[:, :, :, 128], den, ALU.max).then_inc(den_done, 1)
                    dve.wait_ge(den_done, 2 * c + 2)
                    nc.vector.reciprocal(nst[:, e, 1, :], nst[:, e, 0, :]).then_inc(rden_done, 1)
                    dve.wait_ge(rden_done, c + 1)
                    for a in range(2):
                        last = nc.vector.tensor_tensor(
                            hs[:, e, 3 * a:3 * a + 3, :], o[:, a, :, 0:128],
                            nst[:, e, 1, 3 * a:3 * a + 3].unsqueeze(2).to_broadcast([128, 3, 128]), ALU.mult)
                    last.then_inc(num_done, 1)
                    dve.wait_ge(num_done, c + 1)
                    dve.wait_ge(piece_lo, st.piece + 2 * p)
                    nc.vector.tensor_tensor(hsq, hs[:, e, :, :], hs[:, e, :, :], ALU.mult).then_inc(hsq_done, 1)
                    dve.wait_ge(hsq_done, c + 1)
                    nc.vector.reduce_sum(nst[:, e, 2, :], hsq, AX.X).then_inc(ss_done, 1)
                for e in range(2):
                    c = 2 * p + e
                    dve.wait_ge(rms_done, c + 1)
                    nc.vector.reciprocal(nst[:, e, 4, :], nst[:, e, 3, :]).then_inc(rrms_done, 1)
                    dve.wait_ge(rrms_done, c + 1)
                    nc.vector.tensor_tensor(hs[:, e, :, :], hs[:, e, :, :],
                                            nst[:, e, 4, :].unsqueeze(2).to_broadcast([128, 6, 128]),
                                            ALU.mult).then_inc(hs_done, 1)

            def conv(p, c, raw_rows, dst):
                dve.wait_ge(drained[c], st.drain[c] + 3 * p + 2)
                nc.vector.tensor_scalar(dst[:, :], raw_rows[:, 3:3 + NT], pair_p[:, 4 * c + 3:4 * c + 4], None,
                                        ALU.mult).then_inc(conv_step, 1)
                for tap in range(3):
                    dve.wait_ge(conv_step, 8 * p + 4 * c + tap + 1)
                    nc.vector.scalar_tensor_tensor(
                        out=dst[:, :], in0=raw_rows[:, tap:tap + NT], scalar=pair_p[:, 4 * c + tap:4 * c + tap + 1],
                        in1=dst[:, :], op0=ALU.mult, op1=ALU.add).then_inc(conv_step, 1)

            def mlstm_y(p):
                nc.vector.tensor_copy(pair_g[:, :], pair_all[:, bass.ds(p, 1), 8:10].rearrange("p a b -> p (a b)")
                                      ).then_inc(gain_set, 1)
                dve.wait_ge(gain_set, p + 1)
                for e in range(2):
                    dve.wait_ge(y_turned, 2 * p + e + 1)
                    dve.wait_ge(piece_lo, st.piece + 2 * p + e - 1)
                    nc.vector.scalar_tensor_tensor(
                        out=src[:, e, 0:META], in0=bank[:, 2 * e + 1, 0:META], scalar=pair_g[:, e:e + 1],
                        in1=o_sig[:, e, 0:META], op0=ALU.mult, op1=ALU.mult)
                    nc.vector.scalar_tensor_tensor(
                        out=src[:, e, META:NT], in0=bank[:, 2 * e, :], scalar=pair_g[:, e:e + 1],
                        in1=o_sig[:, e, META:NT], op0=ALU.mult, op1=ALU.mult).then_inc(piece_ready, 1)

            def weigh(p, e):
                dve.wait_ge(scores_done, 2 * p + e + 1)
                dve.wait_ge(dec_done, p + 1)
                at = [bank[:, 0, :], bank[:, 1, 0:384], bank[:, 2, 0:256], bank[:, 1, 384:512]]
                for jt in range(XT):
                    w0 = WS_AT[jt]
                    nc.vector.scalar_tensor_tensor(out=ws[:, e, w0:w0 + 128], in0=at[jt][:, 0:128], scalar=scale,
                                                   in1=dec[:, e, jt, :], op0=ALU.mult, op1=ALU.mult)
                    for t in range(jt + 1, XT):
                        o = 128 * (t - jt)
                        idx = 6 + t * (t - 1) // 2 + jt
                        nc.vector.scalar_tensor_tensor(
                            out=ws[:, e, w0 + o:w0 + o + 128], in0=at[jt][:, o:o + 128],
                            scalar=cols_p[:, idx, e:e + 1], in1=a_row[:, e, 128 * t:128 * t + 128],
                            op0=ALU.mult, op1=ALU.mult)
                for t in range(XT):
                    nc.vector.scalar_tensor_tensor(
                        out=ws[0:META, e, JM + 128 * t:JM + 128 * t + 128],
                        in0=bank[0:META, 3, 128 * t:128 * t + 128], scalar=cols_p[0:META, t, e:e + 1],
                        in1=a_row[0:META, e, 128 * t:128 * t + 128], op0=ALU.mult, op1=ALU.mult)
                nc.vector.scalar_tensor_tensor(
                    out=ws[0:META, e, JMM:JMM + META], in0=bank[0:META, 2, 256:256 + META], scalar=scale,
                    in1=dec_m[:, e, :], op0=ALU.mult, op1=ALU.mult).then_inc(ws_done, 1)

            def mlstm(p, first):
                if not first:
                    mlstm_norm(p - 1)
                nc.vector.tensor_copy(pair_p[:, :], pair_all[:, bass.ds(p, 1), 0:8].rearrange("p a b -> p (a b)")
                                      ).then_inc(pair_set, 1)
                nc.vector.tensor_copy(cols_p[:, :, :], cols[:, :, bass.ds(2 * p, 2)]).then_inc(pair_set, 1)
                dve.wait_ge(pair_set, 2 * p + 2)
                conv(p, 0, q_raw, qs)
                if not first:
                    mlstm_y(p - 1)
                dve.wait_ge(l_loaded, 16 * (p + 1))
                for e in range(2):
                    for t in range(XT):
                        a = META + 128 * t
                        nc.vector.tensor_scalar(dec[:, e, t, :], l_row[:, e, a:a + 128], cols_p[:, 12 + t, e:e + 1],
                                                None, ALU.subtract)
                    last = nc.vector.tensor_scalar(dec_m[:, e, :], l_row[0:META, e, 0:META],
                                                   cols_p[0:META, 4, e:e + 1], None, ALU.subtract)
                last.then_inc(sub_done, 1)
                dve.wait_ge(sub_done, p + 1)
                for d in (dec[:, :, :, :].rearrange("p e t n -> p (e t n)"),
                          dec_m[:, :, :].rearrange("p e n -> p (e n)")):
                    last = nc.vector.scalar_tensor_tensor(out=d, in0=d, scalar=-1.0, in1=d, op0=ALU.mult,
                                                          op1=ALU.max)
                last.then_inc(diff_done, 1)
                conv(p, 1, k_raw, ks)
                dve.wait_ge(dec_exp, p + 1)
                nc.vector.memset(dec[64:128, :, :, 0:64], 0.0).then_inc(dec_done, 1)
                weigh(p, 0)
                weigh(p, 1)

            mlstm(0, True)
            with dve.Fori(1, PAIRS) as p:
                mlstm(p, False)
            mlstm_norm(PAIRS - 1)
            mlstm_y(PAIRS - 1)

            def out_proj(stage, r, cs, panels, iters=KT // 2):
                st = Start(stage)
                dve.wait_ge(cleared, r)
                with dve.Fori(0, iters) as i:
                    for c in range(2):
                        residual(stage, st.res + 2 * i + c, st.drain[c] + i + 1,
                                 st.panel + panels * (2 * i + c) + panels - 1, 2 * i + c, c, cs)

            def up(stage, cs):
                st = Start(stage)
                full = cs.start == 0

                def two_tiles(i, base):
                    for c in range(2):
                        f = 2 * (i + base) + c
                        dve.wait_ge(drained[0], st.drain[0] + f + 1)
                        dve.wait_ge(panel_done, st.panel + 2 * f + 2)
                        dve.wait_ge(piece_lo, st.piece + f - 1)
                        nc.vector.tensor_tensor(row_view(src[:, c, :], full), row_view(silu_g[:, c, :], full),
                                                slot_view(1, full), ALU.mult).then_inc(piece_ready, 1)

                with dve.Fori(0, FT // 2) as i:
                    two_tiles(i, 0)

            out_proj("out0", 1, EVERY, 1)
            norm("norm1", 1, EVERY)
            up("up0", EVERY)
            out_proj("down0", 2, EVERY, 3)
            norm("norm2", 2, EVERY)

            sr = Start("reten")

            def rope_first(p, c, dst, full):
                n = sr.panel + 12 * p + 2 * c
                cs = EVERY if full else X
                dve.wait_ge(panel_done, n + 1)
                nc.vector.tensor_tensor(row_view(dst[:, 0, :], full), slot_view(0, full),
                                        row_view(cos_sin[:, 0, :], full), ALU.mult).then_inc(rope_step, 1)
                nc.vector.tensor_tensor(row_view(dst[:, 1, :], full), slot_view(0, full),
                                        row_view(cos_sin[:, 1, :], full), ALU.mult).then_inc(drained[0], 1)

            def rope_second(p, c, dst, full):
                n = sr.panel + 12 * p + 2 * c + 1
                cs = EVERY if full else X
                done = 8 * p + 4 * c
                dve.wait_ge(rope_step, done + 1)
                dve.wait_ge(panel_done, n + 1)
                nc.vector.tensor_tensor(row_view(rtmp[:, :], full), slot_view(1, full),
                                        row_view(cos_sin[:, 1, :], full), ALU.mult).then_inc(rope_step, 1)
                dve.wait_ge(rope_step, done + 2)
                nc.vector.tensor_tensor(dst[:, 0, cs], dst[:, 0, cs], rtmp[:, cs],
                                        ALU.subtract).then_inc(rope_step, 1)
                dve.wait_ge(rope_step, done + 3)
                nc.vector.tensor_tensor(row_view(rtmp[:, :], full), slot_view(1, full),
                                        row_view(cos_sin[:, 0, :], full), ALU.mult).then_inc(drained[1], 1)
                dve.wait_ge(drained[1], sr.drain[1] + 6 * p + c + 1)
                dve.wait_ge(drained[0], sr.drain[0] + 6 * p + c + 1)
                nc.vector.tensor_tensor(dst[:, 1, cs], dst[:, 1, cs], rtmp[:, cs],
                                        ALU.add).then_inc(rope_step, 1)

            def reten_norm(p):
                for t in range(XT):
                    c = 4 * p + t
                    dve.wait_ge(rmix_done, c + 1)
                    nc.vector.bn_stats(bn6[:, t, :], bank[:, t, :]).then_inc(bn_done, 1)
                dve.wait_ge(bn_done, 4 * p + 4)
                nc.vector.memset(rsd[:, :], 0.0)
                for t in range(XT):
                    nc.vector.bn_aggr(mv[:, t, :], bn6[:, t, :]).then_inc(mv_done, 1)
                dve.wait_ge(rsd_done, p + 1)
                nc.vector.reciprocal(rsd[:, :], rsd[:, :]).then_inc(rrsd_done, 1)
                dve.wait_ge(rrsd_done, p + 1)
                for t in range(XT):
                    nc.vector.tensor_scalar(rhs_n[:, t, :], bank[:, t, :], mv[:, t, 0:1], rsd[:, t:t + 1],
                                            ALU.subtract, ALU.mult).then_inc(rhs_done, 1)

            def reten_y(p):
                nc.vector.tensor_copy(stat[:, 4:8], ret_gain[:, bass.ds(4 * p, 4)]).then_inc(gain_set, 1)
                dve.wait_ge(gain_set, PAIRS + p + 1)
                for e in range(4):
                    dve.wait_ge(ry_turned, 4 * p + e + 1)
                    dve.wait_ge(piece_lo, sr.piece + 4 * p + e - 1)
                    nc.vector.scalar_tensor_tensor(
                        out=src[:, e % 2, X], in0=bank[:, e, :], scalar=stat[:, 4 + e:5 + e],
                        in1=rgate[:, e, :], op0=ALU.mult, op1=ALU.mult).then_inc(piece_ready, 1)

            def reten(p, first):
                rope_first(p, 0, rq, False)
                if not first:
                    reten_norm(p - 1)
                rope_second(p, 0, rq, False)
                rope_first(p, 1, rk, True)
                if not first:
                    reten_y(p - 1)
                rope_second(p, 1, rk, True)
                dve.wait_ge(rscores_done, p + 1)
                dve.wait_ge(rdec_loaded, 32 * (p + 1))
                at = [bank[:, 0, :], bank[:, 1, 0:384], bank[:, 2, 0:256], bank[:, 1, 384:512]]
                for jt in range(XT):
                    w = SEQ - 128 * jt
                    nc.vector.tensor_tensor(rws[:, WS_AT[jt]:WS_AT[jt] + w], at[jt], rdec[:, 0:w], ALU.mult)
                nc.vector.tensor_tensor(rws[0:META, JM:JM + SEQ], bank[0:META, 3, :], rdec_m[:, :],
                                        ALU.mult).then_inc(rws_done, 1)

            dve.wait_ge(rope_loaded, 16)
            reten(0, True)
            with dve.Fori(1, RT_HEADS) as p:
                reten(p, False)
            reten_norm(RT_HEADS - 1)
            reten_y(RT_HEADS - 1)
            out_proj("out1", 3, X, 2)
            norm("norm3", 3, X)
            up("up1", X)
            out_proj("down1", 4, X, 3)
            norm("norm4", 4, X)

        @block.tensor
        def _(pe):
            def panel(n, s, out_slot, xs, cols_, first=True, last=True):
                pe.wait_ge(w_lo_done, n + 1)
                for k, (hi, lo) in enumerate(xs):
                    if callable(hi):
                        hi, lo = hi()
                    for w, x in ((w_hi, hi), (w_hi, lo), (w_lo, hi)):
                        for b, a, width in cols_:
                            mm = nc.tensor.matmul(
                                slot[out_slot][:, b, 0:width], w[s][:, k, :], x[:, a:a + width],
                                start=first and k == 0 and w is w_hi and x is hi,
                                stop=last and k == len(xs) - 1 and w is w_lo)
                mm.then_inc(panel_done, 1)

            def x_tiles(st):
                def tile(k):
                    def get():
                        pe.wait_ge(piece_lo, st.piece + k + 1)
                        return x_hi[:, k, :], x_lo[:, k, :]
                    return get, None
                return [tile(k) for k in range(KT)]

            X_READY = [(x_hi[:, k, :], x_lo[:, k, :]) for k in range(KT)]

            def norm(r, cs, res):
                pe.wait_ge(summed, res)
                if cs.start == 0:
                    for b in range(2):
                        mm = nc.tensor.matmul(bank[:, b, 0:HALF], ones[:, :], sumsq[:, b * HALF:(b + 1) * HALF],
                                              start=True, stop=True)
                else:
                    mm = nc.tensor.matmul(bank[:, 0, :], ones[:, :], sumsq[:, META:NT], start=True, stop=True)
                mm.then_inc(stat_done, 1)

            EVERY, X = slice(0, NT), slice(META, NT)
            pe.wait_ge(consts_set, 5)
            norm(0, EVERY, KT)
            pe.wait_ge(wg_lo_done, 2)
            pe.wait_ge(std_done, 1)
            for k in range(KT):
                pe.wait_ge(piece_lo, k + 1)
                for w, x in ((wg_hi, x_hi), (wg_hi, x_lo), (wg_lo, x_hi)):
                    for b in range(2):
                        mm = nc.tensor.matmul(bank[0:40, b, 0:HALF], w[:, k, :], x[:, k, b * HALF:(b + 1) * HALF],
                                              start=k == 0 and w is wg_hi and x is x_hi,
                                              stop=k == KT - 1 and w is wg_lo)
            mm.then_inc(gates_done, 1)

            st = Start("mlstm")

            def mlstm_mix(p):
                pe.wait_ge(ws_done, 2 * p + 2)
                for e in range(2):
                    blocks = [-1, 0, 1, 2, 3, -1]
                    for b, t in enumerate(blocks):
                        o = bank[:, 2 * e + b // 3, 160 * (b % 3):160 * (b % 3) + 129]
                        m0 = JMM if t < 0 else JM + 128 * t
                        mm = nc.tensor.matmul(o, ws[0:META, e, m0:m0 + 128], v_tok[0:META, 4, e, 0:129],
                                              start=True, stop=t < 0)
                        for jt in range(t + 1):
                            w0 = WS_AT[jt] + 128 * (t - jt)
                            mm = nc.tensor.matmul(o, ws[:, e, w0:w0 + 128], v_tok[:, jt, e, 0:129],
                                                  start=False, stop=jt == t)
                    mm.then_inc(mix_done, 1)

            def mlstm_turn(p):
                for e in range(2):
                    pe.wait_ge(hs_done, 2 * p + e + 1)
                    if e == 0:
                        pe.wait_ge(hs_done, 2 * p + 2)
                    for t in range(XT):
                        nc.tensor.transpose(bank[:, 2 * e, 128 * t:128 * t + 128], hs[:, e, 1 + t, :], ident[:, :])
                    nc.tensor.transpose(bank[:, 2 * e + 1, 0:META], hs[0:META, e, 0, :],
                                        ident[0:META, 0:META]).then_inc(y_turned, 1)

            def gate_columns():
                pe.wait_ge(gate_act, 9)
                pe.wait_ge(par_loaded, 48)
                tiles = [(0, META)] + [(META + 128 * t, 128) for t in range(XT)]
                jobs = [(c_row[t], 0) for t in range(4)] + [(lf_row, 0), (li_row, 0)]
                jobs += [(c_row[t], 1 + j) for t in range(4) for j in range(t)]
                jobs += [(lf_row, 1 + t) for t in range(4)] + [(li_row, 1 + t) for t in range(4)]
                for c, (row, tile) in enumerate(jobs):
                    a, w = tiles[tile]
                    mm = nc.tensor.transpose(bank[0:w, 3, 8 * c:8 * c + 8], row[:, a:a + w],
                                             ident[0:ML_HEADS, 0:ML_HEADS])
                mm.then_inc(cols_done, 1)

            def mlstm_scores(p, e):
                r = slice(64 * e, 64 * e + 64)
                at = [bank[:, 0, :], bank[:, 1, 0:384], bank[:, 2, 0:256], bank[:, 1, 384:512]]
                for jt in range(XT):
                    a = META + 128 * jt
                    nc.tensor.matmul(at[jt], ks[r, a:a + 128], qs[r, a:NT], start=True, stop=True)
                nc.tensor.matmul(bank[0:META, 3, :], ks[r, 0:META], qs[r, META:NT], start=True, stop=True)
                nc.tensor.matmul(bank[0:META, 2, 256:256 + META], ks[r, 0:META], qs[r, 0:META],
                                 start=True, stop=True).then_inc(scores_done, 1)

            def mlstm(p, first):
                n, d0, d1 = st.panel + 6 * p, st.drain[0] + 3 * p, st.drain[1] + 3 * p
                xs = x_tiles(st0) if first else X_READY
                if not first:
                    pe.wait_ge(drained[0], d0)
                panel(n, 0, 0, xs, ALL_COLS)
                if not first:
                    mlstm_mix(p - 1)
                    pe.wait_ge(drained[1], d1)
                panel(n + 1, 1, 1, X_READY, ALL_COLS)
                pe.wait_ge(drained[0], d0 + 1)
                panel(n + 2, 0, 0, X_READY, ALL_COLS)
                if first:
                    gate_columns()
                else:
                    mlstm_turn(p - 1)
                pe.wait_ge(drained[1], d1 + 1)
                panel(n + 3, 1, 1, X_READY, ALL_COLS)
                if not first:
                    pe.wait_ge(piece_ready, st.piece + 2 * p)
                for e in range(2):
                    for t in range(XT):
                        a = META + 128 * t
                        nc.tensor.transpose(bank[:, e, 128 * t:128 * t + 128], v_T[:, e, a:a + 128], ident[:, :])
                    mm = nc.tensor.transpose(bank[0:META, 2, 128 * e:128 * e + 128], v_T[:, e, 0:META], ident[:, :])
                mm.then_inc(v_turned, 1)
                pe.wait_ge(drained[0], d0 + 2)
                panel(n + 4, 0, 0, X_READY, ALL_COLS)
                pe.wait_ge(qs_done, p + 1)
                pe.wait_ge(ks_done, p + 1)
                pe.wait_ge(v_tok_done, p + 1)
                if first:
                    pe.wait_ge(cols_out, 2)
                mlstm_scores(p, 0)
                pe.wait_ge(drained[1], d1 + 2)
                panel(n + 5, 1, 1, X_READY, ALL_COLS)
                pe.wait_ge(ws_done, 2 * p + 1)
                mlstm_scores(p, 1)

            st0 = Start("norm0")
            mlstm(0, True)
            with pe.Fori(1, PAIRS) as p:
                mlstm(p, False)
            mlstm_mix(PAIRS - 1)
            mlstm_turn(PAIRS - 1)

            def y_tile(k):
                return (y_hi[:, k, :], y_lo[:, k, :]) if k < YT else (z_hi[:, k - YT, :], z_lo[:, k - YT, :])

            def out_proj(stage, groups, cols_, last_piece):
                st = Start(stage)
                per = len(groups)
                pe.wait_ge(piece_lo, last_piece)
                with pe.Fori(0, KT // 2) as i:
                    for c in range(2):
                        pe.wait_ge(drained[c], st.drain[c] + i)
                        for g, (k0, kn) in enumerate(groups):
                            j = per * c + g
                            panel(st.panel + 2 * per * i + j, j % 2, c, [y_tile(k) for k in range(k0, k0 + kn)],
                                  cols_, first=g == 0, last=g == per - 1)

            def up(stage, stx, cols_):
                st = Start(stage)

                def two_tiles(i):
                    for c in range(2):
                        f = 2 * i + c
                        pe.wait_ge(drained[0], st.drain[0] + f)
                        panel(st.panel + 2 * f, 0, 0, x_tiles(stx) if c == 0 else X_READY, cols_)
                        pe.wait_ge(piece_ready, st.piece + f)
                        panel(st.panel + 2 * f + 1, 1, 1, X_READY, cols_)

                with pe.Fori(0, FT // 2) as i:
                    two_tiles(i)

            out_proj("out0", ((0, 8),), ALL_COLS, Start("norm1").piece)
            norm(1, EVERY, 2 * KT)
            up("up0", Start("norm1"), ALL_COLS)
            out_proj("down0", DOWN_SPLIT, ALL_COLS, Start("norm2").piece)
            norm(2, EVERY, 3 * KT)

            sr = Start("reten")

            def reten_mix(p):
                pe.wait_ge(rws_done, p + 1)
                for t in range(XT):
                    nc.tensor.matmul(bank[:, t, :], rws[0:META, JM + 128 * t:JM + 128 * t + 128],
                                     rv_tok[0:META, 4, :], start=True, stop=False)
                    for jt in range(t + 1):
                        w0 = WS_AT[jt] + 128 * (t - jt)
                        mm = nc.tensor.matmul(bank[:, t, :], rws[:, w0:w0 + 128], rv_tok[:, jt, :],
                                              start=False, stop=jt == t)
                    mm.then_inc(rmix_done, 1)

            def reten_turn(p):
                pe.wait_ge(rhs_done, 4 * p + 4)
                for e in range(4):
                    for t in range(XT):
                        mm = nc.tensor.transpose(bank[:, e, 128 * t:128 * t + 128],
                                                 rhs_n[:, t, 128 * e:128 * e + 128], ident[:, :])
                    mm.then_inc(ry_turned, 1)

            def reten_v_turn(p, j):
                b = 2 * (j % 2)
                pe.wait_ge(drained[j % 2], sr.drain[j % 2] + 6 * p + 3 + j // 2)
                if j >= 2:
                    pe.wait_ge(rv_tok_done, 4 * p + j - 1)
                for t in range(XT):
                    a = META + 128 * t
                    nc.tensor.transpose(bank[:, b, 128 * t:128 * t + 128], rv_T[:, j % 2, a:a + 128], ident[:, :])
                nc.tensor.transpose(bank[0:META, b + 1, 0:128], rv_T[:, j % 2, 0:META],
                                    ident[:, :]).then_inc(rv_turned, 1)

            def reten(p, first):
                n = sr.panel + 12 * p
                d = [sr.drain[0] + 6 * p, sr.drain[1] + 6 * p]
                for j in range(12):
                    pe.wait_ge(drained[j % 2], d[j % 2] + j // 2)
                    xs = x_tiles(Start("norm2")) if first and j == 0 else X_READY
                    panel(n + j, j % 2, j % 2, xs, ALL_COLS if 2 <= j < 8 else X_COLS)
                    if not first and j == 0:
                        reten_mix(p - 1)
                    if not first and j == 2:
                        reten_turn(p - 1)
                    if j == 5:
                        if not first:
                            pe.wait_ge(piece_ready, sr.piece + 4 * p)
                        reten_v_turn(p, 0)
                    if 6 <= j <= 8:
                        reten_v_turn(p, j - 5)
                    if j == 9:
                        pe.wait_ge(rope_step, 8 * p + 8)
                        pe.wait_ge(rv_tok_done, 4 * p + 4)
                        at = [bank[:, 0, :], bank[:, 1, 0:384], bank[:, 2, 0:256], bank[:, 1, 384:512]]
                        for jt in range(XT):
                            a = META + 128 * jt
                            for kk in range(2):
                                nc.tensor.matmul(at[jt], rk[:, kk, a:a + 128], rq[:, kk, a:NT],
                                                 start=kk == 0, stop=kk == 1)
                        for kk in range(2):
                            mm = nc.tensor.matmul(bank[0:META, 3, :], rk[:, kk, 0:META], rq[:, kk, META:NT],
                                                  start=kk == 0, stop=kk == 1)
                        mm.then_inc(rscores_done, 1)

            reten(0, True)
            with pe.Fori(1, RT_HEADS) as p:
                reten(p, False)
            reten_mix(RT_HEADS - 1)
            reten_turn(RT_HEADS - 1)
            out_proj("out1", ((0, 8), (8, 8)), X_COLS, Start("norm3").piece)
            norm(3, X, 4 * KT)
            up("up1", Start("norm3"), X_COLS)
            out_proj("down1", DOWN_SPLIT, X_COLS, Start("norm4").piece)
            norm(4, X, 5 * KT)


def kernel(x, meta_tokens, norm_mix, norm_ffn, norm_final, ml_w_in, ml_b_gate, ml_w_conv, ml_norm,
           ml_w_out, rt_w_in, rt_norm, rt_w_out, ffn_w_gu, ffn_w_down):
    import numpy as np
    import concourse.bacc as bacc
    from concourse.bass_utils import run_bass_kernel_spmd

    f = np.float32
    arr = [np.asarray(a) for a in (x, meta_tokens, norm_mix, norm_ffn, norm_final, ml_w_in, ml_b_gate,
                                   ml_w_conv, ml_norm, ml_w_out, rt_w_in, rt_norm, rt_w_out, ffn_w_gu, ffn_w_down)]
    (x, meta_tokens, norm_mix, norm_ffn, norm_final, ml_w_in, ml_b_gate, ml_w_conv, ml_norm, ml_w_out,
     rt_w_in, rt_norm, rt_w_out, ffn_w_gu, ffn_w_down) = arr

    def tiles(v):
        return v.reshape(-1, 128).T

    h_in = np.concatenate([meta_tokens, x[0]], 0).T.reshape(KT, 128, NT).transpose(1, 0, 2)
    small = np.zeros((128, 5 * KT + 17), f)
    for r, v in enumerate((norm_mix[0], norm_ffn[0], norm_mix[1], norm_ffn[1], norm_final)):
        small[:, KT * r:KT * (r + 1)] = tiles(v)
    small[:, 5 * KT:5 * KT + 16] = tiles(rt_norm[0])
    small[0:8, 5 * KT + 16] = ml_b_gate[0, 0:8]
    small[32:40, 5 * KT + 16] = ml_b_gate[0, 8:16]
    pair = np.zeros((128, PAIRS, 10), f)
    for p in range(PAIRS):
        pair[:, p, 0:4] = ml_w_conv[0, :, 128 * p:128 * p + 128].T
        pair[:, p, 4:8] = ml_w_conv[0, :, 512 + 128 * p:512 + 128 * p + 128].T
        pair[:, p, 8:10] = tiles(ml_norm[0])[:, 2 * p:2 * p + 2]

    stream = np.zeros((PANELS, 128, KT, 128), f)
    at = 0

    def put(w, c, k0=0, kn=KT):
        nonlocal at
        stream[at, :, 0:kn, :] = w[128 * k0:128 * (k0 + kn), 128 * c:128 * c + 128].reshape(kn, 128, 128
                                                                                         ).transpose(1, 0, 2)
        at += 1

    def ffn(layer):
        for c in range(FT):
            put(ffn_w_gu[layer], c)
            put(ffn_w_gu[layer], FT + c)
        for m in range(KT):
            for k0, kn in DOWN_SPLIT:
                put(ffn_w_down[layer], m, k0, kn)

    for p in range(PAIRS):
        for c in (8 + 2 * p, 9 + 2 * p, p, 4 + p, 16 + 2 * p, 17 + 2 * p):
            put(ml_w_in[0], c)
    for m in range(KT):
        put(ml_w_out[0], m)
    ffn(0)
    for p in range(RT_HEADS):
        for c in [2 * p, 2 * p + 1, 8 + 2 * p, 9 + 2 * p] + [16 + 4 * p + e for e in range(4)] + \
                [32 + 4 * p + e for e in range(4)]:
            put(rt_w_in[0], c)
    for m in range(KT):
        put(rt_w_out[0], m, 0, 8)
        put(rt_w_out[0], m, 8, 8)
    ffn(1)

    half = D_MODEL // RT_HEADS // 2
    inv = (f(10000.0) ** (-np.arange(half, dtype=f) / f(half))).astype(f)
    ang = np.arange(NT, dtype=f)[None, :] * inv[:, None]
    rope = np.stack([np.cos(ang), np.sin(ang)], 1).astype(f)
    decay = np.zeros((RT_HEADS, 128 + META, SEQ), f)
    j, i = np.arange(128)[:, None], np.arange(SEQ)[None, :]
    for hd in range(RT_HEADS):
        lg = np.log1p(-np.exp2(-5.0 - hd))
        decay[hd, 0:128] = np.exp(lg * abs(i - j)) * (j // CHUNK <= i // CHUNK) / 16.0
        decay[hd, 128:] = np.exp(lg * (i + META - np.arange(META)[:, None])) / 16.0

    feeds = {
        "h_in": h_in, "stream": stream.reshape(PANELS, 128, KT * 128),
        "w_gates": ml_w_in[0][:, 3072:3088].reshape(KT, 128, 16).transpose(1, 0, 2), "small": small,
        "pair_par": pair, "rope_tab": rope, "decay_tab": decay, "ident_in": np.eye(128, dtype=f),
    }
    feeds = {n: np.ascontiguousarray(a) for n, a in feeds.items()}
    nc = bacc.Bacc("TRN2", target_bir_lowering=False, num_devices=1)
    dt = mybir.dt.float32
    args = [nc.dram_tensor(n, a.shape, dt, kind="ExternalInput").ap() for n, a in feeds.items()]
    out = nc.dram_tensor("out", (128, KT, SEQ), dt, kind="ExternalOutput").ap()
    build_hybrid(nc, *args, out)
    r = run_bass_kernel_spmd(nc, [feeds], core_ids=[0])
    return r.results[0]["out"].transpose(2, 1, 0).reshape(1, SEQ, D_MODEL)
```

```python
import concourse.bass as bass
from concourse import mybir
from contextlib import ExitStack

D_MODEL, SEQ, META, CHUNK = 1024, 512, 16, 64
NT = META + SEQ
HALF = NT // 2
KT = D_MODEL // 128
XT = SEQ // 128
D_FF = ((8 * D_MODEL + 3 * 256 - 1) // (3 * 256)) * 256
FT = D_FF // 128
ML_HEADS, RT_HEADS = 8, 4
PAIRS = ML_HEADS // 2
YT = 16
GATE_CAP, EPS = 15.0, 1e-6
DOWN_SPLIT = ((0, 8), (8, 7), (15, 7))
JT0, JT1, JT2, JT3, JM, JMM, WSW = 0, 512, 896, 1152, 1280, 1792, 1920
WS_AT = (JT0, JT1, JT2, JT3)

POOL_OUT = 3
GATE_STEPS = 1 + 5 + 1 + 4 + 1 + 6

STAGES = (
    ("mlstm", 6 * PAIRS, 3 * PAIRS, 3 * PAIRS, ML_HEADS, 0), ("out0", KT, KT // 2, KT // 2, 0, KT),
    ("up0", 2 * FT, FT, FT, FT, 0), ("down0", 3 * KT, KT // 2, KT // 2, 0, KT),
    ("reten", 12 * RT_HEADS, 6 * RT_HEADS, 6 * RT_HEADS, 16, 0),
    ("out1", 2 * KT, KT // 2, KT // 2, 0, KT),
    ("up1", 2 * FT, FT, FT, FT, 0), ("down1", 3 * KT, KT // 2, KT // 2, 0, KT),
    ("end", 0, 0, 0, 0, 0),
)
PANELS = sum(s[1] for s in STAGES)


class Start:

    def __init__(self, stage):
        before = STAGES[:[s[0] for s in STAGES].index(stage)]
        self.panel, drain0, drain1, self.piece, res = (sum(s[c] for s in before) for c in range(1, 6))
        self.drain = (drain0, drain1)
        self.res = KT + res


def build_hybrid(nc, h_in, stream, w_gates, small, pair_par, rope_tab, decay_tab, ident_in, out):
    f32, f32r = mybir.dt.float32, mybir.dt.float32r
    ALU, ACT, AX = mybir.AluOpType, mybir.ActivationFunctionType, mybir.AxisListType

    with ExitStack() as keep:
        def sb(name, shape, dt=f32, ctx=keep):
            return ctx.enter_context(nc.sbuf_tensor(name, shape, dt))

        def sem(name):
            return keep.enter_context(nc.semaphore(name))

        h = sb("h", [128, KT, NT])
        x_hi, x_lo = sb("x_hi", [128, KT, NT], f32r), sb("x_lo", [128, KT, NT], f32r)
        y_hi, y_lo = sb("y_hi", [128, YT, NT], f32r), sb("y_lo", [128, YT, NT], f32r)
        raw = [sb(f"raw{s}", [128, KT, 128]) for s in range(2)]
        w_hi = [sb(f"w_hi{s}", [128, KT, 128], f32r) for s in range(2)]
        w_lo = [sb(f"w_lo{s}", [128, KT, 128], f32r) for s in range(2)]
        src = sb("src", [128, 2, NT])
        square = sb("square", [128, NT])
        sumsq = sb("sumsq", [128, NT])
        rstd = sb("rstd", [128, NT])
        ident = sb("ident", [128, 128])
        ones = sb("ones", [128, 128])
        par = sb("par", [128, small.shape[1]])
        gain = [par[:, KT * r:KT * (r + 1)] for r in range(5)]
        ret_gain = par[:, 5 * KT:5 * KT + 16]
        b_gate = par[:, 5 * KT + 16:5 * KT + 17]
        eps = sb("eps", [128, 1])
        half_tanh = square
        stat = sb("stat", [128, 64])

        with ExitStack() as c:
            v_T = sb("v_T", [128, 2, NT], f32, c)
            v_tok = sb("v_tok", [128, 5, 2, 130], f32, c)
            q_raw = sb("q_raw", [128, 3 + NT], f32, c)
            k_raw = sb("k_raw", [128, 3 + NT], f32, c)
            qs, ks = sb("qs", [128, NT], f32, c), sb("ks", [128, NT], f32, c)
            o_sig = sb("o_sig", [128, 2, NT], f32, c)
            ws = sb("ws", [128, 2, WSW], f32, c)
            hs = sb("hs", [128, 2, 6, 128], f32, c)
            l_row = sb("l_row", [128, 2, NT], f32, c)
            a_row = sb("a_row", [128, 2, SEQ], f32, c)
            dec = sb("dec", [128, 2, XT, 128], f32, c)
            dec_m = sb("dec_m", [META, 2, META], f32, c)
            cols = sb("cols", [128, 20, ML_HEADS], f32, c)
            cols_p = sb("cols_p", [128, 20, 2], f32, c)
            pair_all = sb("pair_all", [128, PAIRS, 10], f32, c)
            pair_p = sb("pair_p", [128, 8], f32, c)
            pair_g = sb("pair_g", [128, 2], f32, c)
            nst = sb("nst", [128, 2, 5, 6], f32, c)
            b_cap = sb("b_cap", [40, 1], f32, c)
        wg_raw = a_row[:, 0, 0:16 * KT].rearrange("p (k n) -> p k n", k=KT)
        wg_hi = y_hi[:, 0, 0:40 * KT].rearrange("p (k n) -> p k n", k=KT)
        wg_lo = y_hi[:, 1, 0:40 * KT].rearrange("p (k n) -> p k n", k=KT)
        gate_rows = ws[:, :, :].rearrange("p a b -> p (a b)")
        tanh_rows = l_row[0:40, 0, :]
        sp_row = l_row[0:ML_HEADS, 1, :]
        li_row = gate_rows[0:ML_HEADS, 0:NT]
        lf_row = gate_rows[0:ML_HEADS, NT:2 * NT]
        e_row = gate_rows[0:ML_HEADS, 2 * NT:3 * NT]
        c_row = [gate_rows[0:ML_HEADS, (3 + t) * NT:(4 + t) * NT] for t in range(4)]
        hsq = src[:, :, :].rearrange("p a b -> p (a b)")[:, 0:768].rearrange("p (a b) -> p a b", a=6)

        with ExitStack() as c:
            z_hi = sb("z_hi", [128, FT - YT, NT], f32r, c)
            z_lo = sb("z_lo", [128, FT - YT, NT], f32r, c)
            silu_g = sb("silu_g", [128, 2, NT], f32, c)

        with ExitStack() as c:
            rv_T = sb("rv_T", [128, 2, NT], f32, c)
            rv_tok = sb("rv_tok", [128, 5, 512], f32, c)
            rq = sb("rq", [128, 2, NT], f32, c)
            rk = sb("rk", [128, 2, NT], f32, c)
            rtmp = sb("rtmp", [128, NT], f32, c)
            rdec = sb("rdec", [128, SEQ], f32, c)
            cos_sin = sb("cos_sin", [128, 2, NT], f32, c)
            rdec_m = sb("rdec_m", [META, SEQ], f32, c)
            rws = sb("rws", [128, JMM], f32, c)
            rgate = sb("rgate", [128, 4, SEQ], f32, c)
            rhs_n = sb("rhs_n", [128, XT, 512], f32, c)
            bn6 = sb("bn6", [128, XT, 6], f32, c)
            mv = sb("mv", [128, XT, 2], f32, c)
            rsd = sb("rsd", [128, XT], f32, c)

        slot = [keep.enter_context(nc.psum_tensor(f"slot{s}", [128, 2, 512], f32)) for s in range(2)]
        bank = keep.enter_context(nc.psum_tensor("bank", [128, 4, 512], f32))
        l_dram = nc.dram_tensor("l_dram", (ML_HEADS, NT), f32, kind="Internal").ap()

        h_loaded = [sem(f"h_loaded{c}") for c in range(4)]
        par_loaded, tab_loaded, gate_w_loaded = sem("par_loaded"), sem("tab_loaded"), sem("gate_w_loaded")
        consts_set = sem("consts_set")
        raw_loaded = [sem("raw_loaded0"), sem("raw_loaded1")]
        w_hi_done, w_lo_done, panel_done = sem("w_hi_done"), sem("w_lo_done"), sem("panel_done")
        drained = [sem("slot0_drained"), sem("slot1_drained")]
        piece_ready, piece_hi, piece_lo = sem("piece_ready"), sem("piece_hi"), sem("piece_lo")
        x_hi_done, x_split = sem("x_hi_done"), sem("x_split")
        squared, summed, cleared = sem("squared"), sem("summed"), sem("sumsq_cleared")
        stat_done, std_done, rstd_done = sem("stat_done"), sem("std_done"), sem("rstd_done")
        out_ready, out_ready_pool, out_stored = sem("out_ready"), sem("out_ready_pool"), sem("out_stored")
        gained = sem("gained")
        wg_hi_done, wg_lo_done, gates_done = sem("wg_hi_done"), sem("wg_lo_done"), sem("gates_done")
        gate_act, gate_dve = sem("gate_act"), sem("gate_dve")
        l_stored, l_loaded, cols_done, cols_out = sem("l_stored"), sem("l_loaded"), sem("cols_done"), sem("cols_out")
        conv_step, conv_tanh, silu_done = sem("conv_step"), sem("conv_tanh"), sem("silu_done")
        o_tanh, o_done = sem("o_tanh"), sem("o_done")
        v_turned, v_tok_done = sem("v_turned"), sem("v_tok_done")
        pair_set, diff_done, a_row_done, dec_exp, dec_done = (
            sem("pair_set"), sem("diff_done"), sem("a_row_done"), sem("dec_exp"), sem("dec_done"))
        gain_set, sub_done, pair_one = sem("gain_set"), sem("sub_done"), sem("pair_one")
        gates_scaled = sem("gates_scaled")
        scores_done, ws_done, mix_done = sem("scores_done"), sem("ws_done"), sem("mix_done")
        den_done, rden_done, num_done, hsq_done, ss_done, rms_done, rrms_done, hs_done = (
            sem(n) for n in ("den_done", "rden_done", "num_done", "hsq_done", "ss_done", "rms_done",
                             "rrms_done", "hs_done"))
        y_turned, up_silu = sem("y_turned"), sem("up_silu")
        rope_loaded, rope_scaled, rope_step, rv_turned, rv_tok_done = (
            sem("rope_loaded"), sem("rope_scaled"), sem("rope_step"), sem("rv_turned"), sem("rv_tok_done"))
        rdec_loaded, rgate_done = sem("rdec_loaded"), sem("rgate_done")
        rscores_done, rws_done, rmix_done = sem("rscores_done"), sem("rws_done"), sem("rmix_done")
        bn_done, mv_done, rsd_done, rrsd_done, rhs_done, ry_turned = (
            sem(n) for n in ("bn_done", "mv_done", "rsd_done", "rrsd_done", "rhs_done", "ry_turned"))

        ALL_COLS = ((0, 0, HALF), (1, HALF, HALF))
        X_COLS = ((0, META, SEQ),)

        BANKS = [bank[:, b, :] for b in range(4)]
        SLOTS = [slot[b // 2][:, b % 2, :] for b in range(4)]

        def score_blocks(banks):
            return [banks[0], banks[1][:, 0:384], banks[2][:, 0:256], banks[1][:, 384:512]]

        def slot_view(s, all_tokens):
            return slot[s][:, :, 0:HALF] if all_tokens else slot[s][:, 0, :]

        def row_view(ap, all_tokens):
            return ap.rearrange("p (a b) -> p a b", a=2) if all_tokens else ap[:, META:NT]

        def dyn(t, m):
            return t[:, bass.ds(m, 1), :].rearrange("p a b -> p (a b)")

        def col(ap, m):
            return ap[:, m:m + 1]

        block = keep.enter_context(nc.Block())

        @block.sync
        def _(sp):
            sp.dma_start(par[:, :], small).then_inc(par_loaded, 16)
            def load(i, s):
                sp.dma_start(raw[s][:, :, :].rearrange("p k n -> p (k n)"),
                             stream[bass.ds(2 * i + s, 1), :, :].rearrange("a p n -> (a p) n")
                             ).then_inc(raw_loaded[s], 16)

            load(0, 0)
            for c in range(4):
                sp.dma_start(h[:, 2 * c:2 * c + 2, :], h_in[:, 2 * c:2 * c + 2, :]).then_inc(h_loaded[c], 16)
            sp.dma_start(wg_raw[:, :, :], w_gates).then_inc(gate_w_loaded, 16)
            load(0, 1)
            sp.dma_start(ident[:, :], ident_in).then_inc(tab_loaded, 16)
            sp.dma_start(pair_all[:, :, :], pair_par).then_inc(tab_loaded, 16)
            with sp.Fori(1, PANELS // 2) as i:
                for s in range(2):
                    sp.wait_ge(w_lo_done, 2 * i + s - 1)
                    load(i, s)
            for event, n, k in ((out_ready, 1, 3), (out_ready_pool, 1, 0), (out_ready, 2, 4), (out_ready, 3, 5),
                                (out_ready_pool, 2, 1), (out_ready, 4, 6), (out_ready, 5, 7), (out_ready_pool, 3, 2)):
                sp.wait_ge(event, n)
                sp.dma_start(out[:, k, :], h[:, k, META:NT]).then_inc(out_stored, 16)
            sp.wait_ge(out_stored, 16 * KT)

        @block.gpsimd
        def _(pool):
            nc.gpsimd.memset(ones[:, :], 1.0).then_inc(consts_set, 1)
            nc.gpsimd.memset(eps[:, :], EPS).then_inc(consts_set, 1)
            nc.gpsimd.memset(wg_hi[:, :, :].bitcast(f32), 0.0).then_inc(consts_set, 1)
            nc.gpsimd.memset(wg_lo[:, :, :].bitcast(f32), 0.0).then_inc(consts_set, 1)
            nc.gpsimd.memset(sumsq[:, :], 0.0).then_inc(consts_set, 1)

            def split_lo(n, s):
                pool.wait_ge(w_hi_done, n + 1)
                nc.gpsimd.tensor_tensor(w_lo[s][:, :, :], raw[s][:, :, :], w_hi[s][:, :, :].bitcast(f32),
                                        ALU.subtract).then_inc(w_lo_done, 1)

            def piece_low(c, dst, hi, b, cs):
                pool.wait_ge(piece_hi, c + 1)
                nc.gpsimd.tensor_tensor(dst[:, cs], src[:, b, cs], hi[:, cs].bitcast(f32),
                                        ALU.subtract).then_inc(piece_lo, 1)

            EVERY, X = slice(0, NT), slice(META, NT)
            pool.wait_ge(wg_hi_done, 2)
            nc.gpsimd.tensor_tensor(wg_lo[:, :, 0:8], wg_raw[:, :, 0:8], wg_hi[:, :, 0:8].bitcast(f32),
                                    ALU.subtract).then_inc(wg_lo_done, 1)
            nc.gpsimd.tensor_tensor(wg_lo[:, :, 32:40], wg_raw[:, :, 8:16], wg_hi[:, :, 32:40].bitcast(f32),
                                    ALU.subtract).then_inc(wg_lo_done, 1)
            pool.wait_ge(w_lo_done, 1)
            split_lo(1, 1)
            nc.gpsimd.memset(q_raw[:, 0:3], 0.0).then_inc(consts_set, 1)
            nc.gpsimd.memset(k_raw[:, 0:3], 0.0).then_inc(consts_set, 1)
            nc.gpsimd.memset(v_tok[:, :, :, 128:130], 1.0).then_inc(consts_set, 1)
            nc.gpsimd.memset(cols[:, :, :], 0.0).then_inc(consts_set, 1)

            st = Start("mlstm")

            def mlstm_y(p):
                for e in range(2):
                    piece_low(st.piece + 2 * p + e, dyn(y_lo, 2 * p + e), dyn(y_hi, 2 * p + e), e, EVERY)

            def mlstm(p, first):
                n = st.panel + 6 * p
                for j in range(6):
                    split_lo(n + j + 2, j % 2)
                    if j == 4 and not first:
                        mlstm_y(p - 1)

            mlstm(0, True)
            with pool.Fori(1, PAIRS) as p:
                mlstm(p, False)

            def splits(stage, count, done=0):
                st = Start(stage)
                with pool.Fori(done, count // 2) as i:
                    for s in range(2):
                        split_lo(st.panel + 2 * i + s + 2, s)

            def up(stage, cs):
                st = Start(stage)

                def two_tiles(i, base, hi, lo):
                    for c in range(2):
                        split_lo(st.panel + 4 * (i + base) + 2 * c + 2, 0)
                        split_lo(st.panel + 4 * (i + base) + 2 * c + 3, 1)
                        piece_low(st.piece + 2 * (i + base) + c, dyn(lo, 2 * i + c), dyn(hi, 2 * i + c), c, cs)

                with pool.Fori(0, YT // 2) as i:
                    two_tiles(i, 0, y_hi, y_lo)
                with pool.Fori(0, (FT - YT) // 2) as i:
                    two_tiles(i, YT // 2, z_hi, z_lo)

            splits("out0", KT)
            up("up0", EVERY)
            splits("down0", 3 * KT)

            str_ = Start("reten")

            def reten_y(p):
                for e in range(4):
                    piece_low(str_.piece + 4 * p + e, dyn(y_lo, 4 * p + e), dyn(y_hi, 4 * p + e), e % 2, X)

            def reten(p, first):
                n = str_.panel + 12 * p
                for j in range(12):
                    split_lo(n + j + 2, j % 2)
                    if j == 2 and not first:
                        reten_y(p - 1)

            reten(0, True)
            with pool.Fori(1, RT_HEADS) as p:
                reten(p, False)
            splits("out1", 2 * KT)
            up("up1", X)
            st_last = Start("down1")
            with pool.Fori(0, 3 * KT // 2 - 1) as i:
                for s in range(2):
                    split_lo(st_last.panel + 2 * i + s + 2, s)
            pool.wait_ge(gained, POOL_OUT)
            pool.wait_ge(rstd_done, 5)
            for k in range(POOL_OUT):
                nc.gpsimd.tensor_tensor(h[:, k, X], h[:, k, X], rstd[:, X], ALU.mult).then_inc(out_ready_pool, 1)

        @block.scalar
        def _(act):
            def split_hi(half, s, first=False):
                act.wait_ge(raw_loaded[s], 16 * (half + 1))
                if not first:
                    act.wait_ge(panel_done, 2 * half + s - 1)
                nc.scalar.activation(w_hi[s][:, :, :], raw[s][:, :, :], ACT.Copy).then_inc(w_hi_done, 1)

            def piece_high(c, dst, b, cs):
                act.wait_ge(piece_ready, c + 1)
                nc.scalar.activation(dst[:, cs], src[:, b, cs], ACT.Copy).then_inc(piece_hi, 1)

            def row_std(r, cs):
                act.wait_ge(stat_done, r + 1)
                full = cs.start == 0
                ins = bank[:, 0:2, 0:HALF] if full else bank[:, 0, :]
                nc.scalar.activation(row_view(rstd[:, :], full), ins, ACT.Sqrt, bias=eps[:, 0:1],
                                     scale=1.0 / D_MODEL).then_inc(std_done, 1)

            EVERY, X = slice(0, NT), slice(META, NT)
            act.wait_ge(par_loaded, 16)
            nc.scalar.activation(b_cap[:, :], b_gate[0:40, :], ACT.Copy, scale=1.0 / GATE_CAP).then_inc(gate_act, 1)
            act.wait_ge(consts_set, 5)
            split_hi(0, 0, True)
            for k in range(KT):
                if k % 2 == 0:
                    act.wait_ge(h_loaded[k // 2], 16)
                nc.scalar.activation(x_hi[:, k, :], h[:, k, :], ACT.Copy, scale=gain[0][:, k:k + 1]
                                     ).then_inc(x_hi_done, 1)
            act.wait_ge(gate_w_loaded, 16)
            nc.scalar.activation(wg_hi[:, :, 0:8], wg_raw[:, :, 0:8], ACT.Copy).then_inc(wg_hi_done, 1)
            nc.scalar.activation(wg_hi[:, :, 32:40], wg_raw[:, :, 8:16], ACT.Copy).then_inc(wg_hi_done, 1)
            split_hi(0, 1, True)
            for k in range(KT):
                if k >= 2:
                    act.wait_ge(summed, k - 1)
                nc.scalar.activation(src[:, k % 2, :], h[:, k, :], ACT.Square).then_inc(squared, 1)

            def gates():
                act.wait_ge(gate_act, 1)
                act.wait_ge(gates_scaled, 1)
                nc.scalar.activation(tanh_rows, tanh_rows, ACT.Tanh, bias=b_cap[:, 0:1], scale=1.0 / GATE_CAP
                                     ).then_inc(gate_act, 1)
                act.wait_ge(gate_act, 2)
                nc.scalar.activation(sp_row, tanh_rows[32:40, :], ACT.Exp, scale=-GATE_CAP).then_inc(gate_act, 1)
                act.wait_ge(gate_act, 3)
                nc.scalar.activation(sp_row, sp_row, ACT.Ln, bias=1.0).then_inc(gate_act, 1)

            def gate_exps():
                act.wait_ge(gate_dve, GATE_STEPS)
                act.dma_start(l_dram, lf_row).then_inc(l_stored, 16)
                for t in range(XT):
                    w = META + 128 * t
                    nc.scalar.activation(c_row[t][:, 0:w], c_row[t][:, 0:w], ACT.Exp).then_inc(gate_act, 1)
                act.wait_ge(l_stored, 16)

            st = Start("mlstm")

            def mlstm_rms(p):
                for e in range(2):
                    act.wait_ge(ss_done, 2 * p + e + 1)
                    nc.scalar.activation(nst[:, e, 3, :], nst[:, e, 2, :], ACT.Sqrt, bias=eps[:, 0:1],
                                         scale=1.0 / 128).then_inc(rms_done, 1)

            def mlstm_y(p):
                for e in range(2):
                    piece_high(st.piece + 2 * p + e, dyn(y_hi, 2 * p + e), e, EVERY)

            def conv_half_tanh(p, c, rows):
                act.wait_ge(conv_step, 8 * p + 4 * c + 4)
                if c == 1:
                    act.wait_ge(silu_done, 2 * p + 1)
                nc.scalar.activation(half_tanh[:, :], rows[:, :], ACT.Tanh, scale=0.5).then_inc(conv_tanh, 1)

            def load_l_rows(p):
                act.dma_start(l_row[:, :, :], l_dram[bass.ds(2 * p, 2), :].partition_broadcast(128)
                              ).then_inc(l_loaded, 16)

            def decays(p, first):
                act.wait_ge(l_loaded, 16 * (p + 1))
                if not first:
                    act.wait_ge(ws_done, 2 * p)
                nc.scalar.activation(a_row[:, :, :], l_row[:, :, META:NT], ACT.Exp).then_inc(a_row_done, 1)
                act.wait_ge(diff_done, p + 1)
                for e in range(2):
                    for t in range(XT):
                        nc.scalar.activation(dec[:, e, t, :], dec[:, e, t, :], ACT.Exp, scale=-1.0,
                                             bias=cols_p[:, 16 + t, e:e + 1])
                    last = nc.scalar.activation(dec_m[:, e, :], dec_m[:, e, :], ACT.Exp, scale=-1.0,
                                                bias=cols_p[0:META, 5, e:e + 1])
                last.then_inc(dec_exp, 1)

            def mlstm(p, first):
                half = st.panel // 2 + 3 * p
                if not first:
                    act.wait_ge(diff_done, p)
                    act.wait_ge(a_row_done, p)
                    load_l_rows(p)
                split_hi(half + 1, 0)
                if first:
                    row_std(0, EVERY)
                split_hi(half + 1, 1)
                if first:
                    gates()
                split_hi(half + 2, 0)
                if first:
                    gate_exps()
                    load_l_rows(0)
                else:
                    decays(p, False)
                conv_half_tanh(p, 0, qs)
                if not first:
                    mlstm_rms(p - 1)
                split_hi(half + 2, 1)
                conv_half_tanh(p, 1, ks)
                split_hi(half + 3, 0)
                if first:
                    decays(0, True)
                else:
                    mlstm_y(p - 1)
                split_hi(half + 3, 1)
                for e in range(2):
                    act.wait_ge(drained[e], st.drain[e] + 3 * p + 3)
                    nc.scalar.activation(o_sig[:, e, :], o_sig[:, e, :], ACT.Tanh, scale=0.5).then_inc(o_tanh, 1)
                act.wait_ge(v_turned, p + 1)
                for e in range(2):
                    nc.scalar.activation(v_tok[:, 0:4, e, 0:128],
                                         bank[:, e, :].rearrange("p (t n) -> p t n", t=4), ACT.Copy)
                nc.scalar.activation(v_tok[0:META, 4, :, 0:128],
                                     bank[0:META, 2, 0:256].rearrange("p (e n) -> p e n", e=2),
                                     ACT.Copy).then_inc(v_tok_done, 1)

            mlstm(0, True)
            with act.Fori(1, PAIRS) as p:
                mlstm(p, False)
            mlstm_rms(PAIRS - 1)
            mlstm_y(PAIRS - 1)

            def splits(stage, count, done=0):
                half = Start(stage).panel // 2
                with act.Fori(done, count // 2) as i:
                    for s in range(2):
                        split_hi(half + i + 1, s)

            def up(stage, cs):
                st = Start(stage)

                def two_tiles(i, base, hi):
                    for c in range(2):
                        f = 2 * (i + base) + c
                        split_hi(st.panel // 2 + f + 1, 0)
                        act.wait_ge(drained[0], st.drain[0] + f + 1)
                        nc.scalar.activation(silu_g[:, c, cs], silu_g[:, c, cs], ACT.Silu).then_inc(up_silu, 1)
                        split_hi(st.panel // 2 + f + 1, 1)
                        piece_high(st.piece + f, dyn(hi, 2 * i + c), c, cs)

                with act.Fori(0, YT // 2) as i:
                    two_tiles(i, 0, y_hi)
                with act.Fori(0, (FT - YT) // 2) as i:
                    two_tiles(i, YT // 2, z_hi)

            splits("out0", KT)
            row_std(1, EVERY)
            up("up0", EVERY)
            act.dma_start(cos_sin[:, :, :], rope_tab).then_inc(rope_loaded, 16)
            splits("down0", 3 * KT)

            sr = Start("reten")

            def reten_y(p):
                for e in range(4):
                    piece_high(sr.piece + 4 * p + e, dyn(y_hi, 4 * p + e), e % 2, X)

            def reten_rsd(p):
                act.wait_ge(mv_done, 4 * p + 4)
                nc.scalar.activation(rsd[:, :], mv[:, :, 1], ACT.Sqrt, bias=eps[:, 0:1]).then_inc(rsd_done, 1)

            def reten_v_tok(p, j):
                act.wait_ge(rv_turned, 4 * p + j + 1)
                nc.scalar.activation(rv_tok[:, 0:4, 128 * j:128 * j + 128],
                                     bank[:, 2 * (j % 2), :].rearrange("p (t n) -> p t n", t=4), ACT.Copy)
                nc.scalar.activation(rv_tok[0:META, 4, 128 * j:128 * j + 128],
                                     bank[0:META, 2 * (j % 2) + 1, 0:128], ACT.Copy).then_inc(rv_tok_done, 1)

            def reten(p, first):
                half = sr.panel // 2 + 6 * p
                if not first:
                    act.wait_ge(rws_done, p)
                else:
                    act.wait_ge(stat_done, 3)
                act.dma_start(rdec[:, :], decay_tab[bass.ds(p, 1), 0:128, :].rearrange("a p n -> (a p) n")
                              ).then_inc(rdec_loaded, 16)
                act.dma_start(rdec_m[:, :],
                              decay_tab[bass.ds(p, 1), 128:128 + META, :].rearrange("a p n -> (a p) n")
                              ).then_inc(rdec_loaded, 16)
                if first:
                    row_std(2, EVERY)
                split_hi(half + 1, 0)
                split_hi(half + 1, 1)
                if not first:
                    reten_rsd(p - 1)
                split_hi(half + 2, 0)
                if not first:
                    reten_y(p - 1)
                split_hi(half + 2, 1)
                for j in range(4):
                    if j >= 2:
                        reten_v_tok(p, j - 2)
                    split_hi(half + 3 + j // 2, j % 2)
                for j in range(4):
                    if j < 2:
                        reten_v_tok(p, j + 2)
                    split_hi(half + 5 + j // 2, j % 2)
                    act.wait_ge(drained[j % 2], sr.drain[j % 2] + 6 * p + 5 + j // 2)
                    nc.scalar.activation(rgate[:, j, :], rgate[:, j, :], ACT.Silu).then_inc(rgate_done, 1)

            reten(0, True)
            with act.Fori(1, RT_HEADS) as p:
                reten(p, False)
            half = Start("out1").panel // 2
            split_hi(half + 1, 0)
            reten_rsd(RT_HEADS - 1)
            split_hi(half + 1, 1)
            reten_y(RT_HEADS - 1)
            splits("out1", 2 * KT, 1)
            row_std(3, X)
            up("up1", X)
            half = Start("down1").panel // 2
            with act.Fori(0, 3 * KT // 2 - 1) as i:
                for s in range(2):
                    split_hi(half + i + 1, s)
            row_std(4, X)

        @block.vector
        def _(dve):
            def split_x(res, m, r, cs):
                g = gains[:, bass.ds(KT * r + m, 1)]
                nc.vector.tensor_scalar(dyn(x_hi, m)[:, cs], dyn(h, m)[:, cs], g, None,
                                        ALU.mult).then_inc(x_hi_done, 1)
                dve.wait_ge(x_hi_done, res + 1)
                nc.vector.scalar_tensor_tensor(
                    out=dyn(x_lo, m)[:, cs], in0=dyn(h, m)[:, cs], scalar=g,
                    in1=dyn(x_hi, m)[:, cs].bitcast(f32), op0=ALU.mult, op1=ALU.subtract).then_inc(x_split, 1)

            def add_square(res, m, cs):
                nc.vector.tensor_tensor(square[:, cs], dyn(h, m)[:, cs], dyn(h, m)[:, cs],
                                        ALU.mult).then_inc(squared, 1)
                dve.wait_ge(squared, res + 1)
                nc.vector.tensor_tensor(sumsq[:, cs], sumsq[:, cs], square[:, cs], ALU.add).then_inc(summed, 1)

            def residual(res, drains, n_last, m, s, r, cs):
                full = cs.start == 0
                dve.wait_ge(panel_done, n_last + 1)
                hv = row_view(dyn(h, m), full)
                nc.vector.tensor_tensor(hv, hv, slot_view(s, full), ALU.add).then_inc(drained[s], 1)
                dve.wait_ge(drained[s], drains)
                if r < 4:
                    split_x(res, m, r, cs)
                dve.wait_ge(summed, res)
                add_square(res, m, cs)

            def row_rstd(r, cs):
                dve.wait_ge(std_done, r + 1)
                nc.vector.reciprocal(rstd[:, cs], rstd[:, cs]).then_inc(rstd_done, 1)
                if r < 4:
                    nc.vector.memset(sumsq[:, :], 0.0).then_inc(cleared, 1)
                dve.wait_ge(rstd_done, r + 1)

            def scaled(out, s, full, event):
                nc.vector.tensor_tensor(row_view(out, full), slot_view(s, full), row_view(rstd[:, :], full),
                                        ALU.mult).then_inc(event, 1)

            gains = par[:, 0:5 * KT]
            EVERY, X = slice(0, NT), slice(META, NT)
            dve.wait_ge(consts_set, 5)
            dve.wait_ge(par_loaded, 16)
            dve.wait_ge(w_hi_done, 1)
            nc.vector.tensor_tensor(w_lo[0][:, :, :], raw[0][:, :, :], w_hi[0][:, :, :].bitcast(f32),
                                    ALU.subtract).then_inc(w_lo_done, 1)
            for k in range(KT):
                dve.wait_ge(x_hi_done, k + 1)
                nc.vector.scalar_tensor_tensor(
                    out=x_lo[:, k, :], in0=h[:, k, :], scalar=gain[0][:, k:k + 1],
                    in1=x_hi[:, k, :].bitcast(f32), op0=ALU.mult, op1=ALU.subtract).then_inc(x_split, 1)
            for k in range(KT):
                dve.wait_ge(squared, k + 1)
                if k > 0:
                    dve.wait_ge(summed, k)
                nc.vector.tensor_tensor(sumsq[:, :], sumsq[:, :], src[:, k % 2, :], ALU.add).then_inc(summed, 1)

            tiles = [(0, META)] + [(META + 128 * t, 128) for t in range(XT)]

            def gate_chain():
                g = [0]

                def link(ins):
                    g[0] += 1
                    ins.then_inc(gate_dve, 1)
                    dve.wait_ge(gate_dve, g[0])

                dve.wait_ge(gate_act, 4)
                link(nc.vector.tensor_scalar(li_row, tanh_rows[0:ML_HEADS, :], GATE_CAP, None, ALU.mult))
                for a, w in tiles:
                    link(nc.vector.tensor_tensor_scan(lf_row[:, a:a + w], ones[0:ML_HEADS, 0:w],
                                                      sp_row[:, a:a + w], 0.0, ALU.mult, ALU.subtract))
                link(nc.vector.tensor_tensor(e_row, li_row, lf_row, ALU.subtract))
                for t in range(4):
                    a, w = tiles[t]
                    link(nc.vector.tensor_scalar(e_row[:, a:a + w], e_row[:, a:a + w],
                                                 lf_row[:, a + w - 1:a + w], None, ALU.add))
                link(nc.vector.tensor_copy(c_row[0][:, 0:META], e_row[:, 0:META]))
                for t in range(3):
                    a, w = tiles[t + 1]
                    link(nc.vector.tensor_scalar(c_row[t + 1][:, 0:a], c_row[t][:, 0:a],
                                                 lf_row[:, a + w - 1:a + w], None, ALU.add))
                    link(nc.vector.tensor_copy(c_row[t + 1][:, a:a + w], e_row[:, a:a + w]))
                assert g[0] == GATE_STEPS

            scale = (D_MODEL // ML_HEADS // 2) ** -0.5 / 4

            def gate_cols():
                dve.wait_ge(cols_done, 1)
                dve.wait_ge(consts_set, 9)
                pc = bank[:, 3, 0:160].rearrange("p (c h) -> p c h", h=ML_HEADS)
                nc.vector.tensor_scalar(cols[0:META, 0:4, :], pc[0:META, 0:4, :], scale, None, ALU.mult)
                nc.vector.tensor_copy(cols[0:META, 4:6, :], pc[0:META, 4:6, :])
                nc.vector.tensor_scalar(cols[:, 6:12, :], pc[:, 6:12, :], scale, None, ALU.mult)
                nc.vector.tensor_copy(cols[:, 12:20, :], pc[:, 12:20, :]).then_inc(cols_out, 1)
                dve.wait_ge(cols_out, 1)
                nc.vector.memset(ws[0:META, :, JMM + META:WSW], 0.0).then_inc(cols_out, 1)

            st = Start("mlstm")

            def mlstm_ratio(p, heads=(0, 1), last_pair=False):
                for e in heads:
                    c = 2 * p + e
                    dve.wait_ge(mix_done, c + 1)
                    o = slot[e][:, :, 0:480] if last_pair else bank[:, 2 * e:2 * e + 2, 0:480]
                    o = o.rearrange("p a (b n) -> p a b n", b=3)
                    den = nst[:, e, 0, :].rearrange("p (a b) -> p a b", a=2)
                    nc.vector.tensor_scalar(den, o[:, :, :, 128], -1.0, 1.0, ALU.mult, ALU.max
                                            ).then_inc(den_done, 1)
                    dve.wait_ge(den_done, 2 * c + 1)
                    nc.vector.tensor_tensor(den, o[:, :, :, 128], den, ALU.max).then_inc(den_done, 1)
                    dve.wait_ge(den_done, 2 * c + 2)
                    nc.vector.reciprocal(nst[:, e, 1, :], nst[:, e, 0, :]).then_inc(rden_done, 1)
                    dve.wait_ge(rden_done, c + 1)
                    for a in range(2):
                        last = nc.vector.tensor_tensor(
                            hs[:, e, 3 * a:3 * a + 3, :], o[:, a, :, 0:128],
                            nst[:, e, 1, 3 * a:3 * a + 3].unsqueeze(2).to_broadcast([128, 3, 128]), ALU.mult)
                    last.then_inc(num_done, 1)
                    dve.wait_ge(num_done, c + 1)
                    nc.vector.tensor_tensor(hsq, hs[:, e, :, :], hs[:, e, :, :], ALU.mult).then_inc(hsq_done, 1)
                    dve.wait_ge(hsq_done, c + 1)
                    nc.vector.reduce_sum(nst[:, e, 2, :], hsq, AX.X).then_inc(ss_done, 1)

            def mlstm_norm(p, heads=(0, 1)):
                for e in heads:
                    c = 2 * p + e
                    dve.wait_ge(rms_done, c + 1)
                    nc.vector.reciprocal(nst[:, e, 4, :], nst[:, e, 3, :]).then_inc(rrms_done, 1)
                    dve.wait_ge(rrms_done, c + 1)
                    nc.vector.tensor_tensor(hs[:, e, :, :], hs[:, e, :, :],
                                            nst[:, e, 4, :].unsqueeze(2).to_broadcast([128, 6, 128]),
                                            ALU.mult).then_inc(hs_done, 1)

            def conv(p, c, raw_rows, dst):
                dve.wait_ge(drained[c], st.drain[c] + 3 * p + 2)
                nc.vector.tensor_scalar(dst[:, :], raw_rows[:, 3:3 + NT], pair_p[:, 4 * c + 3:4 * c + 4], None,
                                        ALU.mult).then_inc(conv_step, 1)
                for tap in range(3):
                    dve.wait_ge(conv_step, 8 * p + 4 * c + tap + 1)
                    nc.vector.scalar_tensor_tensor(
                        out=dst[:, :], in0=raw_rows[:, tap:tap + NT], scalar=pair_p[:, 4 * c + tap:4 * c + tap + 1],
                        in1=dst[:, :], op0=ALU.mult, op1=ALU.add).then_inc(conv_step, 1)

            def mlstm_y(p, last_pair=False):
                nc.vector.tensor_copy(pair_g[:, :], pair_all[:, bass.ds(p, 1), 8:10].rearrange("p a b -> p (a b)")
                                      ).then_inc(gain_set, 1)
                dve.wait_ge(o_tanh, 2 * p + 2)
                nc.vector.tensor_scalar(o_sig[:, :, :], o_sig[:, :, :], 1.0, 0.5, ALU.add, ALU.mult
                                        ).then_inc(o_done, 1)
                dve.wait_ge(gain_set, p + 1)
                dve.wait_ge(o_done, p + 1)
                for e in range(2):
                    dve.wait_ge(y_turned, 2 * p + e + 1)
                    nc.vector.scalar_tensor_tensor(
                        out=src[:, e, 0:META], in0=bank[:, 2 * e + 1, 0:META], scalar=pair_g[:, e:e + 1],
                        in1=o_sig[:, e, 0:META], op0=ALU.mult, op1=ALU.mult)
                    nc.vector.scalar_tensor_tensor(
                        out=src[:, e, META:NT], in0=bank[:, 2 * e, :], scalar=pair_g[:, e:e + 1],
                        in1=o_sig[:, e, META:NT], op0=ALU.mult, op1=ALU.mult).then_inc(piece_ready, 1)
                    if last_pair:
                        piece_low(st.piece + 2 * p + e, y_lo[:, 2 * p + e, :], y_hi[:, 2 * p + e, :], e, EVERY)

            def piece_low(c, dst, hi, b, cs):
                dve.wait_ge(piece_lo, c)
                dve.wait_ge(piece_hi, c + 1)
                nc.vector.tensor_tensor(dst[:, cs], src[:, b, cs], hi[:, cs].bitcast(f32),
                                        ALU.subtract).then_inc(piece_lo, 1)

            def weigh(p, e, banks=BANKS):
                dve.wait_ge(scores_done, 2 * p + e + 1)
                dve.wait_ge(dec_done, p + 1)
                at = score_blocks(banks)
                for jt in range(XT):
                    w0 = WS_AT[jt]
                    nc.vector.scalar_tensor_tensor(out=ws[:, e, w0:w0 + 128], in0=at[jt][:, 0:128], scalar=scale,
                                                   in1=dec[:, e, jt, :], op0=ALU.mult, op1=ALU.mult)
                    for t in range(jt + 1, XT):
                        o = 128 * (t - jt)
                        idx = 6 + t * (t - 1) // 2 + jt
                        nc.vector.scalar_tensor_tensor(
                            out=ws[:, e, w0 + o:w0 + o + 128], in0=at[jt][:, o:o + 128],
                            scalar=cols_p[:, idx, e:e + 1], in1=a_row[:, e, 128 * t:128 * t + 128],
                            op0=ALU.mult, op1=ALU.mult)
                for t in range(XT):
                    nc.vector.scalar_tensor_tensor(
                        out=ws[0:META, e, JM + 128 * t:JM + 128 * t + 128],
                        in0=banks[3][0:META, 128 * t:128 * t + 128], scalar=cols_p[0:META, t, e:e + 1],
                        in1=a_row[0:META, e, 128 * t:128 * t + 128], op0=ALU.mult, op1=ALU.mult)
                nc.vector.scalar_tensor_tensor(
                    out=ws[0:META, e, JMM:JMM + META], in0=banks[2][0:META, 256:256 + META], scalar=scale,
                    in1=dec_m[:, e, :], op0=ALU.mult, op1=ALU.mult).then_inc(ws_done, 1)

            def pair_decays(p, first):
                if not first:
                    dve.wait_ge(ws_done, 2 * p)
                    dve.wait_ge(conv_step, 8 * p)
                nc.vector.tensor_copy(pair_p[:, :], pair_all[:, bass.ds(p, 1), 0:8].rearrange("p a b -> p (a b)")
                                      ).then_inc(pair_set, 1)
                nc.vector.tensor_copy(cols_p[:, :, :], cols[:, :, bass.ds(2 * p, 2)]).then_inc(pair_set, 1)
                dve.wait_ge(l_loaded, 16 * (p + 1))
                dve.wait_ge(pair_set, 2 * p + 2)
                for e in range(2):
                    for t in range(XT):
                        a = META + 128 * t
                        nc.vector.tensor_scalar(dec[:, e, t, :], l_row[:, e, a:a + 128], cols_p[:, 12 + t, e:e + 1],
                                                None, ALU.subtract)
                    last = nc.vector.tensor_scalar(dec_m[:, e, :], l_row[0:META, e, 0:META],
                                                   cols_p[0:META, 4, e:e + 1], None, ALU.subtract)
                last.then_inc(sub_done, 1)
                dve.wait_ge(sub_done, p + 1)
                for d in (dec[:, :, :, :].rearrange("p e t n -> p (e t n)"),
                          dec_m[:, :, :].rearrange("p e n -> p (e n)")):
                    last = nc.vector.scalar_tensor_tensor(out=d, in0=d, scalar=-1.0, in1=d, op0=ALU.mult,
                                                          op1=ALU.max)
                last.then_inc(diff_done, 1)

            def mask_decays(p):
                dve.wait_ge(dec_exp, p + 1)
                nc.vector.memset(dec[64:128, :, :, 0:64], 0.0).then_inc(dec_done, 1)

            def silu(p, c, rows):
                dve.wait_ge(conv_tanh, 2 * p + c + 1)
                nc.vector.scalar_tensor_tensor(out=rows[:, :], in0=half_tanh[:, :], scalar=1.0, in1=rows[:, :],
                                               op0=ALU.add, op1=ALU.mult).then_inc(silu_done, 1)

            def mlstm(p, first):
                n = st.panel + 6 * p

                def evacuate(j, out):
                    dve.wait_ge(panel_done, n + j + 1)
                    scaled(out, j % 2, True, drained[j % 2])

                if first:
                    row_rstd(0, EVERY)
                evacuate(0, v_T[:, 0, :])
                if not first:
                    weigh(p - 1, 0)
                else:
                    dve.wait_ge(gates_done, 1)
                    nc.vector.tensor_tensor(row_view(tanh_rows, True), bank[0:40, 2:4, 0:HALF],
                                            row_view(rstd[0:40, :], True), ALU.mult).then_inc(gates_scaled, 1)
                evacuate(1, v_T[:, 1, :])
                if not first:
                    weigh(p - 1, 1)
                evacuate(2, q_raw[:, 3:3 + NT])
                if first:
                    gate_chain()
                    dve.wait_ge(tab_loaded, 32)
                    nc.vector.tensor_copy(pair_p[:, :], pair_all[:, 0, 0:8]).then_inc(pair_one, 1)
                    dve.wait_ge(pair_one, 1)
                else:
                    pair_decays(p, False)
                conv(p, 0, q_raw, qs)
                if not first:
                    mlstm_ratio(p - 1)
                evacuate(3, k_raw[:, 3:3 + NT])
                silu(p, 0, qs)
                if not first:
                    mlstm_norm(p - 1)
                conv(p, 1, k_raw, ks)
                if not first:
                    mlstm_y(p - 1)
                silu(p, 1, ks)
                if not first:
                    mask_decays(p)
                    dve.wait_ge(piece_ready, st.piece + 2 * p)
                evacuate(4, o_sig[:, 0, :])
                if first:
                    gate_cols()
                    pair_decays(0, True)
                    mask_decays(0)
                evacuate(5, o_sig[:, 1, :])

            mlstm(0, True)
            with dve.Fori(1, PAIRS) as p:
                mlstm(p, False)
            weigh(PAIRS - 1, 0, SLOTS)
            weigh(PAIRS - 1, 1)
            dve.wait_ge(piece_lo, st.piece + 2 * (PAIRS - 1))
            for e in range(2):
                mlstm_ratio(PAIRS - 1, (e,), True)
                mlstm_norm(PAIRS - 1, (e,))
            mlstm_y(PAIRS - 1, True)

            def out_proj(stage, r, cs, panels):
                st = Start(stage)
                dve.wait_ge(cleared, r)
                with dve.Fori(0, KT // 2) as i:
                    for c in range(2):
                        residual(st.res + 2 * i + c, st.drain[c] + i + 1,
                                 st.panel + 2 * panels * (i + 1) - 2 + c, 2 * i + c, c, r, cs)

            def up(stage, cs):
                st = Start(stage)
                full = cs.start == 0

                with dve.Fori(0, FT // 2) as i:
                    for c in range(2):
                        f = 2 * i + c
                        dve.wait_ge(piece_ready, st.piece + f - 1)
                        dve.wait_ge(panel_done, st.panel + 2 * f + 1)
                        scaled(silu_g[:, c, :], 0, full, drained[0])
                        dve.wait_ge(piece_lo, st.piece + f - 1)
                        dve.wait_ge(panel_done, st.panel + 2 * f + 2)
                        scaled(src[:, c, :], 1, full, drained[1])
                        dve.wait_ge(drained[1], st.drain[1] + f + 1)
                        dve.wait_ge(up_silu, UPS[stage] + f + 1)
                        nc.vector.tensor_tensor(src[:, c, cs], src[:, c, cs], silu_g[:, c, cs],
                                                ALU.mult).then_inc(piece_ready, 1)

            UPS = {"up0": 0, "up1": FT}
            out_proj("out0", 1, EVERY, 1)
            row_rstd(1, EVERY)
            up("up0", EVERY)
            out_proj("down0", 2, EVERY, 3)

            sr = Start("reten")

            def rope_first(p, c, dst, full):
                n = sr.panel + 12 * p + 2 * c
                cs = EVERY if full else X
                dve.wait_ge(panel_done, n + 1)
                nc.vector.tensor_tensor(row_view(dst[:, 0, :], full), slot_view(0, full),
                                        row_view(cos_sin[:, 0, :], full), ALU.mult).then_inc(rope_step, 1)
                nc.vector.tensor_tensor(row_view(dst[:, 1, :], full), slot_view(0, full),
                                        row_view(cos_sin[:, 1, :], full), ALU.mult).then_inc(drained[0], 1)

            def rope_second(p, c, dst, full):
                n = sr.panel + 12 * p + 2 * c + 1
                cs = EVERY if full else X
                done = 8 * p + 4 * c
                dve.wait_ge(rope_step, done + 1)
                dve.wait_ge(panel_done, n + 1)
                nc.vector.tensor_tensor(row_view(rtmp[:, :], full), slot_view(1, full),
                                        row_view(cos_sin[:, 1, :], full), ALU.mult).then_inc(rope_step, 1)
                dve.wait_ge(rope_step, done + 2)
                nc.vector.tensor_tensor(dst[:, 0, cs], dst[:, 0, cs], rtmp[:, cs],
                                        ALU.subtract).then_inc(rope_step, 1)
                dve.wait_ge(rope_step, done + 3)
                nc.vector.tensor_tensor(row_view(rtmp[:, :], full), slot_view(1, full),
                                        row_view(cos_sin[:, 0, :], full), ALU.mult).then_inc(drained[1], 1)
                dve.wait_ge(drained[1], sr.drain[1] + 6 * p + c + 1)
                dve.wait_ge(drained[0], sr.drain[0] + 6 * p + c + 1)
                nc.vector.tensor_tensor(dst[:, 1, cs], dst[:, 1, cs], rtmp[:, cs],
                                        ALU.add).then_inc(rope_step, 1)

            def reten_norm(p):
                for t in range(XT):
                    c = 4 * p + t
                    dve.wait_ge(rmix_done, c + 1)
                    nc.vector.bn_stats(bn6[:, t, :], bank[:, t, :]).then_inc(bn_done, 1)
                dve.wait_ge(bn_done, 4 * p + 4)
                nc.vector.memset(rsd[:, :], 0.0)
                for t in range(XT):
                    nc.vector.bn_aggr(mv[:, t, :], bn6[:, t, :]).then_inc(mv_done, 1)
                dve.wait_ge(rsd_done, p + 1)
                nc.vector.reciprocal(rsd[:, :], rsd[:, :]).then_inc(rrsd_done, 1)
                dve.wait_ge(rrsd_done, p + 1)
                for t in range(XT):
                    nc.vector.tensor_scalar(rhs_n[:, t, :], bank[:, t, :], mv[:, t, 0:1], rsd[:, t:t + 1],
                                            ALU.subtract, ALU.mult).then_inc(rhs_done, 1)

            def reten_y(p, last_head=False):
                nc.vector.tensor_copy(stat[:, 4:8], ret_gain[:, bass.ds(4 * p, 4)]).then_inc(gain_set, 1)
                dve.wait_ge(gain_set, PAIRS + p + 1)
                dve.wait_ge(rgate_done, 4 * p + 4)
                for e in range(4):
                    dve.wait_ge(ry_turned, 4 * p + e + 1)
                    dve.wait_ge(piece_lo, sr.piece + 4 * p + e - 1)
                    nc.vector.scalar_tensor_tensor(
                        out=src[:, e % 2, X], in0=bank[:, e, :], scalar=stat[:, 4 + e:5 + e],
                        in1=rgate[:, e, :], op0=ALU.mult, op1=ALU.mult).then_inc(piece_ready, 1)
                    if last_head and e % 2 == 1:
                        for c in (e - 1, e):
                            piece_low(sr.piece + 4 * p + c, y_lo[:, 4 * p + c, :], y_hi[:, 4 * p + c, :], c % 2, X)

            def reten(p, first):
                rope_first(p, 0, rq, False)
                if first:
                    row_rstd(2, EVERY)
                else:
                    reten_norm(p - 1)
                rope_second(p, 0, rq, False)
                if first:
                    dve.wait_ge(rope_step, 4)
                    for c in range(2):
                        nc.vector.tensor_tensor(rq[:, c, X], rq[:, c, X], rstd[:, X], ALU.mult)
                    for c in range(2):
                        nc.vector.tensor_tensor(cos_sin[:, c, :], cos_sin[:, c, :], rstd[:, :],
                                                ALU.mult).then_inc(rope_scaled, 1)
                    dve.wait_ge(rope_scaled, 2)
                rope_first(p, 1, rk, True)
                if not first:
                    reten_y(p - 1)
                rope_second(p, 1, rk, True)
                n = sr.panel + 12 * p
                for j in range(4):
                    if j >= 2:
                        dve.wait_ge(rv_turned, 4 * p + j - 1)
                    dve.wait_ge(panel_done, n + 5 + j)
                    scaled(rv_T[:, j % 2, :], j % 2, True, drained[j % 2])
                for j in range(2):
                    dve.wait_ge(panel_done, n + 9 + j)
                    nc.vector.tensor_tensor(rgate[:, j, :], slot_view(j % 2, False), rstd[:, X],
                                            ALU.mult).then_inc(drained[j % 2], 1)
                dve.wait_ge(rscores_done, p + 1)
                dve.wait_ge(rdec_loaded, 32 * (p + 1))
                at = [bank[:, 0, :], bank[:, 1, 0:384], bank[:, 2, 0:256], bank[:, 1, 384:512]]
                for jt in range(XT):
                    w = SEQ - 128 * jt
                    nc.vector.tensor_tensor(rws[:, WS_AT[jt]:WS_AT[jt] + w], at[jt], rdec[:, 0:w], ALU.mult)
                nc.vector.tensor_tensor(rws[0:META, JM:JM + SEQ], bank[0:META, 3, :], rdec_m[:, :],
                                        ALU.mult).then_inc(rws_done, 1)
                for j in range(2, 4):
                    dve.wait_ge(panel_done, n + 9 + j)
                    nc.vector.tensor_tensor(rgate[:, j, :], slot_view(j % 2, False), rstd[:, X],
                                            ALU.mult).then_inc(drained[j % 2], 1)

            dve.wait_ge(rope_loaded, 16)
            reten(0, True)
            with dve.Fori(1, RT_HEADS) as p:
                reten(p, False)
            reten_norm(RT_HEADS - 1)
            reten_y(RT_HEADS - 1, True)
            out_proj("out1", 3, X, 2)
            row_rstd(3, X)
            up("up1", X)
            out_proj("down1", 4, X, 3)
            for k in range(POOL_OUT):
                nc.vector.tensor_scalar(h[:, k, X], h[:, k, X], gains[:, 4 * KT + k:4 * KT + k + 1], None,
                                        ALU.mult).then_inc(gained, 1)
            row_rstd(4, X)
            for k in range(POOL_OUT, KT):
                nc.vector.scalar_tensor_tensor(
                    out=h[:, k, X], in0=h[:, k, X], scalar=gains[:, 4 * KT + k:4 * KT + k + 1], in1=rstd[:, X],
                    op0=ALU.mult, op1=ALU.mult).then_inc(out_ready, 1)

        @block.tensor
        def _(pe):
            def panel(n, s, out_slot, xs, cols_, first=True, last=True, k0=0, end=True,
                      within=None):
                pe.wait_ge(w_lo_done, n + 1)
                for k, (hi, lo) in enumerate(xs, k0):
                    if within and k == KT - 3:
                        within()
                    if callable(hi):
                        hi, lo = hi()
                    for w, x in ((w_hi, hi), (w_hi, lo), (w_lo, hi)):
                        for b, a, width in cols_:
                            mm = nc.tensor.matmul(
                                slot[out_slot][:, b, 0:width], w[s][:, k, :], x[:, a:a + width],
                                start=first and k == 0 and w is w_hi and x is hi,
                                stop=last and end and k == k0 + len(xs) - 1 and w is w_lo)
                if end:
                    mm.then_inc(panel_done, 1)

            def x_tiles(r):
                def tile(k):
                    def get():
                        pe.wait_ge(x_split, KT * r + k + 1)
                        return x_hi[:, k, :], x_lo[:, k, :]
                    return get, None
                return [tile(k) for k in range(KT)]

            X_READY = [(x_hi[:, k, :], x_lo[:, k, :]) for k in range(KT)]

            def norm(r, cs):
                pe.wait_ge(summed, KT * (r + 1))
                if cs.start == 0:
                    for b in range(2):
                        mm = nc.tensor.matmul(bank[:, b, 0:HALF], ones[:, :], sumsq[:, b * HALF:(b + 1) * HALF],
                                              start=True, stop=True)
                else:
                    mm = nc.tensor.matmul(bank[:, 0, :], ones[:, :], sumsq[:, META:NT], start=True, stop=True)
                mm.then_inc(stat_done, 1)

            EVERY, X = slice(0, NT), slice(META, NT)
            pe.wait_ge(consts_set, 5)

            def gates():
                pe.wait_ge(wg_lo_done, 2)
                for k in range(KT):
                    if k == KT - 2:
                        norm(0, EVERY)
                    for w, x in ((wg_hi, x_hi), (wg_hi, x_lo), (wg_lo, x_hi)):
                        for b in range(2):
                            mm = nc.tensor.matmul(bank[0:40, 2 + b, 0:HALF], w[:, k, :],
                                                  x[:, k, b * HALF:(b + 1) * HALF],
                                                  start=k == 0 and w is wg_hi and x is x_hi,
                                                  stop=k == KT - 1 and w is wg_lo)
                mm.then_inc(gates_done, 1)

            st = Start("mlstm")

            def mlstm_mix(p, heads=(0, 1), banks=BANKS):
                pe.wait_ge(ws_done, 2 * p + heads[-1] + 1)
                for e in heads:
                    blocks = [-1, 0, 1, 2, 3, -1]
                    for b, t in enumerate(blocks):
                        o = banks[2 * e + b // 3][:, 160 * (b % 3):160 * (b % 3) + 129]
                        m0 = JMM if t < 0 else JM + 128 * t
                        mm = nc.tensor.matmul(o, ws[0:META, e, m0:m0 + 128], v_tok[0:META, 4, e, 0:129],
                                              start=True, stop=t < 0)
                        for jt in range(t + 1):
                            w0 = WS_AT[jt] + 128 * (t - jt)
                            mm = nc.tensor.matmul(o, ws[:, e, w0:w0 + 128], v_tok[:, jt, e, 0:129],
                                                  start=False, stop=jt == t)
                    mm.then_inc(mix_done, 1)

            def mlstm_turn(p, e):
                pe.wait_ge(hs_done, 2 * p + e + 1)
                for t in range(XT):
                    nc.tensor.transpose(bank[:, 2 * e, 128 * t:128 * t + 128], hs[:, e, 1 + t, :], ident[:, :])
                nc.tensor.transpose(bank[:, 2 * e + 1, 0:META], hs[0:META, e, 0, :],
                                    ident[0:META, 0:META]).then_inc(y_turned, 1)

            def gate_columns():
                pe.wait_ge(gate_act, 8)
                pe.wait_ge(tab_loaded, 32)
                tiles = [(0, META)] + [(META + 128 * t, 128) for t in range(XT)]
                jobs = [(c_row[t], 0) for t in range(4)] + [(lf_row, 0), (li_row, 0)]
                jobs += [(c_row[t], 1 + j) for t in range(4) for j in range(t)]
                jobs += [(lf_row, 1 + t) for t in range(4)] + [(li_row, 1 + t) for t in range(4)]
                for c, (row, tile) in enumerate(jobs):
                    a, w = tiles[tile]
                    mm = nc.tensor.transpose(bank[0:w, 3, 8 * c:8 * c + 8], row[:, a:a + w],
                                             ident[0:ML_HEADS, 0:ML_HEADS])
                mm.then_inc(cols_done, 1)

            def mlstm_scores(p, e, banks=BANKS):
                r = slice(64 * e, 64 * e + 64)
                at = score_blocks(banks)
                for jt in range(XT):
                    a = META + 128 * jt
                    nc.tensor.matmul(at[jt], ks[r, a:a + 128], qs[r, a:NT], start=True, stop=True)
                nc.tensor.matmul(banks[3][0:META, :], ks[r, 0:META], qs[r, META:NT], start=True, stop=True)
                nc.tensor.matmul(banks[2][0:META, 256:256 + META], ks[r, 0:META], qs[r, 0:META],
                                 start=True, stop=True).then_inc(scores_done, 1)

            def mlstm(p, first):
                n, d0, d1 = st.panel + 6 * p, st.drain[0] + 3 * p, st.drain[1] + 3 * p
                if not first:
                    pe.wait_ge(drained[0], d0)
                panel(n, 0, 0, x_tiles(0) if first else X_READY, ALL_COLS)
                if first:
                    gates()
                else:
                    pe.wait_ge(silu_done, 2 * p)
                    pe.wait_ge(v_tok_done, p)
                    mlstm_scores(p - 1, 0)
                    pe.wait_ge(drained[1], d1)
                panel(n + 1, 1, 1, X_READY, ALL_COLS)
                if not first:
                    pe.wait_ge(ws_done, 2 * p - 1)
                    mlstm_scores(p - 1, 1)
                pe.wait_ge(drained[0], d0 + 1)
                panel(n + 2, 0, 0, X_READY, ALL_COLS)
                if not first:
                    mlstm_mix(p - 1)
                pe.wait_ge(drained[1], d1 + 1)
                panel(n + 3, 1, 1, X_READY, ALL_COLS)
                pe.wait_ge(drained[0], d0 + 2)
                panel(n + 4, 0, 0, X_READY, ALL_COLS)
                if first:
                    gate_columns()
                else:
                    mlstm_turn(p - 1, 0)
                    mlstm_turn(p - 1, 1)
                pe.wait_ge(drained[1], d1 + 2)
                panel(n + 5, 1, 1, X_READY, ALL_COLS)
                if first:
                    pe.wait_ge(cols_out, 2)
                else:
                    pe.wait_ge(piece_ready, st.piece + 2 * p)
                for e in range(2):
                    for t in range(XT):
                        a = META + 128 * t
                        nc.tensor.transpose(bank[:, e, 128 * t:128 * t + 128], v_T[:, e, a:a + 128], ident[:, :])
                    mm = nc.tensor.transpose(bank[0:META, 2, 128 * e:128 * e + 128], v_T[:, e, 0:META], ident[:, :])
                mm.then_inc(v_turned, 1)

            mlstm(0, True)
            with pe.Fori(1, PAIRS) as p:
                mlstm(p, False)

            def y_tile(k):
                return (y_hi[:, k, :], y_lo[:, k, :]) if k < YT else (z_hi[:, k - YT, :], z_lo[:, k - YT, :])

            def two_outputs(st, groups, i, cols_, pieces=None):
                for g, (k0, kn) in enumerate(groups):
                    for c in range(2):
                        if g == 0:
                            pe.wait_ge(drained[c], st.drain[c] + i)
                        if pieces is not None:
                            pe.wait_ge(piece_lo, pieces + k0 + kn)
                        panel(st.panel + 2 * len(groups) * i + 2 * g + c, c, c,
                              [y_tile(k) for k in range(k0, k0 + kn)], cols_, first=g == 0,
                              last=g == len(groups) - 1)

            def out_proj(stage, groups, cols_, pieces):
                st = Start(stage)
                two_outputs(st, groups, 0, cols_, pieces)
                with pe.Fori(1, KT // 2) as i:
                    two_outputs(st, groups, i, cols_)

            def up(stage, r, cols_, cs):
                st = Start(stage)

                def two_tiles(i, first):
                    for c in range(2):
                        f = 2 * i + c
                        pe.wait_ge(drained[0], st.drain[0] + f)
                        if first and c == 0:
                            panel(st.panel, 0, 0, x_tiles(r), cols_, within=lambda: norm(r, cs))
                        else:
                            panel(st.panel + 2 * f, 0, 0, X_READY, cols_)
                        pe.wait_ge(drained[1], st.drain[1] + f)
                        panel(st.panel + 2 * f + 1, 1, 1, X_READY, cols_)

                two_tiles(0, True)
                with pe.Fori(1, FT // 2) as i:
                    two_tiles(i, False)

            so = Start("out0")
            early = ML_HEADS - 2
            last = PAIRS - 1

            def out0_tiles(c, a, z):
                pe.wait_ge(piece_lo, st.piece + max(z, early))
                panel(so.panel + c, c, c, [y_tile(k) for k in range(a, z)], ALL_COLS, k0=a, last=z == KT, end=z == KT)

            pe.wait_ge(silu_done, 2 * PAIRS)
            for c in range(2):
                pe.wait_ge(drained[c], so.drain[c])
            mlstm_scores(last, 0, SLOTS)
            pe.wait_ge(v_tok_done, PAIRS)
            mlstm_scores(last, 1)
            mlstm_mix(last, (0,), SLOTS)
            mlstm_mix(last, (1,), SLOTS)
            pe.wait_ge(num_done, 2 * PAIRS - 1)
            out0_tiles(0, 0, early)
            mlstm_turn(last, 0)
            pe.wait_ge(num_done, 2 * PAIRS)
            out0_tiles(1, 0, 3)
            mlstm_turn(last, 1)
            out0_tiles(1, 3, 5)
            out0_tiles(0, early, KT)
            out0_tiles(1, 5, KT)
            with pe.Fori(1, KT // 2) as i:
                two_outputs(so, ((0, 8),), i, ALL_COLS)
            up("up0", 1, ALL_COLS, EVERY)
            out_proj("down0", DOWN_SPLIT, ALL_COLS, Start("up0").piece)

            sr = Start("reten")

            def reten_mix(p):
                pe.wait_ge(rws_done, p + 1)
                for t in range(XT):
                    nc.tensor.matmul(bank[:, t, :], rws[0:META, JM + 128 * t:JM + 128 * t + 128],
                                     rv_tok[0:META, 4, :], start=True, stop=False)
                    for jt in range(t + 1):
                        w0 = WS_AT[jt] + 128 * (t - jt)
                        mm = nc.tensor.matmul(bank[:, t, :], rws[:, w0:w0 + 128], rv_tok[:, jt, :],
                                              start=False, stop=jt == t)
                    mm.then_inc(rmix_done, 1)

            def reten_turn(p):
                pe.wait_ge(rhs_done, 4 * p + 4)
                for e in range(4):
                    for t in range(XT):
                        mm = nc.tensor.transpose(bank[:, e, 128 * t:128 * t + 128],
                                                 rhs_n[:, t, 128 * e:128 * e + 128], ident[:, :])
                    mm.then_inc(ry_turned, 1)

            def reten_v_turn(p, j):
                b = 2 * (j % 2)
                pe.wait_ge(drained[j % 2], sr.drain[j % 2] + 6 * p + 3 + j // 2)
                if j >= 2:
                    pe.wait_ge(rv_tok_done, 4 * p + j - 1)
                for t in range(XT):
                    a = META + 128 * t
                    nc.tensor.transpose(bank[:, b, 128 * t:128 * t + 128], rv_T[:, j % 2, a:a + 128], ident[:, :])
                nc.tensor.transpose(bank[0:META, b + 1, 0:128], rv_T[:, j % 2, 0:META],
                                    ident[:, :]).then_inc(rv_turned, 1)

            def reten(p, first):
                n = sr.panel + 12 * p
                d = [sr.drain[0] + 6 * p, sr.drain[1] + 6 * p]
                for j in range(12):
                    pe.wait_ge(drained[j % 2], d[j % 2] + j // 2)
                    xs = x_tiles(2) if first and j == 0 else X_READY
                    panel(n + j, j % 2, j % 2, xs, ALL_COLS if 2 <= j < 8 else X_COLS,
                          within=(lambda: norm(2, EVERY)) if first and j == 0 else None)
                    if not first and j == 0:
                        reten_mix(p - 1)
                    if not first and j == 2:
                        reten_turn(p - 1)
                    if j == 5:
                        if not first:
                            pe.wait_ge(piece_ready, sr.piece + 4 * p)
                        reten_v_turn(p, 0)
                    if 6 <= j <= 8:
                        reten_v_turn(p, j - 5)
                    if j == 9:
                        pe.wait_ge(rope_step, 8 * p + 8)
                        pe.wait_ge(rv_tok_done, 4 * p + 4)
                        at = [bank[:, 0, :], bank[:, 1, 0:384], bank[:, 2, 0:256], bank[:, 1, 384:512]]
                        for jt in range(XT):
                            a = META + 128 * jt
                            for kk in range(2):
                                nc.tensor.matmul(at[jt], rk[:, kk, a:a + 128], rq[:, kk, a:NT],
                                                 start=kk == 0, stop=kk == 1)
                        for kk in range(2):
                            mm = nc.tensor.matmul(bank[0:META, 3, :], rk[:, kk, 0:META], rq[:, kk, META:NT],
                                                  start=kk == 0, stop=kk == 1)
                        mm.then_inc(rscores_done, 1)

            reten(0, True)
            with pe.Fori(1, RT_HEADS) as p:
                reten(p, False)

            so1 = Start("out1")
            def out1_tiles(c, a, z):
                pe.wait_ge(piece_lo, sr.piece + max(z, 4 * (RT_HEADS - 1)))
                panel(so1.panel + 2 * (a // KT) + c, c, c, [y_tile(k) for k in range(a, z)], X_COLS,
                      first=a < KT, last=z == 2 * KT, k0=a % KT, end=z % KT == 0)

            pe.wait_ge(drained[0], so1.drain[0])
            out1_tiles(0, 0, KT)
            reten_mix(RT_HEADS - 1)
            pe.wait_ge(drained[1], so1.drain[1])
            out1_tiles(1, 0, KT)
            reten_turn(RT_HEADS - 1)
            out1_tiles(0, KT, 12)
            out1_tiles(1, KT, 10)
            out1_tiles(0, 12, 16)
            out1_tiles(1, 10, 16)
            with pe.Fori(1, KT // 2) as i:
                two_outputs(so1, ((0, 8), (8, 8)), i, X_COLS)
            up("up1", 3, X_COLS, X)
            out_proj("down1", DOWN_SPLIT, X_COLS, Start("up1").piece)
            norm(4, X)


def kernel(x, meta_tokens, norm_mix, norm_ffn, norm_final, ml_w_in, ml_b_gate, ml_w_conv, ml_norm,
           ml_w_out, rt_w_in, rt_norm, rt_w_out, ffn_w_gu, ffn_w_down):
    import numpy as np
    import concourse.bacc as bacc
    from concourse.bass_utils import run_bass_kernel_spmd

    f = np.float32
    arr = [np.asarray(a) for a in (x, meta_tokens, norm_mix, norm_ffn, norm_final, ml_w_in, ml_b_gate,
                                   ml_w_conv, ml_norm, ml_w_out, rt_w_in, rt_norm, rt_w_out, ffn_w_gu, ffn_w_down)]
    (x, meta_tokens, norm_mix, norm_ffn, norm_final, ml_w_in, ml_b_gate, ml_w_conv, ml_norm, ml_w_out,
     rt_w_in, rt_norm, rt_w_out, ffn_w_gu, ffn_w_down) = arr

    def tiles(v):
        return v.reshape(-1, 128).T

    h_in = np.concatenate([meta_tokens, x[0]], 0).T.reshape(KT, 128, NT).transpose(1, 0, 2)
    small = np.zeros((128, 5 * KT + 17), f)
    for r, v in enumerate((norm_mix[0], norm_ffn[0], norm_mix[1], norm_ffn[1], norm_final)):
        small[:, KT * r:KT * (r + 1)] = tiles(v)
    small[:, 5 * KT:5 * KT + 16] = tiles(rt_norm[0])
    small[0:8, 5 * KT + 16] = ml_b_gate[0, 0:8]
    small[32:40, 5 * KT + 16] = ml_b_gate[0, 8:16]
    pair = np.zeros((128, PAIRS, 10), f)
    for p in range(PAIRS):
        pair[:, p, 0:4] = ml_w_conv[0, :, 128 * p:128 * p + 128].T
        pair[:, p, 4:8] = ml_w_conv[0, :, 512 + 128 * p:512 + 128 * p + 128].T
        pair[:, p, 8:10] = tiles(ml_norm[0])[:, 2 * p:2 * p + 2]

    stream = np.zeros((PANELS, 128, KT, 128), f)
    at = 0

    def put(w, c, k0=0, kn=KT):
        nonlocal at
        stream[at, :, 0:kn, :] = w[128 * k0:128 * (k0 + kn), 128 * c:128 * c + 128].reshape(kn, 128, 128
                                                                                         ).transpose(1, 0, 2)
        at += 1

    def ffn(layer):
        for c in range(FT):
            put(ffn_w_gu[layer], c)
            put(ffn_w_gu[layer], FT + c)
        for m in range(0, KT, 2):
            for k0, kn in DOWN_SPLIT:
                put(ffn_w_down[layer], m, k0, kn)
                put(ffn_w_down[layer], m + 1, k0, kn)

    for p in range(PAIRS):
        for c in (8 + 2 * p, 9 + 2 * p, p, 4 + p, 16 + 2 * p, 17 + 2 * p):
            put(ml_w_in[0], c)
    for m in range(KT):
        put(ml_w_out[0], m)
    ffn(0)
    for p in range(RT_HEADS):
        for c in [2 * p, 2 * p + 1, 8 + 2 * p, 9 + 2 * p] + [16 + 4 * p + e for e in range(4)] + \
                [32 + 4 * p + e for e in range(4)]:
            put(rt_w_in[0], c)
    for m in range(0, KT, 2):
        for k0 in (0, 8):
            put(rt_w_out[0], m, k0, 8)
            put(rt_w_out[0], m + 1, k0, 8)
    ffn(1)

    half = D_MODEL // RT_HEADS // 2
    inv = (f(10000.0) ** (-np.arange(half, dtype=f) / f(half))).astype(f)
    ang = np.arange(NT, dtype=f)[None, :] * inv[:, None]
    rope = np.stack([np.cos(ang), np.sin(ang)], 1).astype(f)
    decay = np.zeros((RT_HEADS, 128 + META, SEQ), f)
    j, i = np.arange(128)[:, None], np.arange(SEQ)[None, :]
    for hd in range(RT_HEADS):
        lg = np.log1p(-np.exp2(-5.0 - hd))
        decay[hd, 0:128] = np.exp(lg * abs(i - j)) * (j // CHUNK <= i // CHUNK) / 16.0
        decay[hd, 128:] = np.exp(lg * (i + META - np.arange(META)[:, None])) / 16.0

    feeds = {
        "h_in": h_in, "stream": stream.reshape(PANELS, 128, KT * 128),
        "w_gates": ml_w_in[0][:, 3072:3088].reshape(KT, 128, 16).transpose(1, 0, 2), "small": small,
        "pair_par": pair, "rope_tab": rope, "decay_tab": decay, "ident_in": np.eye(128, dtype=f),
    }
    feeds = {n: np.ascontiguousarray(a) for n, a in feeds.items()}
    nc = bacc.Bacc("TRN2", target_bir_lowering=False, num_devices=1)
    dt = mybir.dt.float32
    args = [nc.dram_tensor(n, a.shape, dt, kind="ExternalInput").ap() for n, a in feeds.items()]
    out = nc.dram_tensor("out", (128, KT, SEQ), dt, kind="ExternalOutput").ap()
    build_hybrid(nc, *args, out)
    r = run_bass_kernel_spmd(nc, [feeds], core_ids=[0])
    return r.results[0]["out"].transpose(2, 1, 0).reshape(1, SEQ, D_MODEL)
```

```python
import concourse.bass as bass
from concourse import mybir
from contextlib import ExitStack

D_MODEL, SEQ, META, CHUNK = 1024, 512, 16, 64
NT = META + SEQ
HALF = NT // 2
KT = D_MODEL // 128
XT = SEQ // 128
D_FF = ((8 * D_MODEL + 3 * 256 - 1) // (3 * 256)) * 256
FT = D_FF // 128
ML_HEADS, RT_HEADS = 8, 4
PAIRS = ML_HEADS // 2
YT = 16
GATE_CAP, EPS = 15.0, 1e-6
DOWN_SPLIT = ((0, 8), (8, 7), (15, 7))
JT0, JT1, JT2, JT3, JM, JMM, WSW = 0, 512, 896, 1152, 1280, 1792, 1920
WS_AT = (JT0, JT1, JT2, JT3)

V_COLS = 130
POOL_OUT = 3
GATE_STEPS = 1 + 5 + 1 + 4 + 1 + 6

STAGES = (
    ("mlstm", 6 * PAIRS, 3 * PAIRS, 3 * PAIRS, ML_HEADS, 0), ("out0", KT, KT // 2, KT // 2, 0, KT),
    ("up0", 2 * FT, FT, FT, FT, 0), ("down0", 3 * KT, KT // 2, KT // 2, 0, KT),
    ("reten", 12 * RT_HEADS, 6 * RT_HEADS, 6 * RT_HEADS, 16, 0),
    ("out1", 2 * KT, KT // 2, KT // 2, 0, KT),
    ("up1", 2 * FT, FT, FT, FT, 0), ("down1", 3 * KT, KT // 2, KT // 2, 0, KT),
    ("end", 0, 0, 0, 0, 0),
)
PANELS = sum(s[1] for s in STAGES)


class Start:

    def __init__(self, stage):
        before = STAGES[:[s[0] for s in STAGES].index(stage)]
        self.panel, drain0, drain1, self.piece, res = (sum(s[c] for s in before) for c in range(1, 6))
        self.drain = (drain0, drain1)
        self.res = KT + res


def build_hybrid(nc, h_in, stream, w_gates, small, pair_par, rope_tab, decay_tab, ident_in, out):
    f32, f32r = mybir.dt.float32, mybir.dt.float32r
    ALU, ACT, AX = mybir.AluOpType, mybir.ActivationFunctionType, mybir.AxisListType

    with ExitStack() as keep:
        def sb(name, shape, dt=f32, ctx=keep):
            return ctx.enter_context(nc.sbuf_tensor(name, shape, dt))

        def sem(name):
            return keep.enter_context(nc.semaphore(name))

        h = sb("h", [128, KT, NT])
        x_hi, x_lo = sb("x_hi", [128, KT, NT], f32r), sb("x_lo", [128, KT, NT], f32r)
        y_hi, y_lo = sb("y_hi", [128, YT, NT], f32r), sb("y_lo", [128, YT, NT], f32r)
        raw = [sb(f"raw{s}", [128, KT, 128]) for s in range(2)]
        w_hi = [sb(f"w_hi{s}", [128, KT, 128], f32r) for s in range(2)]
        w_lo = [sb(f"w_lo{s}", [128, KT, 128], f32r) for s in range(2)]
        src = sb("src", [128, 2, NT])
        square = sb("square", [128, NT])
        sumsq = sb("sumsq", [128, NT])
        rstd = sb("rstd", [128, NT])
        ident = sb("ident", [128, 128])
        ones = sb("ones", [128, 128])
        par = sb("par", [128, small.shape[1]])
        gain = [par[:, KT * r:KT * (r + 1)] for r in range(5)]
        ret_gain = par[:, 5 * KT:5 * KT + 16]
        b_gate = par[:, 5 * KT + 16:5 * KT + 17]
        eps = sb("eps", [128, 1])
        half_tanh = square
        stat = sb("stat", [128, 64])

        with ExitStack() as c:
            v_T = sb("v_T", [128, 2, NT], f32, c)
            v_tok = sb("v_tok", [128, 5, 2, V_COLS], f32, c)
            q_raw = sb("q_raw", [128, 3 + NT], f32, c)
            k_raw = sb("k_raw", [128, 3 + NT], f32, c)
            qs, ks = sb("qs", [128, NT], f32, c), sb("ks", [128, NT], f32, c)
            o_sig = sb("o_sig", [128, 2, NT], f32, c)
            ws = sb("ws", [128, 2, WSW], f32, c)
            hs = sb("hs", [128, 2, 6, 128], f32, c)
            l_row = sb("l_row", [128, 2, NT], f32, c)
            a_row = sb("a_row", [128, 2, SEQ], f32, c)
            dec = sb("dec", [128, 2, XT, 128], f32, c)
            dec_m = sb("dec_m", [META, 2, META], f32, c)
            cols = sb("cols", [128, 20, ML_HEADS], f32, c)
            cols_p = sb("cols_p", [128, 20, 2], f32, c)
            pair_all = sb("pair_all", [128, PAIRS, 10], f32, c)
            pair_p = sb("pair_p", [128, 8], f32, c)
            pair_g = sb("pair_g", [128, 2], f32, c)
            nst = sb("nst", [128, 2, 5, 6], f32, c)
            b_cap = sb("b_cap", [40, 1], f32, c)
        free_hi = y_hi[:, ML_HEADS:YT, :]
        k_stack = [free_hi[:, e, :] for e in range(2)]
        q_stack = [free_hi[:, 2 + e, :] for e in range(2)]
        q_low, q_natural = free_hi[:, 4, :], free_hi[:, 5, :]
        free_lo = y_lo[:, ML_HEADS:YT, :].rearrange("p a b -> p (a b)")
        META_HI, META_MID, META_END = slice(0, META), slice(32, 32 + META), slice(64, 64 + META)
        META_K = slice(0, 64 + META)
        w_meta = free_lo[:, 0:2 * (WSW - JM)].rearrange("p (e n) -> p e n", e=2)
        v_meta = free_lo[:, 2 * (WSW - JM):2 * (WSW - JM) + 2 * V_COLS].rearrange("p (e n) -> p e n", e=2)
        wg_raw = a_row[:, 0, 0:16 * KT].rearrange("p (k n) -> p k n", k=KT)
        wg_hi = y_hi[:, 0, 0:40 * KT].rearrange("p (k n) -> p k n", k=KT)
        wg_lo = y_hi[:, 1, 0:40 * KT].rearrange("p (k n) -> p k n", k=KT)
        gate_rows = ws[:, :, :].rearrange("p a b -> p (a b)")
        tanh_rows = l_row[0:40, 0, :]
        sp_row = l_row[0:ML_HEADS, 1, :]
        li_row = gate_rows[0:ML_HEADS, 0:NT]
        lf_row = gate_rows[0:ML_HEADS, NT:2 * NT]
        e_row = gate_rows[0:ML_HEADS, 2 * NT:3 * NT]
        c_row = [gate_rows[0:ML_HEADS, (3 + t) * NT:(4 + t) * NT] for t in range(4)]
        hsq = src[:, :, :].rearrange("p a b -> p (a b)")[:, 0:768].rearrange("p (a b) -> p a b", a=6)

        with ExitStack() as c:
            z_hi = sb("z_hi", [128, FT - YT, NT], f32r, c)
            z_lo = sb("z_lo", [128, FT - YT, NT], f32r, c)
            silu_g = sb("silu_g", [128, 2, NT], f32, c)

        with ExitStack() as c:
            rv_T = sb("rv_T", [128, 2, NT], f32, c)
            rv_hi = sb("rv_hi", [128, 5, 512], f32r, c)
            rq = sb("rq", [128, 2, NT], f32, c)
            rk = sb("rk", [128, 2, NT], f32, c)
            rtmp = sb("rtmp", [128, NT], f32, c)
            rdec = sb("rdec", [128, SEQ], f32, c)
            cos_sin = sb("cos_sin", [128, 2, NT], f32, c)
            rdec_m = sb("rdec_m", [META, SEQ], f32, c)
            rws_low = sb("rws_low", [128, JM], f32r, c)
            rws_m = sb("rws_m", [META, SEQ], f32, c)
            rgate = sb("rgate", [128, 4, SEQ], f32, c)
            rhs_n = sb("rhs_n", [128, XT, 512], f32, c)
            bn6 = sb("bn6", [128, XT, 6], f32, c)
            mv = sb("mv", [128, XT, 2], f32, c)
            rsd = sb("rsd", [128, XT], f32, c)

        tail_hi = y_hi[:, YT - 4:YT, :].rearrange("p a b -> p (a b)")
        tail_lo = y_lo[:, YT - 4:YT, :].rearrange("p a b -> p (a b)")
        R_AT = (0, 512, 1024, 896)
        rws_at = (rv_T[:, 0, 0:512], rv_T[:, 1, 0:384], rtmp[:, 0:256], rv_T[:, 1, 384:512])
        rws_parts = ((rv_T[:, :, 0:512], 0, 1024), (rtmp[:, 0:256], 1024, JM))

        def part_of(t, a, z):
            return t[:, 0:1024].rearrange("p (a b) -> p a b", a=2) if a == 0 else t[:, a:z]

        rws_hi, rws_meta = tail_hi[:, 0:JM], tail_hi[:, JM:JM + SEQ]
        rv_lo = tail_lo[:, 0:4 * 512].rearrange("p (t n) -> p t n", t=4)
        rv_meta = rv_hi[:, 4, :]

        slot = [keep.enter_context(nc.psum_tensor(f"slot{s}", [128, 2, 512], f32)) for s in range(2)]
        bank = keep.enter_context(nc.psum_tensor("bank", [128, 4, 512], f32))
        l_dram = nc.dram_tensor("l_dram", (ML_HEADS, NT), f32, kind="Internal").ap()

        h_loaded = [sem(f"h_loaded{c}") for c in range(4)]
        par_loaded, tab_loaded, gate_w_loaded = sem("par_loaded"), sem("tab_loaded"), sem("gate_w_loaded")
        consts_set = sem("consts_set")
        half_loaded, half_hi, half_lo = sem("half_loaded"), sem("half_hi"), sem("half_lo")
        raw_loaded = [sem("raw_loaded0"), sem("raw_loaded1")]
        w_hi_done, w_lo_done, panel_done = sem("w_hi_done"), sem("w_lo_done"), sem("panel_done")
        drained = [sem("slot0_drained"), sem("slot1_drained")]
        piece_ready, piece_hi, piece_lo = sem("piece_ready"), sem("piece_hi"), sem("piece_lo")
        x_hi_done, x_split = sem("x_hi_done"), sem("x_split")
        squared, summed, cleared = sem("squared"), sem("summed"), sem("sumsq_cleared")
        stat_done, std_done, rstd_done = sem("stat_done"), sem("std_done"), sem("rstd_done")
        out_ready, out_ready_pool, out_stored = sem("out_ready"), sem("out_ready_pool"), sem("out_stored")
        gained = sem("gained")
        wg_hi_done, wg_lo_done, gates_done = sem("wg_hi_done"), sem("wg_lo_done"), sem("gates_done")
        gate_act, gate_dve = sem("gate_act"), sem("gate_dve")
        l_stored, l_loaded, cols_done, cols_out = sem("l_stored"), sem("l_loaded"), sem("cols_done"), sem("cols_out")
        conv_step, conv_tanh, silu_done = sem("conv_step"), sem("conv_tanh"), sem("silu_done")
        o_tanh, o_done = sem("o_tanh"), sem("o_done")
        v_turned, v_tok_done = sem("v_turned"), sem("v_tok_done")
        pair_set, diff_done, a_row_done, dec_exp, dec_done = (
            sem("pair_set"), sem("diff_done"), sem("a_row_done"), sem("dec_exp"), sem("dec_done"))
        gain_set, pair_one = sem("gain_set"), sem("pair_one")
        gates_scaled = sem("gates_scaled")
        q_high_done, q_stacked, q_split, k_high_done, k_split = (
            sem(n) for n in ("q_high_done", "q_stacked", "q_split", "k_high_done", "k_split"))
        v_meta_high, v_meta_done, ws_meta_done, w_meta_high, w_meta_done = (
            sem(n) for n in ("v_meta_high", "v_meta_done", "ws_meta_done", "w_meta_high", "w_meta_done"))
        meta_cleared = sem("meta_cleared")
        scores_done, ws_done, mix_done = sem("scores_done"), sem("ws_done"), sem("mix_done")
        den_done, rden_done, num_done, hsq_done, ss_done, rms_done, rrms_done, hs_done = (
            sem(n) for n in ("den_done", "rden_done", "num_done", "hsq_done", "ss_done", "rms_done",
                             "rrms_done", "hs_done"))
        y_turned, up_silu = sem("y_turned"), sem("up_silu")
        rope_loaded, rope_scaled, rope_step, rv_turned = (
            sem("rope_loaded"), sem("rope_scaled"), sem("rope_step"), sem("rv_turned"))
        rv_high_done, rv_split, rws_high_done, rws_split, rws_meta_split = (
            sem(n) for n in ("rv_high_done", "rv_split", "rws_high_done", "rws_split", "rws_meta_split"))
        rdec_loaded, rgate_done = sem("rdec_loaded"), sem("rgate_done")
        rscores_done, rws_done, rmix_done = sem("rscores_done"), sem("rws_done"), sem("rmix_done")
        bn_done, mv_done, rsd_done, rrsd_done, rhs_done, ry_turned = (
            sem(n) for n in ("bn_done", "mv_done", "rsd_done", "rrsd_done", "rhs_done", "ry_turned"))

        ALL_COLS = ((0, 0, HALF), (1, HALF, HALF))
        X_COLS = ((0, META, SEQ),)

        BANKS = [bank[:, b, :] for b in range(4)]
        SLOTS = [slot[b // 2][:, b % 2, :] for b in range(4)]

        def score_blocks(banks):
            return [banks[0], banks[1][:, 0:384], banks[2][:, 0:256], banks[1][:, 384:512]]

        def slot_view(s, all_tokens):
            return slot[s][:, :, 0:HALF] if all_tokens else slot[s][:, 0, :]

        def row_view(ap, all_tokens):
            return ap.rearrange("p (a b) -> p a b", a=2) if all_tokens else ap[:, META:NT]

        def dyn(t, m):
            return t[:, bass.ds(m, 1), :].rearrange("p a b -> p (a b)")

        block = keep.enter_context(nc.Block())

        @block.sync
        def _(sp):
            sp.dma_start(par[:, :], small).then_inc(par_loaded, 16)
            def load(i, s):
                sp.dma_start(raw[s][:, :, :].rearrange("p k n -> p (k n)"),
                             stream[bass.ds(2 * i + s, 1), :, :].rearrange("a p n -> (a p) n")
                             ).then_inc(raw_loaded[s], 16)

            for a in (0, KT // 2):
                sp.dma_start(raw[0][:, a:a + KT // 2, :].rearrange("p k n -> p (k n)"),
                             stream[0, :, 128 * a:128 * (a + KT // 2)]
                             ).then_inc(half_loaded if a == 0 else raw_loaded[0], 16)
                if a == 0:
                    sp.dma_start(h[:, 0:2, :], h_in[:, 0:2, :]).then_inc(h_loaded[0], 16)
            for c in range(1, 4):
                sp.dma_start(h[:, 2 * c:2 * c + 2, :], h_in[:, 2 * c:2 * c + 2, :]).then_inc(h_loaded[c], 16)
            sp.dma_start(wg_raw[:, :, :], w_gates).then_inc(gate_w_loaded, 16)
            load(0, 1)
            sp.dma_start(ident[:, :], ident_in).then_inc(tab_loaded, 16)
            sp.dma_start(pair_all[:, :, :], pair_par).then_inc(tab_loaded, 16)
            with sp.Fori(1, PANELS // 2) as i:
                for s in range(2):
                    sp.wait_ge(w_lo_done, 2 * i + s - 1)
                    load(i, s)
            for event, n, k in ((out_ready, 1, 3), (out_ready_pool, 1, 0), (out_ready, 2, 4), (out_ready, 3, 5),
                                (out_ready_pool, 2, 1), (out_ready, 4, 6), (out_ready, 5, 7), (out_ready_pool, 3, 2)):
                sp.wait_ge(event, n)
                sp.dma_start(out[:, k, :], h[:, k, META:NT]).then_inc(out_stored, 16)
            sp.wait_ge(out_stored, 16 * KT)

        @block.gpsimd
        def _(pool):
            nc.gpsimd.memset(ones[:, :], 1.0).then_inc(consts_set, 1)
            nc.gpsimd.memset(eps[:, :], EPS).then_inc(consts_set, 1)
            nc.gpsimd.memset(wg_hi[:, :, :].bitcast(f32), 0.0).then_inc(consts_set, 1)
            nc.gpsimd.memset(wg_lo[:, :, :].bitcast(f32), 0.0).then_inc(consts_set, 1)
            nc.gpsimd.memset(sumsq[:, :], 0.0).then_inc(consts_set, 1)

            def split_lo(n, s):
                pool.wait_ge(w_hi_done, n + 1)
                nc.gpsimd.tensor_tensor(w_lo[s][:, :, :], raw[s][:, :, :], w_hi[s][:, :, :].bitcast(f32),
                                        ALU.subtract).then_inc(w_lo_done, 1)

            def piece_low(c, dst, hi, b, cs):
                pool.wait_ge(piece_hi, c + 1)
                nc.gpsimd.tensor_tensor(dst[:, cs], src[:, b, cs], hi[:, cs].bitcast(f32),
                                        ALU.subtract).then_inc(piece_lo, 1)

            EVERY, X = slice(0, NT), slice(META, NT)
            pool.wait_ge(wg_hi_done, 2)
            nc.gpsimd.tensor_tensor(wg_lo[:, :, 0:8], wg_raw[:, :, 0:8], wg_hi[:, :, 0:8].bitcast(f32),
                                    ALU.subtract).then_inc(wg_lo_done, 1)
            nc.gpsimd.tensor_tensor(wg_lo[:, :, 32:40], wg_raw[:, :, 8:16], wg_hi[:, :, 32:40].bitcast(f32),
                                    ALU.subtract).then_inc(wg_lo_done, 1)
            pool.wait_ge(w_lo_done, 1)
            split_lo(1, 1)
            nc.gpsimd.memset(q_raw[:, 0:3], 0.0).then_inc(consts_set, 1)
            nc.gpsimd.memset(k_raw[:, 0:3], 0.0).then_inc(consts_set, 1)
            nc.gpsimd.memset(v_tok[:, :, :, 128:130], 1.0).then_inc(consts_set, 1)
            nc.gpsimd.memset(cols[:, :, :], 0.0).then_inc(consts_set, 1)

            st = Start("mlstm")

            def mlstm_y(p):
                for e in range(2):
                    piece_low(st.piece + 2 * p + e, dyn(y_lo, 2 * p + e), dyn(y_hi, 2 * p + e), e, EVERY)

            def mlstm(p, first):
                n = st.panel + 6 * p
                for j in range(6):
                    split_lo(n + j + 2, j % 2)
                    if j == 3:
                        pool.wait_ge(q_high_done, p + 1)
                        nc.gpsimd.tensor_tensor(q_low, qs[:, :], q_natural.bitcast(f32), ALU.subtract
                                                ).then_inc(q_split, 1)
                    if j == 4 and not first:
                        mlstm_y(p - 1)

            mlstm(0, True)
            with pool.Fori(1, PAIRS) as p:
                mlstm(p, False)

            def splits(stage, count, done=0):
                st = Start(stage)
                with pool.Fori(done, count // 2) as i:
                    for s in range(2):
                        split_lo(st.panel + 2 * i + s + 2, s)

            def up(stage, cs):
                st = Start(stage)

                def two_tiles(i, base, hi, lo):
                    for c in range(2):
                        split_lo(st.panel + 4 * (i + base) + 2 * c + 2, 0)
                        split_lo(st.panel + 4 * (i + base) + 2 * c + 3, 1)
                        piece_low(st.piece + 2 * (i + base) + c, dyn(lo, 2 * i + c), dyn(hi, 2 * i + c), c, cs)

                with pool.Fori(0, YT // 2) as i:
                    two_tiles(i, 0, y_hi, y_lo)
                with pool.Fori(0, (FT - YT) // 2) as i:
                    two_tiles(i, YT // 2, z_hi, z_lo)

            splits("out0", KT)
            up("up0", EVERY)
            splits("down0", 3 * KT)

            str_ = Start("reten")

            def reten_y(p, parts):
                for e in parts:
                    piece_low(str_.piece + 4 * p + e, dyn(y_lo, 4 * p + e), dyn(y_hi, 4 * p + e), e % 2, X)

            def reten(p, first):
                n = str_.panel + 12 * p
                for j in range(12):
                    split_lo(n + j + 2, j % 2)
                    if j == 2 and not first:
                        reten_y(p - 1, (0, 1))
                    if j == 3 and not first:
                        reten_y(p - 1, (2, 3))
                    if j == 9:
                        pool.wait_ge(rws_high_done, p + 1)
                        for source, a, z in rws_parts:
                            last = nc.gpsimd.tensor_tensor(part_of(rws_low, a, z), source,
                                                           part_of(rws_hi, a, z).bitcast(f32), ALU.subtract)
                        last.then_inc(rws_split, 1)

            reten(0, True)
            with pool.Fori(1, RT_HEADS) as p:
                reten(p, False)
            splits("out1", 2 * KT)
            up("up1", X)
            st_last = Start("down1")
            with pool.Fori(0, 3 * KT // 2 - 1) as i:
                for s in range(2):
                    split_lo(st_last.panel + 2 * i + s + 2, s)
            pool.wait_ge(gained, POOL_OUT)
            pool.wait_ge(rstd_done, 5)
            for k in range(POOL_OUT):
                nc.gpsimd.tensor_tensor(h[:, k, X], h[:, k, X], rstd[:, X], ALU.mult).then_inc(out_ready_pool, 1)

        @block.scalar
        def _(act):
            def split_hi(half, s, first=False):
                act.wait_ge(raw_loaded[s], 16 * (half + 1))
                if not first:
                    act.wait_ge(panel_done, 2 * half + s - 1)
                nc.scalar.activation(w_hi[s][:, :, :], raw[s][:, :, :], ACT.Copy).then_inc(w_hi_done, 1)

            def piece_high(c, dst, b, cs):
                act.wait_ge(piece_ready, c + 1)
                nc.scalar.activation(dst[:, cs], src[:, b, cs], ACT.Copy).then_inc(piece_hi, 1)

            def row_std(r, cs):
                act.wait_ge(stat_done, r + 1)
                full = cs.start == 0
                ins = bank[:, 0:2, 0:HALF] if full else bank[:, 0, :]
                nc.scalar.activation(row_view(rstd[:, :], full), ins, ACT.Sqrt, bias=eps[:, 0:1],
                                     scale=1.0 / D_MODEL).then_inc(std_done, 1)

            EVERY, X = slice(0, NT), slice(META, NT)
            act.wait_ge(par_loaded, 16)
            nc.scalar.activation(b_cap[:, :], b_gate[0:40, :], ACT.Copy, scale=1.0 / GATE_CAP).then_inc(gate_act, 1)
            act.wait_ge(consts_set, 5)
            act.wait_ge(half_loaded, 16)
            nc.scalar.activation(w_hi[0][:, 0:KT // 2, :], raw[0][:, 0:KT // 2, :], ACT.Copy).then_inc(half_hi, 1)
            for k in range(KT):
                if k == 2:
                    act.wait_ge(raw_loaded[0], 16)
                    nc.scalar.activation(w_hi[0][:, KT // 2:KT, :], raw[0][:, KT // 2:KT, :], ACT.Copy
                                         ).then_inc(w_hi_done, 1)
                if k % 2 == 0:
                    act.wait_ge(h_loaded[k // 2], 16)
                nc.scalar.activation(x_hi[:, k, :], h[:, k, :], ACT.Copy, scale=gain[0][:, k:k + 1]
                                     ).then_inc(x_hi_done, 1)
            act.wait_ge(gate_w_loaded, 16)
            nc.scalar.activation(wg_hi[:, :, 0:8], wg_raw[:, :, 0:8], ACT.Copy).then_inc(wg_hi_done, 1)
            nc.scalar.activation(wg_hi[:, :, 32:40], wg_raw[:, :, 8:16], ACT.Copy).then_inc(wg_hi_done, 1)
            split_hi(0, 1, True)
            for k in range(KT):
                if k >= 2:
                    act.wait_ge(summed, k - 1)
                nc.scalar.activation(src[:, k % 2, :], h[:, k, :], ACT.Square).then_inc(squared, 1)

            def gates():
                act.wait_ge(gate_act, 1)
                act.wait_ge(gates_scaled, 1)
                nc.scalar.activation(tanh_rows, tanh_rows, ACT.Tanh, bias=b_cap[:, 0:1], scale=1.0 / GATE_CAP
                                     ).then_inc(gate_act, 1)
                act.wait_ge(gate_act, 2)
                nc.scalar.activation(sp_row, tanh_rows[32:40, :], ACT.Exp, scale=-GATE_CAP).then_inc(gate_act, 1)
                act.wait_ge(gate_act, 3)
                nc.scalar.activation(sp_row, sp_row, ACT.Ln, bias=1.0).then_inc(gate_act, 1)

            def gate_exps():
                act.wait_ge(gate_dve, GATE_STEPS)
                act.dma_start(l_dram, lf_row).then_inc(l_stored, 16)
                for t in range(XT):
                    w = META + 128 * t
                    nc.scalar.activation(c_row[t][:, 0:w], c_row[t][:, 0:w], ACT.Exp).then_inc(gate_act, 1)
                act.wait_ge(l_stored, 16)

            st = Start("mlstm")

            def mlstm_rms(p):
                for e in range(2):
                    act.wait_ge(ss_done, 2 * p + e + 1)
                    nc.scalar.activation(nst[:, e, 3, :], nst[:, e, 2, :], ACT.Sqrt, bias=eps[:, 0:1],
                                         scale=1.0 / 128).then_inc(rms_done, 1)

            def mlstm_y(p):
                for e in range(2):
                    piece_high(st.piece + 2 * p + e, dyn(y_hi, 2 * p + e), e, EVERY)

            def conv_half_tanh(p, c, rows):
                act.wait_ge(conv_step, 8 * p + 4 * c + 4)
                if c == 1:
                    act.wait_ge(silu_done, 2 * p + 1)
                nc.scalar.activation(half_tanh[:, :], rows[:, :], ACT.Tanh, scale=0.5).then_inc(conv_tanh, 1)

            def q_high(p):
                act.wait_ge(silu_done, 2 * p + 1)
                nc.scalar.activation(q_natural[:, :], qs[:, :], ACT.Copy).then_inc(q_high_done, 1)
                for e in range(2):
                    own, other = slice(64 * e, 64 * e + 64), slice(64 - 64 * e, 128 - 64 * e)
                    nc.scalar.activation(q_stack[e][own, :], qs[own, :], ACT.Copy)
                    last = nc.scalar.activation(q_stack[e][other, :], qs[own, :], ACT.Copy)
                last.then_inc(q_stacked, 1)

            def k_high(p):
                act.wait_ge(silu_done, 2 * p + 2)
                for e in range(2):
                    own = slice(64 * e, 64 * e + 64)
                    last = nc.scalar.activation(k_stack[e][own, :], ks[own, :], ACT.Copy)
                last.then_inc(k_high_done, 1)

            def meta_weights_high(p, e):
                act.wait_ge(ws_meta_done, 2 * p + e + 1)
                nc.scalar.activation(w_meta[META_HI, e, :], ws[0:META, e, JM:WSW], ACT.Copy)
                nc.scalar.activation(w_meta[META_MID, e, :], ws[0:META, e, JM:WSW], ACT.Copy
                                     ).then_inc(w_meta_high, 1)

            def load_l_rows(p):
                act.dma_start(l_row[:, :, :], l_dram[bass.ds(2 * p, 2), :].partition_broadcast(128)
                              ).then_inc(l_loaded, 16)

            def decay_exponents(p, first):
                act.wait_ge(l_loaded, 16 * (p + 1))
                if not first:
                    act.wait_ge(ws_done, 2 * p)
                nc.scalar.activation(a_row[:, :, :], l_row[:, :, META:NT], ACT.Exp).then_inc(a_row_done, 1)
                act.wait_ge(pair_set, 2 * p + 2)
                for e in range(2):
                    for t in range(XT):
                        a = META + 128 * t
                        nc.scalar.activation(dec[:, e, t, :], l_row[:, e, a:a + 128], ACT.Abs,
                                             bias=cols_p[:, 12 + t, e:e + 1])
                    last = nc.scalar.activation(dec_m[:, e, :], l_row[0:META, e, 0:META], ACT.Abs,
                                                bias=cols_p[0:META, 4, e:e + 1])
                last.then_inc(diff_done, 1)

            def decays(p):
                act.wait_ge(diff_done, p + 1)
                for e in range(2):
                    for t in range(XT):
                        nc.scalar.activation(dec[:, e, t, :], dec[:, e, t, :], ACT.Exp, scale=-1.0,
                                             bias=cols_p[:, 16 + t, e:e + 1])
                    last = nc.scalar.activation(dec_m[:, e, :], dec_m[:, e, :], ACT.Exp, scale=-1.0,
                                                bias=cols_p[0:META, 5, e:e + 1])
                last.then_inc(dec_exp, 1)

            def v_tokens(p):
                act.wait_ge(v_turned, p + 1)
                for e in range(2):
                    nc.scalar.activation(v_tok[:, 0:4, e, 0:128],
                                         bank[:, e, :].rearrange("p (t n) -> p t n", t=4), ACT.Copy)
                nc.scalar.activation(v_tok[0:META, 4, :, 0:128],
                                     bank[0:META, 2, 0:256].rearrange("p (e n) -> p e n", e=2),
                                     ACT.Copy).then_inc(v_tok_done, 1)
                act.wait_ge(v_tok_done, p + 1)
                act.wait_ge(meta_cleared, 2)
                nc.scalar.activation(v_meta[META_HI, :, :], v_tok[0:META, 4, :, :], ACT.Copy)
                nc.scalar.activation(v_meta[META_END, :, :], v_tok[0:META, 4, :, :], ACT.Copy
                                     ).then_inc(v_meta_high, 1)

            def mlstm(p, first):
                half = st.panel // 2 + 3 * p
                if not first:
                    act.wait_ge(diff_done, p)
                    act.wait_ge(a_row_done, p)
                    load_l_rows(p)
                split_hi(half + 1, 0)
                if first:
                    row_std(0, EVERY)
                else:
                    meta_weights_high(p - 1, 0)
                split_hi(half + 1, 1)
                if first:
                    gates()
                else:
                    meta_weights_high(p - 1, 1)
                split_hi(half + 2, 0)
                if first:
                    split_hi(half + 2, 1)
                    gate_exps()
                    load_l_rows(0)
                else:
                    decay_exponents(p, False)
                    decays(p)
                conv_half_tanh(p, 0, qs)
                if not first:
                    mlstm_rms(p - 1)
                    split_hi(half + 2, 1)
                q_high(p)
                conv_half_tanh(p, 1, ks)
                split_hi(half + 3, 0)
                k_high(p)
                if first:
                    decay_exponents(0, True)
                else:
                    mlstm_y(p - 1)
                split_hi(half + 3, 1)
                if first:
                    v_tokens(0)
                    decays(0)
                for e in range(2):
                    act.wait_ge(drained[e], st.drain[e] + 3 * p + 3)
                    nc.scalar.activation(o_sig[:, e, :], o_sig[:, e, :], ACT.Tanh, scale=0.5).then_inc(o_tanh, 1)
                if not first:
                    v_tokens(p)

            mlstm(0, True)
            with act.Fori(1, PAIRS) as p:
                mlstm(p, False)
            for e in range(2):
                meta_weights_high(PAIRS - 1, e)
            mlstm_rms(PAIRS - 1)
            mlstm_y(PAIRS - 1)

            def splits(stage, count, done=0):
                half = Start(stage).panel // 2
                with act.Fori(done, count // 2) as i:
                    for s in range(2):
                        split_hi(half + i + 1, s)

            def up(stage, cs):
                st = Start(stage)

                def two_tiles(i, base, hi):
                    for c in range(2):
                        f = 2 * (i + base) + c
                        split_hi(st.panel // 2 + f + 1, 0)
                        act.wait_ge(drained[0], st.drain[0] + f + 1)
                        nc.scalar.activation(silu_g[:, c, cs], silu_g[:, c, cs], ACT.Silu).then_inc(up_silu, 1)
                        split_hi(st.panel // 2 + f + 1, 1)
                        piece_high(st.piece + f, dyn(hi, 2 * i + c), c, cs)

                with act.Fori(0, YT // 2) as i:
                    two_tiles(i, 0, y_hi)
                with act.Fori(0, (FT - YT) // 2) as i:
                    two_tiles(i, YT // 2, z_hi)

            splits("out0", KT)
            row_std(1, EVERY)
            up("up0", EVERY)
            act.dma_start(cos_sin[:, :, :], rope_tab).then_inc(rope_loaded, 16)
            splits("down0", 3 * KT)

            sr = Start("reten")

            def reten_y(p, parts=range(4)):
                for e in parts:
                    piece_high(sr.piece + 4 * p + e, dyn(y_hi, 4 * p + e), e % 2, X)

            def reten_rsd(p):
                act.wait_ge(mv_done, 4 * p + 4)
                nc.scalar.activation(rsd[:, :], mv[:, :, 1], ACT.Sqrt, bias=eps[:, 0:1]).then_inc(rsd_done, 1)

            def reten_v_high(p, j):
                act.wait_ge(rv_turned, 4 * p + j + 1)
                if j == 0:
                    act.wait_ge(meta_cleared, 4)
                nc.scalar.activation(rv_hi[:, 0:4, 128 * j:128 * j + 128],
                                     bank[:, 2 * (j % 2), :].rearrange("p (t n) -> p t n", t=4), ACT.Copy)
                for rows in (META_HI, META_END):
                    last = nc.scalar.activation(rv_meta[rows, 128 * j:128 * j + 128],
                                                bank[0:META, 2 * (j % 2) + 1, 0:128], ACT.Copy)
                last.then_inc(rv_high_done, 1)

            def reten_weights_high(p):
                act.wait_ge(rws_done, p + 1)
                for rows in (META_HI, META_MID):
                    nc.scalar.activation(rws_meta[rows, :], rws_m[:, :], ACT.Copy)
                for source, a, z in rws_parts:
                    last = nc.scalar.activation(part_of(rws_hi, a, z), source, ACT.Copy)
                last.then_inc(rws_high_done, 1)

            def reten(p, first):
                half = sr.panel // 2 + 6 * p
                if not first:
                    act.wait_ge(rws_done, p)
                else:
                    act.wait_ge(stat_done, 3)
                act.dma_start(rdec[:, :], decay_tab[bass.ds(p, 1), 0:128, :].rearrange("a p n -> (a p) n")
                              ).then_inc(rdec_loaded, 16)
                act.dma_start(rdec_m[:, :],
                              decay_tab[bass.ds(p, 1), 128:128 + META, :].rearrange("a p n -> (a p) n")
                              ).then_inc(rdec_loaded, 16)
                if first:
                    row_std(2, EVERY)
                split_hi(half + 1, 0)
                if not first:
                    reten_rsd(p - 1)
                split_hi(half + 1, 1)
                split_hi(half + 2, 0)
                if not first:
                    reten_y(p - 1, (0, 1))
                split_hi(half + 2, 1)
                if not first:
                    reten_y(p - 1, (2, 3))
                for j in range(4):
                    if j >= 2:
                        reten_v_high(p, j - 2)
                    split_hi(half + 3 + j // 2, j % 2)
                for j in range(4):
                    if j < 2:
                        reten_v_high(p, j + 2)
                    split_hi(half + 5 + j // 2, j % 2)
                    act.wait_ge(drained[j % 2], sr.drain[j % 2] + 6 * p + 5 + j // 2)
                    nc.scalar.activation(rgate[:, j, :], rgate[:, j, :], ACT.Silu).then_inc(rgate_done, 1)
                    if j == 1:
                        reten_weights_high(p)

            reten(0, True)
            with act.Fori(1, RT_HEADS) as p:
                reten(p, False)
            half = Start("out1").panel // 2
            split_hi(half + 1, 0)
            reten_rsd(RT_HEADS - 1)
            split_hi(half + 1, 1)
            reten_y(RT_HEADS - 1)
            splits("out1", 2 * KT, 1)
            row_std(3, X)
            up("up1", X)
            half = Start("down1").panel // 2
            with act.Fori(0, 3 * KT // 2 - 1) as i:
                for s in range(2):
                    split_hi(half + i + 1, s)
            row_std(4, X)

        @block.vector
        def _(dve):
            def split_x(res, m, r, cs):
                g = gains[:, bass.ds(KT * r + m, 1)]
                nc.vector.tensor_scalar(dyn(x_hi, m)[:, cs], dyn(h, m)[:, cs], g, None,
                                        ALU.mult).then_inc(x_hi_done, 1)
                dve.wait_ge(x_hi_done, res + 1)
                nc.vector.scalar_tensor_tensor(
                    out=dyn(x_lo, m)[:, cs], in0=dyn(h, m)[:, cs], scalar=g,
                    in1=dyn(x_hi, m)[:, cs].bitcast(f32), op0=ALU.mult, op1=ALU.subtract).then_inc(x_split, 1)

            def add_square(res, m, cs, add=True):
                nc.vector.tensor_tensor(square[:, cs], dyn(h, m)[:, cs], dyn(h, m)[:, cs],
                                        ALU.mult).then_inc(squared, 1)
                if add:
                    dve.wait_ge(squared, res + 1)
                    nc.vector.tensor_tensor(sumsq[:, cs], sumsq[:, cs], square[:, cs], ALU.add).then_inc(summed, 1)

            def residual(res, drains, n_last, m, s, r, cs, add=True):
                full = cs.start == 0
                dve.wait_ge(panel_done, n_last + 1)
                hv = row_view(dyn(h, m), full)
                nc.vector.tensor_tensor(hv, hv, slot_view(s, full), ALU.add).then_inc(drained[s], 1)
                dve.wait_ge(drained[s], drains)
                if r < 4:
                    split_x(res, m, r, cs)
                dve.wait_ge(summed, res)
                add_square(res, m, cs, add)

            def row_rstd(r, cs):
                dve.wait_ge(std_done, r + 1)
                nc.vector.reciprocal(rstd[:, cs], rstd[:, cs]).then_inc(rstd_done, 1)
                if r < 4:
                    nc.vector.memset(sumsq[:, :], 0.0).then_inc(cleared, 1)
                dve.wait_ge(rstd_done, r + 1)

            def scaled(out, s, full, event):
                nc.vector.tensor_tensor(row_view(out, full), slot_view(s, full), row_view(rstd[:, :], full),
                                        ALU.mult).then_inc(event, 1)

            gains = par[:, 0:5 * KT]
            EVERY, X = slice(0, NT), slice(META, NT)
            dve.wait_ge(consts_set, 5)
            dve.wait_ge(par_loaded, 16)
            for t in (w_meta, v_meta):
                nc.vector.memset(t[META_K, :, :].bitcast(f32), 0.0).then_inc(meta_cleared, 1)
            for k in range(KT):
                if k in (0, 2):
                    dve.wait_ge(half_hi if k == 0 else w_hi_done, 1)
                    part = slice(0, KT // 2) if k == 0 else slice(KT // 2, KT)
                    nc.vector.tensor_tensor(w_lo[0][:, part, :], raw[0][:, part, :], w_hi[0][:, part, :].bitcast(f32),
                                            ALU.subtract).then_inc(half_lo if k == 0 else w_lo_done, 1)
                dve.wait_ge(x_hi_done, k + 1)
                nc.vector.scalar_tensor_tensor(
                    out=x_lo[:, k, :], in0=h[:, k, :], scalar=gain[0][:, k:k + 1],
                    in1=x_hi[:, k, :].bitcast(f32), op0=ALU.mult, op1=ALU.subtract).then_inc(x_split, 1)
            for k in range(KT):
                dve.wait_ge(squared, k + 1)
                if k > 0:
                    dve.wait_ge(summed, k)
                nc.vector.tensor_tensor(sumsq[:, :], sumsq[:, :], src[:, k % 2, :], ALU.add).then_inc(summed, 1)

            tiles = [(0, META)] + [(META + 128 * t, 128) for t in range(XT)]

            def gate_chain():
                g = [0]

                def link(ins):
                    g[0] += 1
                    ins.then_inc(gate_dve, 1)
                    dve.wait_ge(gate_dve, g[0])

                dve.wait_ge(gate_act, 4)
                link(nc.vector.tensor_scalar(li_row, tanh_rows[0:ML_HEADS, :], GATE_CAP, None, ALU.mult))
                for a, w in tiles:
                    link(nc.vector.tensor_tensor_scan(lf_row[:, a:a + w], ones[0:ML_HEADS, 0:w],
                                                      sp_row[:, a:a + w], 0.0, ALU.mult, ALU.subtract))
                link(nc.vector.tensor_tensor(e_row, li_row, lf_row, ALU.subtract))
                for t in range(4):
                    a, w = tiles[t]
                    link(nc.vector.tensor_scalar(e_row[:, a:a + w], e_row[:, a:a + w],
                                                 lf_row[:, a + w - 1:a + w], None, ALU.add))
                link(nc.vector.tensor_copy(c_row[0][:, 0:META], e_row[:, 0:META]))
                for t in range(3):
                    a, w = tiles[t + 1]
                    link(nc.vector.tensor_scalar(c_row[t + 1][:, 0:a], c_row[t][:, 0:a],
                                                 lf_row[:, a + w - 1:a + w], None, ALU.add))
                    link(nc.vector.tensor_copy(c_row[t + 1][:, a:a + w], e_row[:, a:a + w]))
                assert g[0] == GATE_STEPS

            scale = (D_MODEL // ML_HEADS // 2) ** -0.5 / 4

            def gate_cols():
                dve.wait_ge(cols_done, 1)
                dve.wait_ge(consts_set, 9)
                pc = bank[:, 3, 0:160].rearrange("p (c h) -> p c h", h=ML_HEADS)
                nc.vector.tensor_scalar(cols[0:META, 0:4, :], pc[0:META, 0:4, :], scale, None, ALU.mult)
                nc.vector.tensor_scalar(cols[0:META, 4, :], pc[0:META, 4, :], -1.0, None, ALU.mult)
                nc.vector.tensor_copy(cols[0:META, 5, :], pc[0:META, 5, :])
                nc.vector.tensor_scalar(cols[:, 6:12, :], pc[:, 6:12, :], scale, None, ALU.mult)
                nc.vector.tensor_scalar(cols[:, 12:16, :], pc[:, 12:16, :], -1.0, None, ALU.mult)
                nc.vector.tensor_copy(cols[:, 16:20, :], pc[:, 16:20, :]).then_inc(cols_out, 1)
                dve.wait_ge(cols_out, 1)
                nc.vector.memset(ws[0:META, :, JMM + META:WSW], 0.0).then_inc(cols_out, 1)

            st = Start("mlstm")

            def mlstm_ratio(p, heads=(0, 1), last_pair=False):
                for e in heads:
                    c = 2 * p + e
                    dve.wait_ge(mix_done, c + 1)
                    o = slot[e][:, :, 0:480] if last_pair else bank[:, 2 * e:2 * e + 2, 0:480]
                    o = o.rearrange("p a (b n) -> p a b n", b=3)
                    den = nst[:, e, 0, :].rearrange("p (a b) -> p a b", a=2)
                    nc.vector.tensor_scalar(den, o[:, :, :, 128], -1.0, 1.0, ALU.mult, ALU.max
                                            ).then_inc(den_done, 1)
                    dve.wait_ge(den_done, 2 * c + 1)
                    nc.vector.tensor_tensor(den, o[:, :, :, 128], den, ALU.max).then_inc(den_done, 1)
                    dve.wait_ge(den_done, 2 * c + 2)
                    nc.vector.reciprocal(nst[:, e, 1, :], nst[:, e, 0, :]).then_inc(rden_done, 1)
                    dve.wait_ge(rden_done, c + 1)
                    for a in range(2):
                        last = nc.vector.tensor_tensor(
                            hs[:, e, 3 * a:3 * a + 3, :], o[:, a, :, 0:128],
                            nst[:, e, 1, 3 * a:3 * a + 3].unsqueeze(2).to_broadcast([128, 3, 128]), ALU.mult)
                    last.then_inc(num_done, 1)
                    dve.wait_ge(num_done, c + 1)
                    nc.vector.tensor_tensor(hsq, hs[:, e, :, :], hs[:, e, :, :], ALU.mult).then_inc(hsq_done, 1)
                    dve.wait_ge(hsq_done, c + 1)
                    nc.vector.reduce_sum(nst[:, e, 2, :], hsq, AX.X).then_inc(ss_done, 1)

            def mlstm_norm(p, heads=(0, 1)):
                for e in heads:
                    c = 2 * p + e
                    dve.wait_ge(rms_done, c + 1)
                    nc.vector.reciprocal(nst[:, e, 4, :], nst[:, e, 3, :]).then_inc(rrms_done, 1)
                    dve.wait_ge(rrms_done, c + 1)
                    nc.vector.tensor_tensor(hs[:, e, :, :], hs[:, e, :, :],
                                            nst[:, e, 4, :].unsqueeze(2).to_broadcast([128, 6, 128]),
                                            ALU.mult).then_inc(hs_done, 1)

            def conv(p, c, raw_rows, dst):
                dve.wait_ge(drained[c], st.drain[c] + 3 * p + 2)
                nc.vector.tensor_scalar(dst[:, :], raw_rows[:, 3:3 + NT], pair_p[:, 4 * c + 3:4 * c + 4], None,
                                        ALU.mult).then_inc(conv_step, 1)
                for tap in range(3):
                    dve.wait_ge(conv_step, 8 * p + 4 * c + tap + 1)
                    nc.vector.scalar_tensor_tensor(
                        out=dst[:, :], in0=raw_rows[:, tap:tap + NT], scalar=pair_p[:, 4 * c + tap:4 * c + tap + 1],
                        in1=dst[:, :], op0=ALU.mult, op1=ALU.add).then_inc(conv_step, 1)

            def mlstm_sigmoid(p):
                nc.vector.tensor_copy(pair_g[:, :], pair_all[:, bass.ds(p, 1), 8:10].rearrange("p a b -> p (a b)")
                                      ).then_inc(gain_set, 1)
                dve.wait_ge(o_tanh, 2 * p + 2)
                nc.vector.tensor_scalar(o_sig[:, :, :], o_sig[:, :, :], 1.0, 0.5, ALU.add, ALU.mult
                                        ).then_inc(o_done, 1)

            def mlstm_y(p, last_pair=False):
                dve.wait_ge(gain_set, p + 1)
                dve.wait_ge(o_done, p + 1)
                for e in range(2):
                    dve.wait_ge(y_turned, 2 * p + e + 1)
                    nc.vector.scalar_tensor_tensor(
                        out=src[:, e, 0:META], in0=bank[:, 2 * e + 1, 0:META], scalar=pair_g[:, e:e + 1],
                        in1=o_sig[:, e, 0:META], op0=ALU.mult, op1=ALU.mult)
                    nc.vector.scalar_tensor_tensor(
                        out=src[:, e, META:NT], in0=bank[:, 2 * e, :], scalar=pair_g[:, e:e + 1],
                        in1=o_sig[:, e, META:NT], op0=ALU.mult, op1=ALU.mult).then_inc(piece_ready, 1)
                if last_pair:
                    for e in range(2):
                        piece_low(st.piece + 2 * p + e, y_lo[:, 2 * p + e, :], y_hi[:, 2 * p + e, :], e, EVERY)

            def piece_low(c, dst, hi, b, cs):
                dve.wait_ge(piece_lo, c)
                dve.wait_ge(piece_hi, c + 1)
                nc.vector.tensor_tensor(dst[:, cs], src[:, b, cs], hi[:, cs].bitcast(f32),
                                        ALU.subtract).then_inc(piece_lo, 1)

            def weigh(p, e, banks=BANKS):
                dve.wait_ge(scores_done, 2 * p + e + 1)
                dve.wait_ge(dec_done, p + 1)
                at = score_blocks(banks)
                for t in range(XT):
                    nc.vector.scalar_tensor_tensor(
                        out=ws[0:META, e, JM + 128 * t:JM + 128 * t + 128],
                        in0=banks[3][0:META, 128 * t:128 * t + 128], scalar=cols_p[0:META, t, e:e + 1],
                        in1=a_row[0:META, e, 128 * t:128 * t + 128], op0=ALU.mult, op1=ALU.mult)
                nc.vector.scalar_tensor_tensor(
                    out=ws[0:META, e, JMM:JMM + META], in0=banks[2][0:META, 256:256 + META], scalar=scale,
                    in1=dec_m[:, e, :], op0=ALU.mult, op1=ALU.mult).then_inc(ws_meta_done, 1)
                for jt in range(XT):
                    w0 = WS_AT[jt]
                    last = nc.vector.scalar_tensor_tensor(out=ws[:, e, w0:w0 + 128], in0=at[jt][:, 0:128], scalar=scale,
                                                   in1=dec[:, e, jt, :], op0=ALU.mult, op1=ALU.mult)
                    for t in range(jt + 1, XT):
                        o = 128 * (t - jt)
                        idx = 6 + t * (t - 1) // 2 + jt
                        nc.vector.scalar_tensor_tensor(
                            out=ws[:, e, w0 + o:w0 + o + 128], in0=at[jt][:, o:o + 128],
                            scalar=cols_p[:, idx, e:e + 1], in1=a_row[:, e, 128 * t:128 * t + 128],
                            op0=ALU.mult, op1=ALU.mult)
                last.then_inc(ws_done, 1)

            def meta_weights_low(p, e):
                dve.wait_ge(w_meta_high, 2 * p + e + 1)
                nc.vector.tensor_tensor(w_meta[META_END, e, :], ws[0:META, e, JM:WSW],
                                        w_meta[META_HI, e, :].bitcast(f32), ALU.subtract).then_inc(w_meta_done, 1)

            def meta_v_low(p):
                dve.wait_ge(v_meta_high, p + 1)
                nc.vector.tensor_tensor(v_meta[META_MID, :, :], v_tok[0:META, 4, :, :],
                                        v_meta[META_HI, :, :].bitcast(f32), ALU.subtract).then_inc(v_meta_done, 1)

            def k_lows(p):
                dve.wait_ge(k_high_done, p + 1)
                for e in range(2):
                    own, other = slice(64 * e, 64 * e + 64), slice(64 - 64 * e, 128 - 64 * e)
                    last = nc.vector.tensor_tensor(k_stack[e][other, :], ks[own, :],
                                                   k_stack[e][own, :].bitcast(f32), ALU.subtract)
                last.then_inc(k_split, 1)
            def pair_columns(p, first):
                if not first:
                    dve.wait_ge(ws_done, 2 * p)
                    dve.wait_ge(conv_step, 8 * p)
                nc.vector.tensor_copy(pair_p[:, :], pair_all[:, bass.ds(p, 1), 0:8].rearrange("p a b -> p (a b)")
                                      ).then_inc(pair_set, 1)
                nc.vector.tensor_copy(cols_p[:, :, :], cols[:, :, bass.ds(2 * p, 2)]).then_inc(pair_set, 1)
                dve.wait_ge(pair_set, 2 * p + 2)

            def mask_decays(p):
                dve.wait_ge(dec_exp, p + 1)
                nc.vector.memset(dec[64:128, :, :, 0:64], 0.0).then_inc(dec_done, 1)

            def silu(p, c, rows):
                dve.wait_ge(conv_tanh, 2 * p + c + 1)
                nc.vector.scalar_tensor_tensor(out=rows[:, :], in0=half_tanh[:, :], scalar=1.0, in1=rows[:, :],
                                               op0=ALU.add, op1=ALU.mult).then_inc(silu_done, 1)

            def mlstm(p, first):
                n = st.panel + 6 * p

                def evacuate(j, out):
                    dve.wait_ge(panel_done, n + j + 1)
                    scaled(out, j % 2, True, drained[j % 2])

                if first:
                    row_rstd(0, EVERY)
                evacuate(0, v_T[:, 0, :])
                if not first:
                    weigh(p - 1, 0)
                    meta_v_low(p - 1)
                    meta_weights_low(p - 1, 0)
                else:
                    dve.wait_ge(gates_done, 1)
                    nc.vector.tensor_tensor(row_view(tanh_rows, True), bank[0:40, 2:4, 0:HALF],
                                            row_view(rstd[0:40, :], True), ALU.mult).then_inc(gates_scaled, 1)
                evacuate(1, v_T[:, 1, :])
                if not first:
                    weigh(p - 1, 1)
                    meta_weights_low(p - 1, 1)
                evacuate(2, q_raw[:, 3:3 + NT])
                if first:
                    gate_chain()
                    dve.wait_ge(tab_loaded, 32)
                    nc.vector.tensor_copy(pair_p[:, :], pair_all[:, 0, 0:8]).then_inc(pair_one, 1)
                    dve.wait_ge(pair_one, 1)
                else:
                    pair_columns(p, False)
                conv(p, 0, q_raw, qs)
                if not first:
                    mlstm_ratio(p - 1)
                evacuate(3, k_raw[:, 3:3 + NT])
                silu(p, 0, qs)
                if not first:
                    mlstm_norm(p - 1)
                conv(p, 1, k_raw, ks)
                if not first:
                    mlstm_sigmoid(p - 1)
                silu(p, 1, ks)
                if not first:
                    mlstm_y(p - 1)
                    k_lows(p)
                    mask_decays(p)
                    dve.wait_ge(piece_ready, st.piece + 2 * p)
                evacuate(4, o_sig[:, 0, :])
                if first:
                    gate_cols()
                    pair_columns(0, True)
                    k_lows(0)
                evacuate(5, o_sig[:, 1, :])
                if first:
                    mask_decays(0)

            mlstm(0, True)
            with dve.Fori(1, PAIRS) as p:
                mlstm(p, False)
            weigh(PAIRS - 1, 0, SLOTS)
            meta_v_low(PAIRS - 1)
            meta_weights_low(PAIRS - 1, 0)
            weigh(PAIRS - 1, 1)
            meta_weights_low(PAIRS - 1, 1)
            mlstm_sigmoid(PAIRS - 1)
            dve.wait_ge(piece_lo, st.piece + 2 * (PAIRS - 1))
            for e in range(2):
                mlstm_ratio(PAIRS - 1, (e,), True)
                mlstm_norm(PAIRS - 1, (e,))
            mlstm_y(PAIRS - 1, True)

            def out_proj(stage, r, cs, panels):
                st = Start(stage)
                dve.wait_ge(cleared, r)

                def two_tiles(i, add_last=True):
                    for c in range(2):
                        residual(st.res + 2 * i + c, st.drain[c] + i + 1,
                                 st.panel + 2 * panels * (i + 1) - 2 + c, 2 * i + c, c, r, cs, add_last or c == 0)

                with dve.Fori(0, KT // 2 - 1) as i:
                    two_tiles(i)
                two_tiles(KT // 2 - 1, r < 4)

            def up(stage, cs):
                st = Start(stage)
                full = cs.start == 0

                with dve.Fori(0, FT // 2) as i:
                    for c in range(2):
                        f = 2 * i + c
                        dve.wait_ge(piece_ready, st.piece + f - 1)
                        dve.wait_ge(panel_done, st.panel + 2 * f + 1)
                        scaled(silu_g[:, c, :], 0, full, drained[0])
                        dve.wait_ge(piece_lo, st.piece + f - 1)
                        dve.wait_ge(panel_done, st.panel + 2 * f + 2)
                        scaled(src[:, c, :], 1, full, drained[1])
                        dve.wait_ge(drained[1], st.drain[1] + f + 1)
                        dve.wait_ge(up_silu, UPS[stage] + f + 1)
                        nc.vector.tensor_tensor(src[:, c, cs], src[:, c, cs], silu_g[:, c, cs],
                                                ALU.mult).then_inc(piece_ready, 1)

            UPS = {"up0": 0, "up1": FT}
            out_proj("out0", 1, EVERY, 1)
            row_rstd(1, EVERY)
            up("up0", EVERY)
            out_proj("down0", 2, EVERY, 3)

            sr = Start("reten")

            def rope_first(p, c, dst, full):
                n = sr.panel + 12 * p + 2 * c
                cs = EVERY if full else X
                dve.wait_ge(panel_done, n + 1)
                nc.vector.tensor_tensor(row_view(dst[:, 0, :], full), slot_view(0, full),
                                        row_view(cos_sin[:, 0, :], full), ALU.mult).then_inc(rope_step, 1)
                nc.vector.tensor_tensor(row_view(dst[:, 1, :], full), slot_view(0, full),
                                        row_view(cos_sin[:, 1, :], full), ALU.mult).then_inc(drained[0], 1)

            def rope_second(p, c, dst, full):
                n = sr.panel + 12 * p + 2 * c + 1
                cs = EVERY if full else X
                done = 8 * p + 4 * c
                dve.wait_ge(rope_step, done + 1)
                dve.wait_ge(panel_done, n + 1)
                nc.vector.tensor_tensor(row_view(rtmp[:, :], full), slot_view(1, full),
                                        row_view(cos_sin[:, 1, :], full), ALU.mult).then_inc(rope_step, 1)
                dve.wait_ge(rope_step, done + 2)
                nc.vector.tensor_tensor(dst[:, 0, cs], dst[:, 0, cs], rtmp[:, cs],
                                        ALU.subtract).then_inc(rope_step, 1)
                dve.wait_ge(rope_step, done + 3)
                nc.vector.tensor_tensor(row_view(rtmp[:, :], full), slot_view(1, full),
                                        row_view(cos_sin[:, 0, :], full), ALU.mult).then_inc(drained[1], 1)
                dve.wait_ge(drained[1], sr.drain[1] + 6 * p + c + 1)
                dve.wait_ge(drained[0], sr.drain[0] + 6 * p + c + 1)
                nc.vector.tensor_tensor(dst[:, 1, cs], dst[:, 1, cs], rtmp[:, cs],
                                        ALU.add).then_inc(rope_step, 1)

            def reten_norm(p):
                for t in range(XT):
                    c = 4 * p + t
                    dve.wait_ge(rmix_done, c + 1)
                    nc.vector.bn_stats(bn6[:, t, :], bank[:, t, :]).then_inc(bn_done, 1)
                dve.wait_ge(bn_done, 4 * p + 4)
                nc.vector.memset(rsd[:, :], 0.0)
                for t in range(XT):
                    nc.vector.bn_aggr(mv[:, t, :], bn6[:, t, :]).then_inc(mv_done, 1)
                dve.wait_ge(rsd_done, p + 1)
                nc.vector.reciprocal(rsd[:, :], rsd[:, :]).then_inc(rrsd_done, 1)
                dve.wait_ge(rrsd_done, p + 1)
                for t in range(XT):
                    nc.vector.tensor_scalar(rhs_n[:, t, :], bank[:, t, :], mv[:, t, 0:1], rsd[:, t:t + 1],
                                            ALU.subtract, ALU.mult).then_inc(rhs_done, 1)

            def reten_y(p, parts, last_head=False):
                if parts[0] == 0:
                    reten_gain(p)
                for e in parts:
                    dve.wait_ge(ry_turned, 4 * p + e + 1)
                    dve.wait_ge(piece_lo, sr.piece + 4 * p + e - 1)
                    nc.vector.scalar_tensor_tensor(
                        out=src[:, e % 2, X], in0=bank[:, e, :], scalar=stat[:, 4 + e:5 + e],
                        in1=rgate[:, e, :], op0=ALU.mult, op1=ALU.mult).then_inc(piece_ready, 1)
                if last_head:
                    for e in parts:
                        piece_low(sr.piece + 4 * p + e, y_lo[:, 4 * p + e, :], y_hi[:, 4 * p + e, :], e % 2, X)

            def reten_gain(p):
                nc.vector.tensor_copy(stat[:, 4:8], ret_gain[:, bass.ds(4 * p, 4)]).then_inc(gain_set, 1)
                dve.wait_ge(gain_set, PAIRS + p + 1)
                dve.wait_ge(rgate_done, 4 * p + 4)

            def reten_v_low(p, j):
                dve.wait_ge(rv_high_done, 4 * p + j + 1)
                part = slice(128 * j, 128 * j + 128)
                nc.vector.tensor_tensor(
                    rv_lo[:, :, part], bank[:, 2 * (j % 2), :].rearrange("p (t n) -> p t n", t=4),
                    rv_hi[:, 0:4, part].bitcast(f32), ALU.subtract)
                nc.vector.tensor_tensor(rv_meta[META_MID, part], bank[0:META, 2 * (j % 2) + 1, 0:128],
                                        rv_meta[META_HI, part].bitcast(f32), ALU.subtract).then_inc(rv_split, 1)

            def reten(p, first):
                rope_first(p, 0, rq, False)
                if first:
                    row_rstd(2, EVERY)
                else:
                    reten_norm(p - 1)
                rope_second(p, 0, rq, False)
                if first:
                    dve.wait_ge(rope_step, 4)
                    for c in range(2):
                        nc.vector.tensor_tensor(rq[:, c, X], rq[:, c, X], rstd[:, X], ALU.mult)
                    for c in range(2):
                        nc.vector.tensor_tensor(cos_sin[:, c, :], cos_sin[:, c, :], rstd[:, :],
                                                ALU.mult).then_inc(rope_scaled, 1)
                    dve.wait_ge(rope_scaled, 2)
                rope_first(p, 1, rk, True)
                if not first:
                    reten_y(p - 1, (0, 1))
                rope_second(p, 1, rk, True)
                if not first:
                    reten_y(p - 1, (2, 3))
                n = sr.panel + 12 * p
                for j in range(4):
                    if j >= 2:
                        dve.wait_ge(rv_turned, 4 * p + j - 1)
                    dve.wait_ge(panel_done, n + 5 + j)
                    scaled(rv_T[:, j % 2, :], j % 2, True, drained[j % 2])
                    if j >= 2:
                        reten_v_low(p, j - 2)
                for j in range(2):
                    dve.wait_ge(panel_done, n + 9 + j)
                    nc.vector.tensor_tensor(rgate[:, j, :], slot_view(j % 2, False), rstd[:, X],
                                            ALU.mult).then_inc(drained[j % 2], 1)
                    if j == 0:
                        reten_v_low(p, 2)
                        reten_v_low(p, 3)
                dve.wait_ge(rscores_done, p + 1)
                dve.wait_ge(rdec_loaded, 32 * (p + 1))
                at = [bank[:, 0, :], bank[:, 1, 0:384], bank[:, 2, 0:256], bank[:, 1, 384:512]]
                for jt in range(XT):
                    w = SEQ - 128 * jt
                    nc.vector.tensor_tensor(rws_at[jt], at[jt], rdec[:, 0:w], ALU.mult)
                nc.vector.tensor_tensor(rws_m[:, :], bank[0:META, 3, :], rdec_m[:, :],
                                        ALU.mult).then_inc(rws_done, 1)
                for j in range(2, 4):
                    dve.wait_ge(panel_done, n + 9 + j)
                    nc.vector.tensor_tensor(rgate[:, j, :], slot_view(j % 2, False), rstd[:, X],
                                            ALU.mult).then_inc(drained[j % 2], 1)
                    if j == 2:
                        dve.wait_ge(rws_high_done, p + 1)
                        nc.vector.tensor_tensor(rws_meta[META_END, :], rws_m[:, :],
                                                rws_meta[META_HI, :].bitcast(f32), ALU.subtract
                                                ).then_inc(rws_meta_split, 1)

            for t in (rws_meta, rv_meta):
                nc.vector.memset(t[META_K, :].bitcast(f32), 0.0).then_inc(meta_cleared, 1)
            dve.wait_ge(rope_loaded, 16)
            reten(0, True)
            with dve.Fori(1, RT_HEADS) as p:
                reten(p, False)
            reten_norm(RT_HEADS - 1)
            for parts in ((0, 1), (2, 3)):
                reten_y(RT_HEADS - 1, parts, True)
            out_proj("out1", 3, X, 2)
            row_rstd(3, X)
            up("up1", X)
            out_proj("down1", 4, X, 3)
            for k in range(POOL_OUT):
                nc.vector.tensor_scalar(h[:, k, X], h[:, k, X], gains[:, 4 * KT + k:4 * KT + k + 1], None,
                                        ALU.mult).then_inc(gained, 1)
            row_rstd(4, X)
            for k in range(POOL_OUT, KT):
                nc.vector.scalar_tensor_tensor(
                    out=h[:, k, X], in0=h[:, k, X], scalar=gains[:, 4 * KT + k:4 * KT + k + 1], in1=rstd[:, X],
                    op0=ALU.mult, op1=ALU.mult).then_inc(out_ready, 1)

        @block.tensor
        def _(pe):
            def panel(n, s, out_slot, xs, cols_, first=True, last=True, k0=0, end=True,
                      within=None, halves=False):
                pe.wait_ge(half_lo if halves else w_lo_done, n + 1)
                for k, (hi, lo) in enumerate(xs, k0):
                    if halves and k == KT // 2:
                        pe.wait_ge(w_lo_done, n + 1)
                    if within and k == KT - 2:
                        within()
                    if callable(hi):
                        hi, lo = hi()
                    for w, x in ((w_hi, hi), (w_hi, lo), (w_lo, hi)):
                        for b, a, width in cols_:
                            mm = nc.tensor.matmul(
                                slot[out_slot][:, b, 0:width], w[s][:, k, :], x[:, a:a + width],
                                start=first and k == 0 and w is w_hi and x is hi,
                                stop=last and end and k == k0 + len(xs) - 1 and w is w_lo)
                if end:
                    mm.then_inc(panel_done, 1)

            def x_tiles(r):
                def tile(k):
                    def get():
                        pe.wait_ge(x_split, KT * r + k + 1)
                        return x_hi[:, k, :], x_lo[:, k, :]
                    return get, None
                return [tile(k) for k in range(KT)]

            X_READY = [(x_hi[:, k, :], x_lo[:, k, :]) for k in range(KT)]

            def norm(r, cs):
                pe.wait_ge(summed, KT * (r + 1) - (r == 4))
                if cs.start == 0:
                    for b in range(2):
                        mm = nc.tensor.matmul(bank[:, b, 0:HALF], ones[:, :], sumsq[:, b * HALF:(b + 1) * HALF],
                                              start=True, stop=True)
                else:
                    mm = nc.tensor.matmul(bank[:, 0, :], ones[:, :], sumsq[:, META:NT], start=True, stop=r < 4)
                if r == 4:
                    pe.wait_ge(squared, KT * 5)
                    mm = nc.tensor.matmul(bank[:, 0, :], ones[:, :], square[:, META:NT], start=False, stop=True)
                mm.then_inc(stat_done, 1)

            EVERY, X = slice(0, NT), slice(META, NT)
            pe.wait_ge(consts_set, 5)

            def gates():
                pe.wait_ge(wg_lo_done, 2)
                for k in range(KT):
                    for w, x in ((wg_hi, x_hi), (wg_hi, x_lo), (wg_lo, x_hi)):
                        for b in range(2):
                            mm = nc.tensor.matmul(bank[0:40, 2 + b, 0:HALF], w[:, k, :],
                                                  x[:, k, b * HALF:(b + 1) * HALF],
                                                  start=k == 0 and w is wg_hi and x is x_hi,
                                                  stop=k == KT - 1 and w is wg_lo)
                mm.then_inc(gates_done, 1)

            st = Start("mlstm")

            def mlstm_mix(p, heads=(0, 1), banks=BANKS):
                pe.wait_ge(ws_done, 2 * p + heads[-1] + 1)
                for e in heads:
                    outs = [banks[2 * e + b // 3][:, 160 * (b % 3):160 * (b % 3) + V_COLS] for b in range(6)]
                    for b in (4, 3, 2, 1, 0, 5):
                        t = b - 1 if 1 <= b <= XT else -1
                        for jt in range(t + 1):
                            w0 = WS_AT[jt] + 128 * (t - jt)
                            nc.tensor.matmul(outs[b], ws[:, e, w0:w0 + 128], v_tok[:, jt, e, :],
                                             start=jt == 0, stop=False)
                        if e == heads[0] and b == 4:
                            pe.wait_ge(v_meta_done, p + 1)
                            pe.wait_ge(w_meta_done, 2 * p + heads[-1] + 1)
                        m0 = 128 * t if t >= 0 else JMM - JM
                        mm = nc.tensor.matmul(outs[b], w_meta[META_K, e, m0:m0 + 128], v_meta[META_K, e, :],
                                              start=t < 0, stop=True)
                    mm.then_inc(mix_done, 1)

            def mlstm_turn(p, e):
                pe.wait_ge(hs_done, 2 * p + e + 1)
                for t in range(XT):
                    nc.tensor.transpose(bank[:, 2 * e, 128 * t:128 * t + 128], hs[:, e, 1 + t, :], ident[:, :])
                nc.tensor.transpose(bank[:, 2 * e + 1, 0:META], hs[0:META, e, 0, :],
                                    ident[0:META, 0:META]).then_inc(y_turned, 1)

            def gate_columns():
                pe.wait_ge(gate_act, 8)
                pe.wait_ge(tab_loaded, 32)
                tiles = [(0, META)] + [(META + 128 * t, 128) for t in range(XT)]
                jobs = [(c_row[t], 0) for t in range(4)] + [(lf_row, 0), (li_row, 0)]
                jobs += [(c_row[t], 1 + j) for t in range(4) for j in range(t)]
                jobs += [(lf_row, 1 + t) for t in range(4)] + [(li_row, 1 + t) for t in range(4)]
                for c, (row, tile) in enumerate(jobs):
                    a, w = tiles[tile]
                    mm = nc.tensor.transpose(bank[0:w, 3, 8 * c:8 * c + 8], row[:, a:a + w],
                                             ident[0:ML_HEADS, 0:ML_HEADS])
                mm.then_inc(cols_done, 1)

            def mlstm_scores(p, e, banks=BANKS):
                r = slice(64 * e, 64 * e + 64)
                blocks = [(at, slice(META + 128 * t, META + 128 * t + 128), slice(META + 128 * t, NT))
                          for t, at in enumerate(score_blocks(banks))]
                blocks += [(banks[3][0:META, :], slice(0, META), slice(META, NT)),
                           (banks[2][0:META, 256:256 + META], slice(0, META), slice(0, META))]
                for o, keys, queries in blocks:
                    nc.tensor.matmul(o, k_stack[e][:, keys], q_stack[e][:, queries], start=True, stop=False)
                    mm = nc.tensor.matmul(o, k_stack[e][r, keys], q_low[r, queries], start=False, stop=True)
                mm.then_inc(scores_done, 1)

            def mlstm(p, first):
                n, d0, d1 = st.panel + 6 * p, st.drain[0] + 3 * p, st.drain[1] + 3 * p
                if not first:
                    pe.wait_ge(drained[0], d0)
                panel(n, 0, 0, x_tiles(0) if first else X_READY, ALL_COLS, halves=first)
                if first:
                    gates()
                    norm(0, EVERY)
                else:
                    pe.wait_ge(q_stacked, p)
                    pe.wait_ge(q_split, p)
                    pe.wait_ge(k_split, p)
                    pe.wait_ge(v_tok_done, p)
                    mlstm_scores(p - 1, 0)
                    pe.wait_ge(drained[1], d1)
                panel(n + 1, 1, 1, X_READY, ALL_COLS)
                if not first:
                    pe.wait_ge(ws_done, 2 * p - 1)
                    mlstm_scores(p - 1, 1)
                pe.wait_ge(drained[0], d0 + 1)
                panel(n + 2, 0, 0, X_READY, ALL_COLS)
                if not first:
                    mlstm_mix(p - 1)
                pe.wait_ge(drained[1], d1 + 1)
                panel(n + 3, 1, 1, X_READY, ALL_COLS)
                pe.wait_ge(drained[0], d0 + 2)
                panel(n + 4, 0, 0, X_READY, ALL_COLS)
                if first:
                    gate_columns()
                else:
                    mlstm_turn(p - 1, 0)
                    mlstm_turn(p - 1, 1)
                pe.wait_ge(drained[1], d1 + 2)
                panel(n + 5, 1, 1, X_READY, ALL_COLS)
                if first:
                    pe.wait_ge(cols_out, 2)
                else:
                    pe.wait_ge(piece_ready, st.piece + 2 * p)
                for e in range(2):
                    for t in range(XT):
                        a = META + 128 * t
                        nc.tensor.transpose(bank[:, e, 128 * t:128 * t + 128], v_T[:, e, a:a + 128], ident[:, :])
                    mm = nc.tensor.transpose(bank[0:META, 2, 128 * e:128 * e + 128], v_T[:, e, 0:META], ident[:, :])
                mm.then_inc(v_turned, 1)

            mlstm(0, True)
            with pe.Fori(1, PAIRS) as p:
                mlstm(p, False)

            def y_tile(k):
                return (y_hi[:, k, :], y_lo[:, k, :]) if k < YT else (z_hi[:, k - YT, :], z_lo[:, k - YT, :])

            def two_outputs(st, groups, i, cols_, pieces=None):
                for g, (k0, kn) in enumerate(groups):
                    for c in range(2):
                        if g == 0:
                            pe.wait_ge(drained[c], st.drain[c] + i)
                        if pieces is not None:
                            pe.wait_ge(piece_lo, pieces + k0 + kn)
                        panel(st.panel + 2 * len(groups) * i + 2 * g + c, c, c,
                              [y_tile(k) for k in range(k0, k0 + kn)], cols_, first=g == 0,
                              last=g == len(groups) - 1)

            def out_proj(stage, groups, cols_, pieces):
                st = Start(stage)
                two_outputs(st, groups, 0, cols_, pieces)
                with pe.Fori(1, KT // 2) as i:
                    two_outputs(st, groups, i, cols_)

            def up(stage, r, cols_, cs):
                st = Start(stage)

                def two_tiles(i, first):
                    for c in range(2):
                        f = 2 * i + c
                        pe.wait_ge(drained[0], st.drain[0] + f)
                        if first and c == 0:
                            panel(st.panel, 0, 0, x_tiles(r), cols_, within=lambda: norm(r, cs))
                        else:
                            panel(st.panel + 2 * f, 0, 0, X_READY, cols_)
                        pe.wait_ge(drained[1], st.drain[1] + f)
                        panel(st.panel + 2 * f + 1, 1, 1, X_READY, cols_)

                two_tiles(0, True)
                with pe.Fori(1, FT // 2) as i:
                    two_tiles(i, False)

            so = Start("out0")
            early = ML_HEADS - 2
            last = PAIRS - 1

            def out0_tiles(c, a, z):
                pe.wait_ge(piece_lo, st.piece + max(z, early))
                panel(so.panel + c, c, c, [y_tile(k) for k in range(a, z)], ALL_COLS, k0=a, last=z == KT, end=z == KT)

            pe.wait_ge(q_stacked, PAIRS)
            pe.wait_ge(q_split, PAIRS)
            pe.wait_ge(k_split, PAIRS)
            for c in range(2):
                pe.wait_ge(drained[c], so.drain[c])
            mlstm_scores(last, 0, SLOTS)
            pe.wait_ge(v_tok_done, PAIRS)
            mlstm_scores(last, 1)
            mlstm_mix(last, (0,), SLOTS)
            mlstm_mix(last, (1,), SLOTS)
            pe.wait_ge(num_done, 2 * PAIRS - 1)
            out0_tiles(0, 0, early)
            mlstm_turn(last, 0)
            pe.wait_ge(num_done, 2 * PAIRS)
            out0_tiles(1, 0, 3)
            mlstm_turn(last, 1)
            out0_tiles(1, 3, 5)
            out0_tiles(0, early, KT - 1)
            out0_tiles(0, KT - 1, KT)
            out0_tiles(1, 5, KT)
            with pe.Fori(1, KT // 2) as i:
                two_outputs(so, ((0, 8),), i, ALL_COLS)
            up("up0", 1, ALL_COLS, EVERY)
            out_proj("down0", DOWN_SPLIT, ALL_COLS, Start("up0").piece)

            sr = Start("reten")

            def reten_mix(p):
                pe.wait_ge(rws_split, p + 1)
                pe.wait_ge(rws_meta_split, p + 1)
                for t in range(XT):
                    nc.tensor.matmul(bank[:, t, :], rws_meta[META_K, 128 * t:128 * t + 128], rv_meta[META_K, :],
                                     start=True, stop=False)
                    for jt in range(t + 1):
                        w0 = R_AT[jt] + 128 * (t - jt)
                        for w, v in ((rws_hi, rv_hi), (rws_hi, rv_lo), (rws_low, rv_hi)):
                            mm = nc.tensor.matmul(bank[:, t, :], w[:, w0:w0 + 128], v[:, jt, :],
                                                  start=False, stop=jt == t and w is rws_low)
                    mm.then_inc(rmix_done, 1)

            def reten_turn(p):
                pe.wait_ge(rhs_done, 4 * p + 4)
                for e in range(4):
                    for t in range(XT):
                        mm = nc.tensor.transpose(bank[:, e, 128 * t:128 * t + 128],
                                                 rhs_n[:, t, 128 * e:128 * e + 128], ident[:, :])
                    mm.then_inc(ry_turned, 1)

            def reten_v_turn(p, j):
                b = 2 * (j % 2)
                pe.wait_ge(drained[j % 2], sr.drain[j % 2] + 6 * p + 3 + j // 2)
                if j >= 2:
                    pe.wait_ge(rv_split, 4 * p + j - 1)
                for t in range(XT):
                    a = META + 128 * t
                    nc.tensor.transpose(bank[:, b, 128 * t:128 * t + 128], rv_T[:, j % 2, a:a + 128], ident[:, :])
                nc.tensor.transpose(bank[0:META, b + 1, 0:128], rv_T[:, j % 2, 0:META],
                                    ident[:, :]).then_inc(rv_turned, 1)

            def reten(p, first):
                n = sr.panel + 12 * p
                d = [sr.drain[0] + 6 * p, sr.drain[1] + 6 * p]
                for j in range(12):
                    pe.wait_ge(drained[j % 2], d[j % 2] + j // 2)
                    xs = x_tiles(2) if first and j == 0 else X_READY
                    panel(n + j, j % 2, j % 2, xs, ALL_COLS if 2 <= j < 8 else X_COLS,
                          within=(lambda: norm(2, EVERY)) if first and j == 0 else None)
                    if not first and j == 0:
                        reten_mix(p - 1)
                    if not first and j == 2:
                        reten_turn(p - 1)
                    if j == 5:
                        if not first:
                            pe.wait_ge(piece_ready, sr.piece + 4 * p)
                        reten_v_turn(p, 0)
                    if 6 <= j <= 8:
                        reten_v_turn(p, j - 5)
                    if j == 9:
                        pe.wait_ge(rope_step, 8 * p + 8)
                        pe.wait_ge(rv_split, 4 * p + 4)
                        at = [bank[:, 0, :], bank[:, 1, 0:384], bank[:, 2, 0:256], bank[:, 1, 384:512]]
                        for jt in range(XT):
                            a = META + 128 * jt
                            for kk in range(2):
                                nc.tensor.matmul(at[jt], rk[:, kk, a:a + 128], rq[:, kk, a:NT],
                                                 start=kk == 0, stop=kk == 1)
                        for kk in range(2):
                            mm = nc.tensor.matmul(bank[0:META, 3, :], rk[:, kk, 0:META], rq[:, kk, META:NT],
                                                  start=kk == 0, stop=kk == 1)
                        mm.then_inc(rscores_done, 1)

            reten(0, True)
            with pe.Fori(1, RT_HEADS) as p:
                reten(p, False)

            so1 = Start("out1")
            def out1_tiles(c, a, z):
                pe.wait_ge(piece_lo, sr.piece + max(z, 4 * (RT_HEADS - 1)))
                panel(so1.panel + 2 * (a // KT) + c, c, c, [y_tile(k) for k in range(a, z)], X_COLS,
                      first=a < KT, last=z == 2 * KT, k0=a % KT, end=z % KT == 0)

            pe.wait_ge(drained[0], so1.drain[0])
            out1_tiles(0, 0, KT)
            reten_mix(RT_HEADS - 1)
            pe.wait_ge(drained[1], so1.drain[1])
            out1_tiles(1, 0, KT)
            reten_turn(RT_HEADS - 1)
            out1_tiles(0, KT, 12)
            out1_tiles(1, KT, 10)
            out1_tiles(0, 12, 14)
            out1_tiles(0, 14, 16)
            out1_tiles(1, 10, 16)
            with pe.Fori(1, KT // 2) as i:
                two_outputs(so1, ((0, 8), (8, 8)), i, X_COLS)
            up("up1", 3, X_COLS, X)
            out_proj("down1", DOWN_SPLIT, X_COLS, Start("up1").piece)
            norm(4, X)


def kernel(x, meta_tokens, norm_mix, norm_ffn, norm_final, ml_w_in, ml_b_gate, ml_w_conv, ml_norm,
           ml_w_out, rt_w_in, rt_norm, rt_w_out, ffn_w_gu, ffn_w_down):
    import numpy as np
    import concourse.bacc as bacc
    from concourse.bass_utils import run_bass_kernel_spmd

    f = np.float32
    arr = [np.asarray(a) for a in (x, meta_tokens, norm_mix, norm_ffn, norm_final, ml_w_in, ml_b_gate,
                                   ml_w_conv, ml_norm, ml_w_out, rt_w_in, rt_norm, rt_w_out, ffn_w_gu, ffn_w_down)]
    (x, meta_tokens, norm_mix, norm_ffn, norm_final, ml_w_in, ml_b_gate, ml_w_conv, ml_norm, ml_w_out,
     rt_w_in, rt_norm, rt_w_out, ffn_w_gu, ffn_w_down) = arr

    def tiles(v):
        return v.reshape(-1, 128).T

    h_in = np.concatenate([meta_tokens, x[0]], 0).T.reshape(KT, 128, NT).transpose(1, 0, 2)
    small = np.zeros((128, 5 * KT + 17), f)
    for r, v in enumerate((norm_mix[0], norm_ffn[0], norm_mix[1], norm_ffn[1], norm_final)):
        small[:, KT * r:KT * (r + 1)] = tiles(v)
    small[:, 5 * KT:5 * KT + 16] = tiles(rt_norm[0])
    small[0:8, 5 * KT + 16] = ml_b_gate[0, 0:8]
    small[32:40, 5 * KT + 16] = ml_b_gate[0, 8:16]
    pair = np.zeros((128, PAIRS, 10), f)
    for p in range(PAIRS):
        pair[:, p, 0:4] = ml_w_conv[0, :, 128 * p:128 * p + 128].T
        pair[:, p, 4:8] = ml_w_conv[0, :, 512 + 128 * p:512 + 128 * p + 128].T
        pair[:, p, 8:10] = tiles(ml_norm[0])[:, 2 * p:2 * p + 2]

    stream = np.zeros((PANELS, 128, KT, 128), f)
    at = 0

    def put(w, c, k0=0, kn=KT):
        nonlocal at
        stream[at, :, 0:kn, :] = w[128 * k0:128 * (k0 + kn), 128 * c:128 * c + 128].reshape(kn, 128, 128
                                                                                         ).transpose(1, 0, 2)
        at += 1

    def ffn(layer):
        for c in range(FT):
            put(ffn_w_gu[layer], c)
            put(ffn_w_gu[layer], FT + c)
        for m in range(0, KT, 2):
            for k0, kn in DOWN_SPLIT:
                put(ffn_w_down[layer], m, k0, kn)
                put(ffn_w_down[layer], m + 1, k0, kn)

    for p in range(PAIRS):
        for c in (8 + 2 * p, 9 + 2 * p, p, 4 + p, 16 + 2 * p, 17 + 2 * p):
            put(ml_w_in[0], c)
    for m in range(KT):
        put(ml_w_out[0], m)
    ffn(0)
    for p in range(RT_HEADS):
        for c in [2 * p, 2 * p + 1, 8 + 2 * p, 9 + 2 * p] + [16 + 4 * p + e for e in range(4)] + \
                [32 + 4 * p + e for e in range(4)]:
            put(rt_w_in[0], c)
    for m in range(0, KT, 2):
        for k0 in (0, 8):
            put(rt_w_out[0], m, k0, 8)
            put(rt_w_out[0], m + 1, k0, 8)
    ffn(1)

    half = D_MODEL // RT_HEADS // 2
    inv = (f(10000.0) ** (-np.arange(half, dtype=f) / f(half))).astype(f)
    ang = np.arange(NT, dtype=f)[None, :] * inv[:, None]
    rope = np.stack([np.cos(ang), np.sin(ang)], 1).astype(f)
    decay = np.zeros((RT_HEADS, 128 + META, SEQ), f)
    j, i = np.arange(128)[:, None], np.arange(SEQ)[None, :]
    for hd in range(RT_HEADS):
        lg = np.log1p(-np.exp2(-5.0 - hd))
        decay[hd, 0:128] = np.exp(lg * abs(i - j)) * (j // CHUNK <= i // CHUNK) / 16.0
        decay[hd, 128:] = np.exp(lg * (i + META - np.arange(META)[:, None])) / 16.0

    feeds = {
        "h_in": h_in, "stream": stream.reshape(PANELS, 128, KT * 128),
        "w_gates": ml_w_in[0][:, 3072:3088].reshape(KT, 128, 16).transpose(1, 0, 2), "small": small,
        "pair_par": pair, "rope_tab": rope, "decay_tab": decay, "ident_in": np.eye(128, dtype=f),
    }
    feeds = {n: np.ascontiguousarray(a) for n, a in feeds.items()}
    nc = bacc.Bacc("TRN2", target_bir_lowering=False, num_devices=1)
    dt = mybir.dt.float32
    args = [nc.dram_tensor(n, a.shape, dt, kind="ExternalInput").ap() for n, a in feeds.items()]
    out = nc.dram_tensor("out", (128, KT, SEQ), dt, kind="ExternalOutput").ap()
    build_hybrid(nc, *args, out)
    r = run_bass_kernel_spmd(nc, [feeds], core_ids=[0])
    return r.results[0]["out"].transpose(2, 1, 0).reshape(1, SEQ, D_MODEL)
```
